# Optimizing a Trainium2 kernel written in Bass

```python
import math
import jax, jax.numpy as jnp
from jax import lax
import numpy as np

D_MODEL = 1024
BATCH = 1
SEQ = 256
DEPTH = 2
DEC_BATCH = 1
DEC_SEQ = 1024
PAST_LEN = 256

GRID_W = 64
HY_WIDTH = D_MODEL // 4
CF_WIDTH = D_MODEL // 4
ATT_WIDTH = D_MODEL // 2
DIFF_HEAD_DIM = 64
DIFF_HEADS = ATT_WIDTH // (2 * DIFF_HEAD_DIM)
MIX_WIDTH = HY_WIDTH + CF_WIDTH + ATT_WIDTH
IN_WIDTH = 3 * HY_WIDTH + 2 * CF_WIDTH + 3 * ATT_WIDTH
HY_SHORT_K = 3
HY_FILTER_EMB = 33
HY_FILTER_HIDDEN = 64
HY_FAST_DECAY_PCT = 0.3
HY_SLOW_DECAY_PCT = 1.5
HY_DECAY_TARGET = 1e-2
CF_CONV_K = 31
D_FF = 4 * D_MODEL
ROPE_BASE = 10000.0
AX_DIM = DIFF_HEAD_DIM // 2
DEEPNORM_ALPHA = (2 * DEPTH) ** 0.25
DEEPNORM_BETA = (8 * DEPTH) ** -0.25
DENSE_KEY_LIMIT = 2048
Q_BLOCK = 128
LN_EPS = 1e-5

kernel_name = 'hyena_conformer_diffattn_prefix_dit'

def _layer_norm(x, g, b):
    xf = x.astype(jnp.float32)
    mu = jnp.mean(xf, -1, keepdims=True)
    var = jnp.mean(jnp.square(xf - mu), -1, keepdims=True)
    return ((xf - mu) * lax.rsqrt(var + LN_EPS) * g.astype(jnp.float32) + b.astype(jnp.float32)).astype(x.dtype)

def _rms_norm(x, g):
    xf = x.astype(jnp.float32)
    return xf * lax.rsqrt(jnp.mean(jnp.square(xf), -1, keepdims=True) + LN_EPS) * g.astype(jnp.float32)

def _dwconv(x, w, b):
    K, C = w.shape
    y = lax.conv_general_dilated(x, w.astype(x.dtype)[:, None, :], (1,), [(K // 2, K // 2)],
                                 dimension_numbers=('NWC', 'WIO', 'NWC'), feature_group_count=C)
    return y + b.astype(x.dtype)

def _hyena_filter(L, w1, b1, freq, w2, b2, w3):
    f32 = jnp.float32
    bands = (HY_FILTER_EMB - 1) // 2
    t = jnp.linspace(0.0, 1.0, L, dtype=f32)[:, None]
    w = (2.0 * math.pi / L) * jnp.arange(L, dtype=f32)[:, None]
    fr = jnp.linspace(1e-4, bands - 1, bands, dtype=f32)[None, :]
    feats = jnp.concatenate([t, jnp.cos(fr * w), -jnp.sin(fr * w)], -1)
    fq = freq.astype(f32)
    hid = jnp.sin(fq * (feats @ w1.astype(f32) + b1.astype(f32)))
    hid = jnp.sin(fq * (hid @ w2.astype(f32) + b2.astype(f32)))
    hf = hid @ w3.astype(f32)
    deltas = jnp.abs(jnp.linspace(math.log(HY_DECAY_TARGET) / HY_FAST_DECAY_PCT,
                                  math.log(HY_DECAY_TARGET) / HY_SLOW_DECAY_PCT, HY_WIDTH, dtype=f32))
    decay = jnp.exp(-t * deltas[None, :])
    h_fwd = hf[:, :HY_WIDTH] * decay
    h_bwd = hf[:, HY_WIDTH:] * decay
    return jnp.concatenate([h_fwd, jnp.zeros((1, HY_WIDTH), f32), h_bwd[:0:-1]], 0)

def _long_conv(u, filt, bias):
    L = u.shape[1]
    uf = u.astype(jnp.float32)
    U = jnp.fft.rfft(uf, n=2 * L, axis=1)
    G = jnp.fft.rfft(filt, n=2 * L, axis=0)
    y = jnp.fft.irfft(U * G[None], n=2 * L, axis=1)[:, :L]
    return (y + uf * bias.astype(jnp.float32)).astype(u.dtype)

def _axial_rope_tables(n):
    rows = n // GRID_W
    row = jnp.repeat(jnp.arange(rows, dtype=jnp.float32), GRID_W)
    col = jnp.tile(jnp.arange(GRID_W, dtype=jnp.float32), rows)
    inv = ROPE_BASE ** (-jnp.arange(0, AX_DIM, 2, dtype=jnp.float32) / AX_DIM)
    ang_r = row[:, None] * inv[None, :]
    ang_c = col[:, None] * inv[None, :]
    return (jnp.cos(ang_r), jnp.sin(ang_r), jnp.cos(ang_c), jnp.sin(ang_c))

def _rot_half(x, cos, sin):
    x1, x2 = jnp.split(x, 2, axis=-1)
    cos = cos[None, :, None, :]
    sin = sin[None, :, None, :]
    return jnp.concatenate([x1 * cos - x2 * sin, x2 * cos + x1 * sin], -1)

def _apply_axial_rope(x, tables):
    cr, sr, cc, sc = tables
    xr, xc = jnp.split(x, 2, axis=-1)
    return jnp.concatenate([_rot_half(xr, cr, sr), _rot_half(xc, cc, sc)], -1).astype(x.dtype)

def _diff_attention(q, k, v, lam, lambda_init, subln_g):
    B, Sq = q.shape[:2]
    Sk = k.shape[1]
    f32 = jnp.float32
    qh = q.reshape(B, Sq, DIFF_HEADS, 2, DIFF_HEAD_DIM).astype(f32)
    kh = k.reshape(B, Sk, DIFF_HEADS, 2, DIFF_HEAD_DIM).astype(f32)
    vf = v.astype(f32)
    scale = DIFF_HEAD_DIM ** -0.5

    def attend(qb):
        s = jnp.einsum('bqhmd,bkhmd->bhmqk', qb, kh) * scale
        p = jax.nn.softmax(s, axis=-1)
        a = p[:, :, 0] - lam * p[:, :, 1]
        return jnp.einsum('bhqk,bkhe->bqhe', a, vf)

    if Sk >= DENSE_KEY_LIMIT:
        nb = Sq // Q_BLOCK
        blocks = jnp.swapaxes(qh.reshape(B, nb, Q_BLOCK, DIFF_HEADS, 2, DIFF_HEAD_DIM), 0, 1)
        out = lax.map(attend, blocks)
        out = jnp.swapaxes(out, 0, 1).reshape(B, Sq, DIFF_HEADS, 2 * DIFF_HEAD_DIM)
    else:
        out = attend(qh)
    out = _rms_norm(out, subln_g) * (1.0 - lambda_init)
    return out.reshape(B, Sq, ATT_WIDTH).astype(q.dtype)

def _token_mixers(h, pl, lambda_init, rope, ctx_kv):
    B, L, _ = h.shape
    dt = h.dtype
    z = h @ pl['w_in']
    o1 = 3 * HY_WIDTH
    o2 = o1 + 2 * CF_WIDTH
    hy = z[..., :o1]
    cf = z[..., o1:o2]
    q = z[..., o2:o2 + ATT_WIDTH].reshape(B, L, 2 * DIFF_HEADS, DIFF_HEAD_DIM)
    k = z[..., o2 + ATT_WIDTH:o2 + 2 * ATT_WIDTH].reshape(B, L, 2 * DIFF_HEADS, DIFF_HEAD_DIM)
    v = z[..., o2 + 2 * ATT_WIDTH:].reshape(B, L, DIFF_HEADS, 2 * DIFF_HEAD_DIM)
    hy = _dwconv(hy, pl['hy_conv_w'], pl['hy_conv_b'])
    x0, x1, hv = jnp.split(hy, 3, axis=-1)
    filt = _hyena_filter(L, pl['hf_w1'], pl['hf_b1'], pl['hf_freq'], pl['hf_w2'], pl['hf_b2'], pl['hf_w3'])
    y_hy = x0 * _long_conv(x1 * hv, filt, pl['hy_bias'])
    a, g = jnp.split(cf, 2, axis=-1)
    u = _dwconv(a * jax.nn.sigmoid(g), pl['cf_conv_w'], pl['cf_conv_b'])
    y_cf = jax.nn.silu(_layer_norm(u, pl['cf_ln_g'], pl['cf_ln_b']))
    f32 = jnp.float32
    lam = (jnp.exp(jnp.sum(pl['lam_q1'].astype(f32) * pl['lam_k1'].astype(f32)))
           - jnp.exp(jnp.sum(pl['lam_q2'].astype(f32) * pl['lam_k2'].astype(f32))) + lambda_init)
    if ctx_kv is None:
        k_all, v_all = k, v
    else:
        q = _apply_axial_rope(q, rope)
        k = _apply_axial_rope(k, rope)
        k_all = jnp.concatenate([ctx_kv[0].astype(dt), k], axis=1)
        v_all = jnp.concatenate([ctx_kv[1].astype(dt), v], axis=1)
    y_at = _diff_attention(q, k_all, v_all, lam, lambda_init, pl['subln_g'])
    y = jnp.concatenate([y_hy, y_cf.astype(dt), y_at], axis=-1) @ pl['w_out']
    return y, k, v

def _layer(x, cond, pl, lambda_init, rope=None, ctx_kv=None):
    ada = (jax.nn.silu(cond) @ pl['w_ada'] + pl['b_ada']).astype(x.dtype)
    sh1, sc1, g1, sh2, sc2, g2 = jnp.split(ada[:, None, :], 6, axis=-1)
    h = x * (1 + sc1) + sh1
    y, k, v = _token_mixers(h, pl, lambda_init, rope, ctx_kv)
    x = _layer_norm(DEEPNORM_ALPHA * x + g1 * y, pl['ln1_g'], pl['ln1_b'])
    h = x * (1 + sc2) + sh2
    m = jnp.square(jax.nn.relu(h @ pl['w_mlp1'])) @ pl['w_mlp2']
    x = _layer_norm(DEEPNORM_ALPHA * x + g2 * m, pl['ln2_g'], pl['ln2_b'])
    return x, k, v

def _lambda_init(l):
    return 0.8 - 0.6 * math.exp(-0.3 * l)

def setup_inputs(seed: int = 0) -> dict:
    key = jax.random.key(seed)
    keys = iter(jax.random.split(key, 40))
    nrm = lambda shape, s: jax.random.normal(next(keys), shape, jnp.float32) * s
    D = D_MODEL
    return {
        'x_prompt': nrm((BATCH, SEQ, D), 1.0),
        'x_sample': nrm((DEC_BATCH, DEC_SEQ, D), 1.0),
        'cache_k': nrm((DEC_BATCH, DEPTH, PAST_LEN, 2 * DIFF_HEADS, DIFF_HEAD_DIM), 1.0),
        'cache_v': nrm((DEC_BATCH, DEPTH, PAST_LEN, DIFF_HEADS, 2 * DIFF_HEAD_DIM), 1.0),
        'c': nrm((DEC_BATCH, D), 1.0),
        'c_ctx': nrm((D,), 1.0),
        'w_ada': nrm((DEPTH, D, 6 * D), D ** -0.5),
        'b_ada': nrm((DEPTH, 6 * D), 0.02),
        'w_in': nrm((DEPTH, D, IN_WIDTH), D ** -0.5),
        'hy_conv_w': nrm((DEPTH, HY_SHORT_K, 3 * HY_WIDTH), HY_SHORT_K ** -0.5),
        'hy_conv_b': nrm((DEPTH, 3 * HY_WIDTH), 0.02),
        'hf_w1': nrm((DEPTH, HY_FILTER_EMB, HY_FILTER_HIDDEN), HY_FILTER_EMB ** -0.5),
        'hf_b1': nrm((DEPTH, HY_FILTER_HIDDEN), 0.02),
        'hf_freq': 1.0 + nrm((DEPTH, HY_FILTER_HIDDEN), 0.05),
        'hf_w2': nrm((DEPTH, HY_FILTER_HIDDEN, HY_FILTER_HIDDEN), HY_FILTER_HIDDEN ** -0.5),
        'hf_b2': nrm((DEPTH, HY_FILTER_HIDDEN), 0.02),
        'hf_w3': nrm((DEPTH, HY_FILTER_HIDDEN, 2 * HY_WIDTH), HY_FILTER_HIDDEN ** -0.5),
        'hy_bias': nrm((DEPTH, HY_WIDTH), 0.1),
        'cf_conv_w': nrm((DEPTH, CF_CONV_K, CF_WIDTH), CF_CONV_K ** -0.5),
        'cf_conv_b': nrm((DEPTH, CF_WIDTH), 0.02),
        'cf_ln_g': 1.0 + nrm((DEPTH, CF_WIDTH), 0.02),
        'cf_ln_b': nrm((DEPTH, CF_WIDTH), 0.02),
        'lam_q1': nrm((DEPTH, DIFF_HEAD_DIM), 0.1),
        'lam_k1': nrm((DEPTH, DIFF_HEAD_DIM), 0.1),
        'lam_q2': nrm((DEPTH, DIFF_HEAD_DIM), 0.1),
        'lam_k2': nrm((DEPTH, DIFF_HEAD_DIM), 0.1),
        'subln_g': 1.0 + nrm((DEPTH, 2 * DIFF_HEAD_DIM), 0.02),
        'w_out': nrm((DEPTH, MIX_WIDTH, D), MIX_WIDTH ** -0.5 * DEEPNORM_BETA),
        'ln1_g': 1.0 + nrm((DEPTH, D), 0.02),
        'ln1_b': nrm((DEPTH, D), 0.02),
        'w_mlp1': nrm((DEPTH, D, D_FF), D ** -0.5),
        'w_mlp2': nrm((DEPTH, D_FF, D), D_FF ** -0.5 * DEEPNORM_BETA),
        'ln2_g': 1.0 + nrm((DEPTH, D), 0.02),
        'ln2_b': nrm((DEPTH, D), 0.02),
    }

def reference(x_prompt, x_sample, cache_k, cache_v, c, c_ctx, w_ada, b_ada, w_in,
              hy_conv_w, hy_conv_b, hf_w1, hf_b1, hf_freq, hf_w2, hf_b2, hf_w3, hy_bias,
              cf_conv_w, cf_conv_b, cf_ln_g, cf_ln_b, lam_q1, lam_k1, lam_q2, lam_k2, subln_g,
              w_out, ln1_g, ln1_b, w_mlp1, w_mlp2, ln2_g, ln2_b):
    params = {
        'w_ada': w_ada, 'b_ada': b_ada, 'w_in': w_in,
        'hy_conv_w': hy_conv_w, 'hy_conv_b': hy_conv_b,
        'hf_w1': hf_w1, 'hf_b1': hf_b1, 'hf_freq': hf_freq, 'hf_w2': hf_w2, 'hf_b2': hf_b2,
        'hf_w3': hf_w3, 'hy_bias': hy_bias,
        'cf_conv_w': cf_conv_w, 'cf_conv_b': cf_conv_b, 'cf_ln_g': cf_ln_g, 'cf_ln_b': cf_ln_b,
        'lam_q1': lam_q1, 'lam_k1': lam_k1, 'lam_q2': lam_q2, 'lam_k2': lam_k2, 'subln_g': subln_g,
        'w_out': w_out, 'ln1_g': ln1_g, 'ln1_b': ln1_b,
        'w_mlp1': w_mlp1, 'w_mlp2': w_mlp2, 'ln2_g': ln2_g, 'ln2_b': ln2_b,
    }
    xp = x_prompt
    cond_ctx = c_ctx[None, :]
    ks, vs = [], []
    for l in range(DEPTH):
        pl = {n: a[l] for n, a in params.items()}
        xp, k_l, v_l = _layer(xp, cond_ctx, pl, _lambda_init(l))
        ks.append(k_l)
        vs.append(v_l)
    new_cache_k = jnp.stack(ks, axis=1)
    new_cache_v = jnp.stack(vs, axis=1)
    rope = _axial_rope_tables(x_sample.shape[1])
    xs = x_sample
    for l in range(DEPTH):
        pl = {n: a[l] for n, a in params.items()}
        xs, _, _ = _layer(xs, c, pl, _lambda_init(l), rope, (cache_k[:, l], cache_v[:, l]))
    return (xp, xs, new_cache_k, new_cache_v)


_drawn_inputs = setup_inputs


def setup_inputs(seed=0):
    import zlib

    import numpy as np

    out = dict(_drawn_inputs(seed))
    spreads = {}
    factors = {'cache_k': 6.638,
     'cache_v': 5.756,
     'cf_conv_b': 8.0,
     'cf_ln_g': 44.181,
     'cf_ln_b': 34.758,
     'lam_q1': 8.0,
     'lam_k1': 8.0,
     'lam_q2': 8.0,
     'lam_k2': 8.0,
     'subln_g': 24.717,
     'hy_bias': 3.11}
    for name, (base, spread) in spreads.items():
        noise = np.random.default_rng([zlib.crc32(name.encode()), seed]).standard_normal(out[name].shape)
        drawn = base * np.exp(spread * noise) if base else spread * noise
        out[name] = __import__('jax').numpy.asarray(drawn.astype(out[name].dtype))
    for name, factor in factors.items():
        out[name] = (out[name] * factor).astype(out[name].dtype)
    return out
```

```python
import math
from contextlib import ExitStack

import concourse.bass as bass
from concourse import mybir

F32 = mybir.dt.float32
F32R = mybir.dt.float32r
ALU = mybir.AluOpType
ACT = mybir.ActivationFunctionType
AX_X = mybir.AxisListType.X

DEPTH = 2
D = 1024
KT = D // 128
LS, LP = 1024, 256
T = LS + LP
TT = T // 128
ST, PT = LS // 128, LP // 128
PAST = 256
CHUNKS = [(0, 512), (512, 512), (1024, 256)]
COND = [0, 0, 1]
ZT = 22
HEADS = 4
FF_T = 32
GROUPS = FF_T // 2
RING = 6
ALPHA = (2 * DEPTH) ** 0.25
EPS = 1e-5
SCALE = 64 ** -0.5
TWO_PI = 2 * math.pi
ROUND = 1.5 * 2 ** 23
PI_BELOW = 3.1415925

B_IN, B_FWD, B_INV, B_OUT, B_MLP, BLOCKS = 0, 24, 42, 60, 68, 132
LEFT_OUT = {21: 2, 40: 1, 58: 1}
REAL = [b for b in range(BLOCKS) if b not in (22, 23, 41, 59)]
RAW_OF = {b: r for r, b in enumerate(REAL)}

V_BADA, V_LN, V_HYW, V_HYB, V_BIAS, ROWS_A = 0, 32, 64, 82, 88, 90
V_CFW, V_CFB, V_CFG, V_CFBB, V_SUB, ROWS_B = 90, 152, 154, 156, 158, 69
LN_G = [V_LN, V_LN + 16]
LN_B = [V_LN + 8, V_LN + 24]
A_G1, A_SH2, A_SC2, A_G2 = 0, 8, 16, 24

KEYS = PAST + T
S_KEYS = PAST + LS
ITEMS = [(0, S_KEYS)] * ST + [(S_KEYS, LP)] * PT

UNITS = [("hyena", c, q) for c in range(2) for q in range(3)] + \
        [("conformer", c, q) for c in range(2) for q in range(3)]
A_BEFORE, A_STEPS = 0, HEADS * (TT - 1)
V_BEFORE, V_STEPS, V_HEAD = 49, 747, 52
UNIT_AT = [6, 7, 8, 9, 10, 11, 12, 13, 15, 16, 18, 19]


class Signal:

    def __init__(self, sem, per_layer, start=0):
        self.sem, self.per_layer, self.start = sem, per_layer, start

    def at(self, l, k):
        return l * self.per_layer + (k + self.start)


class Chain:

    def __init__(self, engine, sem, per_layer, before):
        self.engine, self.sem, self.per_layer, self.before = engine, sem, per_layer, before
        self.n, self.l, self.i, self.per_i, self.trips, self.at_start = 0, None, None, 0, 0, 0

    def link(self, ins):
        self.n += 1
        ins.then_inc(self.sem, 1)
        value = self.n if self.l is None else self.l * self.per_layer + (self.n + self.before)
        if self.i is not None:
            value = value + self.i * self.per_i
        self.engine.wait_ge(self.sem, value)

    def layer(self, l):
        assert self.n == self.before, self.n
        self.l, self.n = l, 0

    def loop(self, i, per_i, trips):
        self.i, self.per_i, self.trips, self.at_start = i, per_i, trips, self.n

    def end_loop(self):
        assert self.n - self.at_start == self.per_i, self.n - self.at_start
        self.n, self.i = self.at_start + self.per_i * self.trips, None

    def end_layer(self):
        assert self.n == self.per_layer, self.n


def program(nc, ins, consts, outs):
    x_prompt, x_sample, cache_k, cache_v, c, c_ctx, w_ada, b_ada, w_in, hy_conv_w, hy_conv_b, \
        hf_w1, hf_b1, hf_freq, hf_w2, hf_b2, hf_w3, hy_bias, cf_conv_w, cf_conv_b, cf_ln_g, \
        cf_ln_b, lam_q1, lam_k1, lam_q2, lam_k2, subln_g, w_out, ln1_g, ln1_b, w_mlp1, w_mlp2, \
        ln2_g, ln2_b = ins
    ident_d, swap_d, rope_d, feats_d, decay_d, dft_d, dftp_d, weight_d, lam_d = consts
    y_prompt, y_sample, new_k, new_v = outs

    z_d = nc.dram_tensor("z_scratch", (ZT, 128, T), F32, kind="Internal").ap()
    hy_d = nc.dram_tensor("hyena_scratch", (2, 2, 128, T), F32, kind="Internal").ap()
    cf_d = nc.dram_tensor("conformer_scratch", (2, 128, T), F32, kind="Internal").ap()
    y_d = nc.dram_tensor("mixed_scratch", (KT, 128, T), F32, kind="Internal").ap()

    base = (nc.sbuf_base + 63) // 64 * 64

    def place(name, shape, dtype, offset):
        return nc.alloc_sbuf_tensor_at(name, shape, dtype, offset=offset)

    class Stack:
        def __init__(self, at, end):
            self.at, self.end = at, end

        def take(self, name, shape, dtype=F32):
            n = 4
            for s in shape[1:]:
                n *= s
            t = place(name, shape, dtype, self.at)
            self.at += (n + 31) // 32 * 32
            assert self.at <= self.end, (name, self.at - self.end)
            return t

    XT_O = base
    WS = XT_O + KT * T * 4
    HID_O = WS + 2 * KT * T * 4
    ADW_O = HID_O + 16384
    RING_O = ADW_O + 8192
    RAW_O = RING_O + 2 * RING * 4096
    SMALL_O = RAW_O + 8192
    XT = place("XT", [128, KT, T], F32, XT_O)
    HH = place("HH", [128, KT, T], F32R, WS)
    HL = place("HL", [128, KT, T], F32R, WS + KT * T * 4)
    ADW = place("ADW", [128, 2, 8, 128], F32, ADW_O)
    RH = place("RH", [128, RING, 1024], F32R, RING_O)
    RL = place("RL", [128, RING, 1024], F32R, RING_O + RING * 4096)
    RAW = place("RAW", [128, 2, 1024], F32, RAW_O)

    small = Stack(SMALL_O, nc.sbuf_usable_end)
    IDENT = small.take("IDENT", [128, 128])
    SWAPF = small.take("SWAPF", [128, 128])
    SWAP = small.take("SWAP", [128, 128], F32R)
    ONES = small.take("ONES", [128, 128])
    VEC = small.take("VEC", [128, ROWS_A + ROWS_B])
    LNV = small.take("LNV", [128, 32])
    ADA = small.take("ADA", [128, 32, 2])
    AD0 = small.take("AD0", [128, DEPTH + 1, 16, 2])
    CONDS = small.take("CONDS", [128, 16])
    EPSC = small.take("EPSC", [128, 1])
    ONE = small.take("ONE", [128, 1])
    WF = small.take("WF", [128, TT])
    HFV = small.take("HFV", [128, 4])
    LAMS = small.take("LAMS", [128, 4])
    LAMC = small.take("LAMC", [128, 4])
    STAT = small.take("STAT", [128, 2, 8])
    HB2_O = small.at
    VROW = small.take("VROW", [128, 128])
    VROWB = small.take("VROWB", [128, 128])
    LAMR = small.take("LAMR", [128, 4, 64])
    KO = small.take("KO", [128, 2, 128])
    VO = small.take("VO", [128, 2, 128])

    st = Stack(HID_O, ADW_O)
    XIN = st.take("XIN", [128, 2, 1024])
    CROW = st.take("CROW", [128, 128])
    BROW = st.take("BROW", [128, 128])
    B0 = st.take("B0", [128, 32])
    CRAW = st.take("CRAW", [128, 16])
    MODT = st.take("MODT", [128, 2, 512])
    st = Stack(HID_O, ADW_O)
    ZST = st.take("ZST", [128, 2, 512])
    HYIN = place("HYIN", [128, 3, 514], F32, st.at)
    CFIN = place("CFIN", [128, 2, 542], F32, st.at)
    st.at += 6176
    CACC = st.take("CACC", [128, 2, 512])
    st = Stack(WS, RING_O)
    MH = st.take("MH", [128, TT, 768], F32R)
    ML = st.take("ML", [128, TT, 768], F32R)
    FH = st.take("FH", [128, ST, 2, 256], F32R)
    FL = st.take("FL", [128, ST, 2, 256], F32R)
    GS = st.take("GS", [128, 2, 256])
    PR = st.take("PR", [128, 2, 256])
    PR2 = st.take("PR2", [128, 2, 256])
    YF = st.take("YF", [128, 2, 256])
    FPH = place("FPH", [128, PT, 2, 256], F32R, WS)
    FPL = place("FPL", [128, PT, 2, 256], F32R, WS + 4096)
    OLD = place("OLD", [128, 2, 512], F32, WS + 8192)
    OY = place("OY", [128, 512], F32, WS + 12288)
    st2 = Stack(WS + 2 * TT * 768 * 4, RING_O)
    FEAT = st2.take("FEAT", [128, T])
    HID1 = st2.take("HID1", [128, T])
    HID2 = st2.take("HID2", [128, T])
    ARG = st2.take("ARG", [128, T])
    RND = place("RND", [128, T], F32, WS)
    HW1 = place("HW1", [128, 2, 64], F32, WS + 6144)
    HW2 = place("HW2", [128, 2, 64], F32, WS + 6656)
    HW3 = st2.take("HW3", [128, 512])
    DEC = st2.take("DEC", [128, 2, 512])
    FB = st2.take("FB", [128, 512])
    FPM = st2.take("FPM", [128, 2, 256])
    UIN = st2.take("UIN", [128, 2, T])
    st = Stack(WS, RING_O)
    KH = st.take("KH", [128, 2, KEYS], F32R)
    KL = st.take("KL", [128, 2, KEYS], F32R)
    QQ = st.take("QQ", [128, 2, T], F32R)
    V2 = st.take("V2", [128, TT + 2, 256], F32R)
    PB = st.take("PB", [128, 2, S_KEYS])
    AB = st.take("AB", [128, S_KEYS])
    ATH = st.take("ATH", [128, S_KEYS], F32R)
    ATL = st.take("ATL", [128, S_KEYS], F32R)
    OB = st.take("OB", [128, TT, 128])
    KR = st.take("KR", [128, KEYS])
    QR = st.take("QR", [128, T])
    VR = place("VR", [128, T], F32, st.at)
    st.at += 5120
    CKV = place("CKV", [128, 2, 2, 128], F32, st.at)
    st.at += 2048
    ROPE = st.take("ROPE", [128, 2, LS])
    O2 = st.take("O2", [128, 128])
    SSQ = st.take("SSQ", [128, TT])
    RRS = st.take("RRS", [128, TT])
    PB_O = WS + (2 * KEYS * 2 + 2 * T + (TT + 2) * 256) * 4
    ZHL = place("ZHL", [128, 2, 512], F32R, PB_O)
    RT = place("RT", [128, 512], F32, PB_O + 4096)
    st = Stack(HID_O, RING_O)
    YIN = st.take("YIN", [128, 2, 512])
    SQO = place("SQO", [128, 2, 512], F32, HID_O)
    st.at = HID_O + 4096
    ACC1 = st.take("ACC1", [128, 2, T])
    CFU = place("CFU", [128, 2, 512], F32, HID_O + 4096)
    CFS = place("CFS", [128, 2, 512], F32, HID_O + 8192)
    CFY = place("CFY", [128, 2, 512], F32, HID_O + 12288)
    MU = place("MU", [128, 512], F32, ADW_O)
    RS = place("RS", [128, 512], F32, ADW_O + 2048)
    LT = place("LT", [128, 512], F32, ADW_O + 4096)
    LT2 = place("LT2", [128, 512], F32, ADW_O + 6144)
    HBH = place("HBH", [128, 2, 2, 512], F32R, HID_O)
    HBL = place("HBL", [128, 2, 2, 512], F32R, HID_O + 8192)
    HB2H = place("HB2H", [128, 2, 256], F32R, HB2_O)
    HB2L = place("HB2L", [128, 2, 256], F32R, HB2_O + 2048)
    RB = place("RB", [128, 2, 512], F32, ADW_O)
    SB2 = place("SB2", [128, 2, 512], F32, ADW_O + 4096)
    ACC2 = place("ACC2", [128, 2, T], F32, WS + KT * T * 4)
    SQM = place("SQM", [128, 2, T], F32, WS)

    def hidden_hi(q):
        return HBH[:, q] if q < 2 else HB2H[:]

    def hidden_lo(q):
        return HBL[:, q] if q < 2 else HB2L[:]

    nc.disable_value_cache = True
    with ExitStack() as ctx:
        PS = ctx.enter_context(nc.psum_tensor("PS", [128, 8, 512], F32))
        PSF = PS[:, :, :].rearrange("p b n -> p (b n)")

        def signal(name, per_layer=0, start=0):
            return Signal(ctx.enter_context(nc.semaphore(name)), per_layer, start)

        raw_in = [signal(f"raw_in{p}", 64 * 16) for p in range(2)]
        hi_split = signal("hi_split", len(REAL))
        blk_ready = signal("blk_ready", BLOCKS, BLOCKS)
        blk_used = signal("blk_used", BLOCKS, RING)
        ada_in = [signal(f"ada_in{p}", 16 * 16, 16 * 16) for p in range(2)]
        ada_used = signal("ada_used", 32, 34)
        const_in = signal("const_in")
        const_done = signal("const_done")
        one_ready = signal("one_ready")
        x_in = [signal(f"x_in{p}") for p in range(2)]
        x_turned = signal("x_turned")
        x_placed = signal("x_placed")
        row_turned = signal("row_turned")
        row_placed = signal("row_placed")
        silu_done = signal("silu_done")
        vec_in = signal("vec_in", 21 * 16)
        vec_turned = signal("vec_turned", 1)
        vec_ready = signal("vec_ready", 1)
        xn_ready = signal("xn_ready", 48)
        xs_ready = signal("xs_ready", 48)
        hh_ready = signal("hh_ready", 48, 24)
        h_ready = signal("h_ready", 6, 3)
        var_ready = signal("var_ready", 6, 6)
        sd_ready = signal("sd_ready", 6)
        acc_ready = signal("acc_ready", 6)
        stats = signal("stats", 6)
        z_psum = signal("z_psum", 44)
        z_evac = signal("z_evac", 66, 6)
        z_stored = [signal(f"z_stored{p}", 33 * 16, 16) for p in range(2)]
        conv_in = signal("conv_in", 480)
        conv_done = signal("conv_done", 12, 1)
        conv_stored = signal("conv_stored", 288, 16)
        glu_done = signal("glu_done", 6)
        hf_in = signal("hf_in", 6 * 16)
        hf_psum = signal("hf_psum", 6)
        hf_read = signal("hf_read", 6)
        hf_arg = signal("hf_arg", 2)
        hf_sin = signal("hf_sin", 2)
        dec_in = [signal(f"dec_in{p}", 5 * 16) for p in range(2)]
        hft_psum = signal("hft_psum", TT)
        hft_read = signal("hft_read", TT, 1)
        dec_read = signal("dec_read", TT, 2)
        m_sum = signal("m_sum", TT)
        m_hi = signal("m_hi", TT)
        filt_ready = signal("filt_ready", TT)
        u_in = signal("u_in", 32)
        u_psum = signal("u_psum", TT)
        u_hi = signal("u_hi", TT)
        u_ready = signal("u_ready", TT, 2)
        dft_psum = signal("dft_psum", 1)
        g_scaled = signal("g_scaled", TT)
        f_sum = signal("f_sum", TT)
        f_hi = signal("f_hi", TT)
        f_ready = signal("f_ready", TT)
        inv_done = signal("inv_done", 0)
        old_in = signal("old_in", 6 * 32)
        old_read = signal("old_read", 6, 1)
        hy_done = signal("hy_done", 6)
        hy_stored = signal("hy_stored", 6 * 16, 16)
        at_tab = signal("at_tab", 16)
        lam_ready = signal("lam_ready", 1)
        lam_known = signal("lam_known", 1)
        head_in = signal("head_in", HEADS * 5 * 16)
        head_raw_free = signal("head_raw_free", HEADS, 1)
        prep_turned = signal("prep_turned", HEADS)
        kc_placed = signal("kc_placed", HEADS)
        v_hi = signal("v_hi", HEADS)
        v_split = signal("v_split", HEADS)
        rope_hi = signal("rope_hi", HEADS * 4)
        rope_lo = signal("rope_lo", HEADS * 4)
        rope_swapped = signal("rope_swapped", HEADS * 4)
        rope_done = signal("rope_done", HEADS * 4)
        qk_hi = signal("qk_hi", HEADS * 6)
        prep_done = signal("prep_done", HEADS)
        s_psum = signal("s_psum", HEADS * TT * 2)
        smax = signal("smax", HEADS * TT * 2)
        probs = signal("probs", HEADS * TT * 2)
        mixed = signal("mixed", HEADS * TT)
        at_psum = signal("at_psum", HEADS * (ST * 3 + PT))
        at_hi = signal("at_hi", HEADS * (ST * 3 + PT))
        at_lo = signal("at_lo", HEADS * (ST * 3 + PT))
        pv_psum = signal("pv_psum", HEADS * TT)
        o_part = signal("o_part", HEADS * TT)
        o_ready = signal("o_ready", HEADS * TT)
        ssq_done = signal("ssq_done", HEADS)
        sd_head = signal("sd_head", HEADS)
        o_normed = signal("o_normed", HEADS)
        o_turned = signal("o_turned", HEADS)
        o_placed = signal("o_placed", HEADS)
        kv_copied = signal("kv_copied", HEADS)
        kv_stored = signal("kv_stored", HEADS * 32, 32)
        yat_stored = signal("yat_stored", HEADS * 16, 16)
        y_in = [signal(f"y_in{p}", 9 * 16) for p in range(2)]
        y_hi = signal("y_hi", 24)
        y_lo = signal("y_lo", 24, 2)
        cf_in = signal("cf_in", 6 * 16)
        cf_sq = signal("cf_sq", 3)
        cf_stats = signal("cf_stats", 3)
        cf_var = signal("cf_var", 3)
        cf_sd = signal("cf_sd", 3)
        cf_norm = signal("cf_norm", 3)
        cf_silu = signal("cf_silu", 3)
        o_psum = signal("o_psum", 16)
        o_evac = signal("o_evac", 24, 6)
        sq_ready = signal("sq_ready", 48)
        sq_added = signal("sq_added", 48, 2)
        m1_psum = signal("m1_psum", GROUPS * 4)
        relu_done = signal("relu_done", GROUPS * 6)
        hid_hi = signal("hid_hi", GROUPS * 6)
        hid_ready = signal("hid_ready", GROUPS * 6, 2)
        m2_psum = signal("m2_psum", GROUPS * 23, 16)
        m2_evac = signal("m2_evac", GROUPS * 24, 6)
        y_turned = signal("y_turned")
        y_placed = signal("y_placed")
        y_stored = [signal(f"y_stored{p}") for p in range(2)]
        pads_ready = signal("pads_ready", 6)
        sq_kept = signal("sq_kept", GROUPS * 6)
        lam_exp = signal("lam_exp", 1)
        v_chain = ctx.enter_context(nc.semaphore("v_chain"))
        a_chain = ctx.enter_context(nc.semaphore("a_chain"))

        block = ctx.enter_context(nc.Block())

        def column_block(w, l, j):
            return w[l].rearrange("(k p) n -> p k n", p=128)[:, :, bass.ts(j, 128)]

        def raw_view(p):
            return RAW[:, p, :].rearrange("p (k n) -> p k n", k=8)

        def dft_columns(part, j):
            return dft_d[part].rearrange("(k p) n -> p k n", p=128)[:, :, j * 128:(j + 1) * 128]

        def dft_rows(part, j):
            return dft_d[part, j * 128:(j + 1) * 128, :]

        @block.sync
        def _(sp):
            def load_block(l, b, i, source, view3):
                r = RAW_OF[b]
                p = r % 2
                if r >= 2:
                    before = REAL[r - 2] + 1
                else:
                    before = REAL[r - 2] + 1 - BLOCKS
                sp.wait_ge(blk_ready.sem, blk_ready.at(l, before) + i * RING)
                sp.dma_start(raw_view(p) if view3 else RAW[:, p, :], source).then_inc(raw_in[p].sem, 16)

            def load_ada(l, a, t):
                sp.wait_ge(ada_used.sem, ada_used.at(l, a - 1))
                sp.dma_start(ADW[:, a % 2], column_block(w_ada, l, t)).then_inc(ada_in[a % 2].sem, 16)

            for n, (dst, src) in enumerate([(IDENT[:], ident_d), (SWAPF[:], swap_d), (WF[:], weight_d),
                                            (CROW[0:8, :], c.rearrange("a (k p) -> (a k) p", p=128)),
                                            (CROW[8:16, :], c_ctx.rearrange("(k p) -> k p", p=128)),
                                            (BROW[0:16, :], b_ada[0, 0:2048].rearrange("(k p) -> k p", p=128)),
                                            (BROW[16:32, :], b_ada[1, 0:2048].rearrange("(k p) -> k p", p=128))]):
                sp.dma_start(dst, src).then_inc(const_in.sem, 16)
            for t in range(TT):
                if t >= 2:
                    sp.wait_ge(x_turned.sem, t - 1)
                src = x_sample[0, t * 128:(t + 1) * 128, :] if t < ST else \
                    x_prompt[0, (t - ST) * 128:(t - ST + 1) * 128, :]
                sp.dma_start(XIN[:, t % 2], src).then_inc(x_in[t % 2].sem, 16)
            for a in range(32):
                sp.wait_ge(ada_used.sem, a + 1)
                sp.dma_start(ADW[:, a % 2], column_block(w_ada, a // 16, a % 16)).then_inc(ada_in[a % 2].sem, 16)

            with sp.Fori(0, DEPTH) as l:
                with sp.Fori(0, 2) as i:
                    for q in range(6):
                        load_block(l, B_IN + q, i, column_block(w_in, l, i * 6 + q), True)
                        if q == 0:
                            sp.wait_ge(h_ready.sem, h_ready.at(l, 0))
                        for e in range(2):
                            a = 2 * q + e
                            sp.wait_ge(ada_used.sem, ada_used.at(l, a - 1) + i * 12)
                            sp.dma_start(ADW[:, a % 2], column_block(w_ada, l, i * 12 + (16 + a)))\
                              .then_inc(ada_in[a % 2].sem, 16)
                for q in range(12, ZT):
                    load_block(l, B_IN + q, 0, column_block(w_in, l, q), True)
                    if q < 16:
                        for e in range(2):
                            load_ada(l, 2 * q + e, 16 + 2 * q + e)
                for j in range(ST):
                    for part in range(2):
                        load_block(l, B_FWD + 2 * j + part, 0, dft_columns(part, j), True)
                load_block(l, B_FWD + 16, 0, dftp_d, False)
                for j in range(ST):
                    for part in range(2):
                        load_block(l, B_INV + 2 * j + part, 0, dft_rows(part, j), False)
                load_block(l, B_INV + 16, 0, dftp_d, False)

                for p in range(2):
                    sp.wait_ge(z_stored[p].sem, z_stored[p].at(l, 33 * 16))
                sp.wait_ge(hy_stored.sem, hy_stored.at(l, 6 * 16))
                sp.dma_start(ROPE[:], rope_d).then_inc(at_tab.sem, 16)
                with sp.Fori(0, HEADS) as h:
                    sp.wait_ge(head_raw_free.sem, head_raw_free.at(l, 0) + h)
                    sp.dma_start(KR[:, PAST:KEYS], z_d[h + 14]).then_inc(head_in.sem, 16)
                    sp.dma_start(QR[:], z_d[h + 10]).then_inc(head_in.sem, 16)
                    sp.dma_start(VR[:], z_d[h + 18]).then_inc(head_in.sem, 16)
                    sp.dma_start(CKV[:, 0], cache_k[0, l].rearrange("(t p) m d -> p t (m d)", p=128)
                                 [:, :, bass.ts(h, 128)]).then_inc(head_in.sem, 16)
                    sp.dma_start(CKV[:, 1], cache_v[0, l].rearrange("(t p) m d -> p t (m d)", p=128)
                                 [:, :, bass.ts(h, 128)]).then_inc(head_in.sem, 16)
                sp.wait_ge(yat_stored.sem, yat_stored.at(l, HEADS * 16))
                n = 0
                for q, (t0, tn) in enumerate(CHUNKS):
                    if q:
                        sp.wait_ge(cf_norm.sem, cf_norm.at(l, q))
                    for ct in range(2):
                        sp.dma_start(CFU[:, ct, :tn], cf_d[ct, :, t0:t0 + tn]).then_inc(cf_in.sem, 16)
                    for j in (0, 1, 4, 5, 6, 7):
                        before = 8 * ((n - 2) // 6) + (n - 2) % 6 + 1 if n >= 2 else 0
                        sp.wait_ge(y_lo.sem, y_lo.at(l, before))
                        sp.dma_start(YIN[:, n % 2, :tn], y_d[j, :, t0:t0 + tn]).then_inc(y_in[n % 2].sem, 16)
                        n += 1
                for q in range(8):
                    load_block(l, B_OUT + q, 0, column_block(w_out, l, q), True)
                with sp.Fori(0, GROUPS) as g:
                    for e in range(4):
                        b = B_MLP + e
                        p = RAW_OF[b] % 2
                        sp.wait_ge(blk_ready.sem, blk_ready.at(l, b - 1) + g * 4)
                        if e < 2:
                            sp.dma_start(raw_view(p), column_block(w_mlp1, l, g * 2 + e)).then_inc(raw_in[p].sem, 16)
                        else:
                            sp.dma_start(RAW[:, p, :], w_mlp2[l].rearrange("(j p) n -> j p n", p=128)[g * 2 + (e - 2)])\
                              .then_inc(raw_in[p].sem, 16)

        @block.gpsimd
        def _(pool):
            for freed in [blk_ready, blk_used, z_evac, *z_stored, conv_done, conv_stored, var_ready,
                          hft_read, dec_read, u_ready, old_read, hy_stored, head_raw_free,
                          kv_stored, yat_stored, y_lo, o_evac, sq_added, hid_ready, m2_psum, m2_evac]:
                pool.sem_inc(freed.sem, freed.start)
            pool.sem_inc(ada_used.sem, 2)
            nc.gpsimd.memset(ONE[:], 1.0).then_inc(one_ready.sem, 1)
            pool.wait_ge(one_ready.sem, 1)

            def split(l, b, i, per_i):
                r, s = RAW_OF[b], b % RING
                p = r % 2
                pool.wait_ge(raw_in[p].sem, raw_in[p].at(l, 16 * (r // 2 + 1)) + i * (8 * per_i))
                pool.wait_ge(blk_used.sem, blk_used.at(l, b - RING + 1) + i * per_i)
                nc.gpsimd.tensor_tensor(RH[:, s, :], RAW[:, p, :], ONE[:].broadcast_to([128, 1024]), ALU.mult).then_inc(hi_split.sem, 1)
                pool.wait_ge(hi_split.sem, hi_split.at(l, r + 1) + i * per_i)
                nc.gpsimd.tensor_tensor(RL[:, s, :], RAW[:, p, :], RH[:, s, :].bitcast(F32), ALU.subtract)\
                  .then_inc(blk_ready.sem, 1 + LEFT_OUT.get(b, 0))

            with pool.Fori(0, DEPTH) as l:
                with pool.Fori(0, 2) as i:
                    for q in range(6):
                        split(l, B_IN + q, i, 6)
                for b in REAL[12:RAW_OF[B_MLP] + 4]:
                    split(l, b, 0, 4)
                with pool.Fori(0, 5) as i:
                    for q in range(12):
                        split(l, B_MLP + 4 + q, i, 12)

        @block.tensor
        def _(pe):
            def weights_ready(l, b, i=0, per_i=0):
                pe.wait_ge(blk_ready.sem, blk_ready.at(l, b + 1) + i * per_i)

            def column_product(out, s, hi, lo):
                for n, (w, m) in enumerate(((RH, hi), (RH, lo), (RL, hi))):
                    for k in range(KT):
                        mm = pe.matmul(out, w[:, s, k * 128:(k + 1) * 128], m(k),
                                       start=(n == 0 and k == 0), stop=(n == 2 and k == KT - 1))
                return mm

            pe.wait_ge(const_in.sem, 7 * 16)
            pe.transpose(PS[:, 6, 0:16], CROW[0:16, :], IDENT[0:16, 0:16])
            pe.transpose(PS[:, 6, 16:48], BROW[0:32, :], IDENT[0:32, 0:32]).then_inc(row_turned.sem, 1)
            for t in range(TT):
                pe.wait_ge(x_in[t % 2].sem, 16 * (t // 2 + 1))
                if t >= 2:
                    pe.wait_ge(x_placed.sem, t - 1)
                for j in range(KT):
                    mm = pe.transpose(PSF[:, (t % 2) * 1024 + j * 128:(t % 2) * 1024 + (j + 1) * 128],
                                      XIN[:, t % 2, j * 128:(j + 1) * 128], IDENT[:])
                mm.then_inc(x_turned.sem, 1)
            pe.wait_ge(silu_done.sem, 1)

            def ada_tile(a, col):
                cv = CONDS[:, :].rearrange("p (v k) -> p k v", v=2)
                for k in range(KT):
                    mm = pe.matmul(PS[:, 7, 2 * col:2 * col + 2], ADW[:, a % 2, k, :], cv[:, k, :],
                                   start=(k == 0), stop=(k == KT - 1))
                mm.then_inc(ada_used.sem, 1)

            for a in range(32):
                pe.wait_ge(ada_in[a % 2].sem, 16 * (a // 2 + 1))
                ada_tile(a, a)

            with pe.Fori(0, DEPTH) as l:
                def z_tile(n, i, per_i):
                    s, p = n % RING, n % 2
                    weights_ready(l, B_IN + n, i, per_i)
                    for q, (t0, tn) in enumerate(CHUNKS):
                        if n == 0:
                            pe.wait_ge(h_ready.sem, h_ready.at(l, q - 3 + 1))
                            pe.wait_ge(var_ready.sem, var_ready.at(l, -1))
                        pe.wait_ge(z_evac.sem, z_evac.at(l, 3 * n + q - 5) + i * (3 * per_i))
                        mm = column_product(PS[:, 3 * p + q, 0:tn], s, lambda k: HH[:, k, t0:t0 + tn],
                                            lambda k: HL[:, k, t0:t0 + tn])
                        if q < 2:
                            mm.then_inc(z_psum.sem, 1)
                    mm.then_inc(blk_used.sem, 1 + LEFT_OUT.get(n, 0))

                def vectors():
                    pe.wait_ge(h_ready.sem, h_ready.at(l, -2))
                    pe.wait_ge(vec_in.sem, vec_in.at(l, 16 * 21))
                    pe.transpose(PS[:, 6, 0:ROWS_A], VROW[0:ROWS_A, :], IDENT[0:ROWS_A, 0:ROWS_A])
                    pe.transpose(PS[:, 6, ROWS_A:ROWS_A + ROWS_B], VROWB[0:ROWS_B, :],
                                 IDENT[0:ROWS_B, 0:ROWS_B]).then_inc(vec_turned.sem, 1)

                vectors()
                with pe.Fori(0, 2) as i:
                    for n in range(6):
                        z_tile(n, i, 6)
                        for e in range(2):
                            a = 2 * n + e
                            pe.wait_ge(ada_in[a % 2].sem, ada_in[a % 2].at(l, 16 * (a // 2 + 1)) + i * 96)
                            for k in range(KT):
                                mm = pe.matmul(PS[:, 7, bass.ds(i * 24 + 2 * a, 2)], ADW[:, a % 2, k, :],
                                               CONDS[:, :].rearrange("p (v k) -> p k v", v=2)[:, k, :],
                                               start=(k == 0), stop=(k == KT - 1))
                            mm.then_inc(ada_used.sem, 1)
                for n in range(12, ZT):
                    z_tile(n, 0, 0)
                    if n < 16:
                        for e in range(2):
                            a = 2 * n + e
                            pe.wait_ge(ada_in[a % 2].sem, ada_in[a % 2].at(l, 16 * (a // 2 + 1)))
                            ada_tile(a, a)

                pe.wait_ge(hf_in.sem, hf_in.at(l, 6 * 16))
                pe.wait_ge(z_evac.sem, z_evac.at(l, 66))
                for layer_no, (w, kk, src) in enumerate(((HW1, 33, FEAT), (HW2, 64, HID1))):
                    if layer_no:
                        pe.wait_ge(hf_sin.sem, hf_sin.at(l, 1))
                    for q, (t0, tn) in enumerate(CHUNKS):
                        pe.matmul(PS[:, 3 * layer_no + q, 0:tn], w[0:kk].rearrange("p a n -> p (a n)"), src[0:kk, t0:t0 + tn],
                                  start=True, stop=True).then_inc(hf_psum.sem, 1)
                pe.wait_ge(hf_sin.sem, hf_sin.at(l, 2))
                pe.wait_ge(u_in.sem, u_in.at(l, 32))
                for t in range(TT):
                    pe.wait_ge(hft_read.sem, hft_read.at(l, max(t - 1, 0)))
                    pe.matmul(PS[:, t % 2, :], HID2[0:64, t * 128:(t + 1) * 128], HW3[0:64, :],
                              start=True, stop=True).then_inc(hft_psum.sem, 1)
                    pe.wait_ge(u_ready.sem, u_ready.at(l, t - 1))
                    for ct in range(2):
                        mm = pe.transpose(PS[:, 2 + t % 2, ct * 128:(ct + 1) * 128],
                                          UIN[:, ct, t * 128:(t + 1) * 128], IDENT[:])
                    mm.then_inc(u_psum.sem, 1)
                pe.wait_ge(filt_ready.sem, filt_ready.at(l, TT))
                pe.wait_ge(u_ready.sem, u_ready.at(l, TT))
                for j in range(ST):
                    for part in range(2):
                        b = B_FWD + 2 * j + part
                        weights_ready(l, b)
                        if j >= 2:
                            pe.wait_ge(f_sum.sem, f_sum.at(l, j - 1))
                        c0 = 256 * part
                        column_product(PS[:, 2 * (j % 2) + part, :], b % RING,
                                       lambda k: MH[:, k, c0:c0 + 512], lambda k: ML[:, k, c0:c0 + 512])\
                            .then_inc(blk_used.sem, 1)
                b = B_FWD + 16
                weights_ready(l, b)
                pblk = [W[:, b % RING, :].rearrange("p (t n) -> p t n", t=2) for W in (RH, RL)]
                for j in range(PT):
                    pe.wait_ge(f_sum.sem, f_sum.at(l, ST + j - 1))
                    for part in range(2):
                        c0, f0 = 256 * part, 256 * part + 128 * j
                        for n, (w, m) in enumerate(((pblk[0], MH), (pblk[0], ML), (pblk[1], MH))):
                            for k in range(PT):
                                mm = pe.matmul(PS[:, 2 * (j % 2) + part, :], w[:, k, f0:f0 + 128],
                                               m[:, ST + k, c0:c0 + 512],
                                               start=(n == 0 and k == 0), stop=(n == 2 and k == 1))
                    if j == 0:
                        mm.then_inc(dft_psum.sem, 1)
                mm.then_inc(blk_used.sem, 2)
                for j in range(ST):
                    for part in range(2):
                        b = B_INV + 2 * j + part
                        weights_ready(l, b)
                        if part == 0:
                            pe.wait_ge(f_ready.sem, f_ready.at(l, j + 1))
                        for ct in range(2):
                            for n, (f, w) in enumerate(((FH, RH), (FH, RL), (FL, RH))):
                                for q in range(2):
                                    mm = pe.matmul(PS[:, 4 + 2 * ct + q, :], f[:, j, part, ct * 128:(ct + 1) * 128],
                                                   w[:, b % RING, q * 512:(q + 1) * 512],
                                                   start=(j == 0 and part == 0 and n == 0),
                                                   stop=(j == ST - 1 and part == 1 and n == 2))
                        mm.then_inc(blk_used.sem, 1)
                b = B_INV + 16
                weights_ready(l, b)
                pe.wait_ge(f_ready.sem, f_ready.at(l, TT))
                pblk = [W[:, b % RING, :].rearrange("p (t n) -> p t n", t=2) for W in (RH, RL)]
                for ct in range(2):
                    for j in range(PT):
                        for part in range(2):
                            for n, (f, w) in enumerate(((FPH, pblk[0]), (FPH, pblk[1]), (FPL, pblk[0]))):
                                mm = pe.matmul(PS[:, ct, 0:256], f[:, j, part, ct * 128:(ct + 1) * 128],
                                               w[:, j, 256 * part:256 * part + 256],
                                               start=(j == 0 and part == 0 and n == 0),
                                               stop=(j == 1 and part == 1 and n == 2))
                mm.then_inc(blk_used.sem, 2)

                with pe.Fori(0, HEADS) as h:
                    pe.wait_ge(hy_done.sem, hy_done.at(l, 6))
                    pe.wait_ge(head_in.sem, head_in.at(l, 80) + h * 80)
                    for t in range(2):
                        pe.transpose(PS[:, 0, t * 128:(t + 1) * 128], CKV[:, 0, t, :], IDENT[:])
                        pe.transpose(PS[:, 0, 256 + t * 128:256 + (t + 1) * 128],
                                     KR[:, S_KEYS + t * 128:S_KEYS + (t + 1) * 128], IDENT[:])
                    for t in range(TT):
                        mm = pe.transpose(PSF[:, 512 + t * 128:512 + (t + 1) * 128],
                                          VR[:, t * 128:(t + 1) * 128], IDENT[:])
                    mm.then_inc(prep_turned.sem, 1)
                    for n in range(4):
                        pe.wait_ge(rope_lo.sem, rope_lo.at(l, n + 1) + h * 4)
                        pe.matmul(PS[:, 4 + n % 2, :], SWAP[:], ZHL[:, 0, :], start=True, stop=False)
                        pe.matmul(PS[:, 4 + n % 2, :], SWAP[:], ZHL[:, 1, :], start=False, stop=True)\
                            .then_inc(rope_swapped.sem, 1)
                    pe.wait_ge(prep_done.sem, prep_done.at(l, 1) + h)
                    n_at = 0

                    def scores(t):
                        k0, kn = ITEMS[t]
                        for m in range(2):
                            if t:
                                pe.wait_ge(probs.sem, probs.at(l, 2 * t - 1 + m) + h * (2 * TT))
                            pieces = [(o, min(512, kn - o)) for o in range(0, kn, 512)]
                            for o, w in pieces:
                                for x, kk in enumerate((KH, KL)):
                                    mm = pe.matmul(PSF[:, 1536 * m + o:1536 * m + o + w],
                                                   QQ[:, m, t * 128:(t + 1) * 128],
                                                   kk[:, m, k0 + o:k0 + o + w], start=(x == 0), stop=(x == 1))
                            mm.then_inc(s_psum.sem, 1)

                    scores(0)
                    for t in range(TT):
                        if t + 1 < TT:
                            scores(t + 1)
                        k0, kn = ITEMS[t]
                        pe.wait_ge(mixed.sem, mixed.at(l, t + 1) + h * TT)
                        for r, g0 in enumerate(range(0, kn // 128, 4)):
                            gn = min(4, kn // 128 - g0)
                            bank = 6 + r % 2
                            if r == 0 and t:
                                pe.wait_ge(o_ready.sem, o_ready.at(l, t) + h * TT)
                            if r == 2:
                                pe.wait_ge(at_lo.sem, at_lo.at(l, n_at - 1) + h * (ST * 3 + PT))
                            for e in range(gn):
                                mm = pe.transpose(PS[:, bank, e * 128:(e + 1) * 128],
                                                  AB[:, (g0 + e) * 128:(g0 + e + 1) * 128], IDENT[:])
                            mm.then_inc(at_psum.sem, 1)
                            n_at += 1
                        pe.wait_ge(at_lo.sem, at_lo.at(l, n_at) + h * (ST * 3 + PT))
                        nk = kn // 128
                        for k in range(nk):
                            kt = k0 // 128 + k
                            pe.matmul(PS[:, 7, 0:256], ATH[:, k * 128:(k + 1) * 128], V2[:, kt, :],
                                      start=(k == 0), stop=False)
                            mm = pe.matmul(PS[:, 7, 0:128], ATL[:, k * 128:(k + 1) * 128], V2[:, kt, 0:128],
                                           start=False, stop=(k == nk - 1))
                        mm.then_inc(pv_psum.sem, 1)
                    pe.wait_ge(o_normed.sem, o_normed.at(l, 1) + h)
                    for t in range(TT):
                        mm = pe.transpose(PSF[:, t * 128:(t + 1) * 128], OB[:, t, :], IDENT[:])
                    mm.then_inc(o_turned.sem, 1)
                    pe.wait_ge(o_placed.sem, o_placed.at(l, 1) + h)

                for q, (t0, tn) in enumerate(CHUNKS):
                    pe.wait_ge(cf_sq.sem, cf_sq.at(l, q + 1))
                    pe.wait_ge(cf_in.sem, cf_in.at(l, 32 * (q + 1)))
                    for n, src in enumerate((CFU, CFS)):
                        for ct in range(2):
                            mm = pe.matmul(PS[:, 6 + n, 0:tn], ONES[:], src[:, ct, 0:tn], start=(ct == 0), stop=(ct == 1))
                    mm.then_inc(cf_stats.sem, 1)

                for n in range(KT):
                    b = B_OUT + n
                    weights_ready(l, b)
                    for q, (t0, tn) in enumerate(CHUNKS):
                        if n == 0:
                            pe.wait_ge(y_lo.sem, y_lo.at(l, 8 * (q + 1)))
                        pe.wait_ge(o_evac.sem, o_evac.at(l, 3 * n + q - 5))
                        mm = column_product(PS[:, 3 * (n % 2) + q, 0:tn], b % RING,
                                            lambda k: HH[:, k, t0:t0 + tn], lambda k: HL[:, k, t0:t0 + tn])
                        if q < 2:
                            mm.then_inc(o_psum.sem, 1)
                    mm.then_inc(blk_used.sem, 1)

                def norm_sums(which):
                    acc = (ACC1, ACC2)[which]
                    for q, (t0, tn) in enumerate(CHUNKS):
                        pe.wait_ge(acc_ready.sem, acc_ready.at(l, 6 if which else q + 1))
                        bank = (6, 0, 2)[q]
                        for n in range(2):
                            mm = pe.matmul(PS[:, bank + n, 0:tn], ONES[:], acc[:, n, t0:t0 + tn], start=True, stop=True)
                        mm.then_inc(stats.sem, 1)

                norm_sums(0)

                def up(g0, q, i):
                    t0, tn = CHUNKS[q]
                    for e in range(2):
                        b = B_MLP + 4 * g0 + e
                        if q == 0:
                            weights_ready(l, b, i, 12)
                        if e == 0:
                            pe.wait_ge(hid_ready.sem, hid_ready.at(l, 2 * (3 * g0 + q)) + i * 18)
                        mm = column_product(PS[:, e, 0:tn], b % RING,
                                            lambda k: HH[:, k, t0:t0 + tn], lambda k: HL[:, k, t0:t0 + tn])
                        if q < 2:
                            mm.then_inc(m1_psum.sem, 1)
                        else:
                            mm.then_inc(blk_used.sem, 1)

                def down(g0, q, i):
                    t0, tn = CHUNKS[q]
                    b = B_MLP + 4 * g0 + 2
                    if q == 0:
                        weights_ready(l, b + 1, i, 12)
                    pe.wait_ge(hid_ready.sem, hid_ready.at(l, 2 * (3 * g0 + q) + 2) + i * 18)
                    for j in range(KT):
                        m = 8 * (3 * g0 + q) + j
                        pe.wait_ge(m2_evac.sem, m2_evac.at(l, m - 5) + i * 72)
                        for n, (w, x) in enumerate(((RH, hidden_hi(q)), (RH, hidden_lo(q)), (RL, hidden_hi(q)))):
                            for e in range(2):
                                mm = pe.matmul(PS[:, 2 + m % 6, 0:tn], w[:, (b + e) % RING, j * 128:(j + 1) * 128],
                                               x[:, e, 0:tn], start=(n == 0 and e == 0),
                                               stop=(n == 2 and e == 1))
                        if q == 2 and j == KT - 1:
                            mm.then_inc(blk_used.sem, 2)
                        else:
                            mm.then_inc(m2_psum.sem, 1)

                for q in range(3):
                    pe.wait_ge(h_ready.sem, h_ready.at(l, q + 1))
                    pe.wait_ge(var_ready.sem, var_ready.at(l, min(q + 2, 3)))
                    up(0, q, 0)
                    if q:
                        down(0, q - 1, 0)
                with pe.Fori(0, 5) as i:
                    for g in range(1, 4):
                        up(g, 0, i)
                        down(g - 1, 2, i)
                        up(g, 1, i)
                        down(g, 0, i)
                        up(g, 2, i)
                        down(g, 1, i)
                down(GROUPS - 1, 2, 0)
                norm_sums(1)

            pe.wait_ge(h_ready.sem, h_ready.at(DEPTH - 1, 6))
            for t in range(TT):
                if t >= 2:
                    pe.wait_ge(y_placed.sem, t - 1)
                for j in range(KT):
                    mm = pe.transpose(PSF[:, (t % 2) * 1024 + j * 128:(t % 2) * 1024 + (j + 1) * 128],
                                      XT[:, j, t * 128:(t + 1) * 128], IDENT[:])
                mm.then_inc(y_turned.sem, 1)

        @block.scalar
        def _(act):
            A = Chain(act, a_chain, A_STEPS, A_BEFORE)
            S = nc.scalar

            act.wait_ge(row_placed.sem, 1)
            S.activation(CONDS[:], CRAW[:], ACT.Silu).then_inc(silu_done.sem, 1)
            for t in range(TT):
                act.wait_ge(x_turned.sem, t + 1)
                for half in range(2):
                    ins = S.activation(XT[:, 4 * half:4 * half + 4, t * 128:(t + 1) * 128],
                                       PS[:, 2 * (t % 2) + half, :].rearrange("p (j n) -> p j n", j=4),
                                       ACT.Copy, scale=ALPHA)
                ins.then_inc(x_placed.sem, 1)

            def hi_of_h(j, q, scale, bias):
                t0, tn = CHUNKS[q]
                S.activation(HH[:, j, t0:t0 + tn], XT[:, j, t0:t0 + tn], ACT.Identity, scale=scale, bias=bias)\
                    .then_inc(hh_ready.sem, 1)

            act.wait_ge(const_done.sem, 1)
            act.wait_ge(x_placed.sem, TT)
            for q in range(3):
                v = COND[q]
                for j in range(KT):
                    hi_of_h(j, q, AD0[:, 0, 8 + j, v:v + 1], AD0[:, 0, j, v:v + 1])

            def norm(l, which):
                for q, (t0, tn) in enumerate(CHUNKS):
                    v = COND[q]
                    act.wait_ge(var_ready.sem, var_ready.at(l, 3 * which + q + 1))
                    S.activation(RS[:, :tn], RS[:, :tn], ACT.Sqrt, bias=EPSC[:, 0:1]).then_inc(sd_ready.sem, 1)
                    for j in range(KT):
                        n = 8 * (3 * which + q) + j
                        act.wait_ge(xn_ready.sem, xn_ready.at(l, n + 1))
                        S.activation(XT[:, j, t0:t0 + tn], XT[:, j, t0:t0 + tn], ACT.Identity,
                                     scale=LNV[:, 16 * which + j:16 * which + j + 1],
                                     bias=LNV[:, 16 * which + 8 + j:16 * which + 9 + j]).then_inc(xs_ready.sem, 1)
                        act.wait_ge(xs_ready.sem, xs_ready.at(l, n + 1))
                        if which:
                            hi_of_h(j, q, AD0[:, bass.ds(l + 1, 1), 8 + j, v:v + 1].rearrange("p a b -> p (a b)"),
                                    AD0[:, bass.ds(l + 1, 1), j, v:v + 1].rearrange("p a b -> p (a b)"))
                        else:
                            hi_of_h(j, q, ADA[:, A_SC2 + j, v:v + 1], ADA[:, A_SH2 + j, v:v + 1])

            with act.Fori(0, DEPTH) as l:
                A.layer(l)
                rows_a = [(V_BADA, b_ada[l].rearrange("(r p) -> r p", p=128)[16:48]),
                          (V_LN, ln1_g[l].rearrange("(r p) -> r p", p=128)),
                          (V_LN + 8, ln1_b[l].rearrange("(r p) -> r p", p=128)),
                          (V_LN + 16, ln2_g[l].rearrange("(r p) -> r p", p=128)),
                          (V_LN + 24, ln2_b[l].rearrange("(r p) -> r p", p=128)),
                          (V_HYW, hy_conv_w[l].rearrange("k (r p) -> (k r) p", p=128)),
                          (V_HYB, hy_conv_b[l].rearrange("(r p) -> r p", p=128)),
                          (V_BIAS, hy_bias[l].rearrange("(r p) -> r p", p=128))]
                rows_b = [(0, cf_conv_w[l].rearrange("k (r p) -> (k r) p", p=128)),
                          (62, cf_conv_b[l].rearrange("(r p) -> r p", p=128)),
                          (64, cf_ln_g[l].rearrange("(r p) -> r p", p=128)),
                          (66, cf_ln_b[l].rearrange("(r p) -> r p", p=128)),
                          (68, subln_g[l].rearrange("(r p) -> r p", p=128))]
                for dst, rows in ((VROW, rows_a), (VROWB, rows_b)):
                    for r, src in rows:
                        act.dma_start(dst[r:r + src.shape[0], :], src).then_inc(vec_in.sem, 16)
                for n, v in enumerate((hf_b1, hf_freq, hf_b2)):
                    act.dma_start(HFV[0:64, n:n + 1], v[l].rearrange("(p a) -> p a", a=1)).then_inc(vec_in.sem, 16)
                for n, v in enumerate((lam_q1, lam_k1, lam_q2, lam_k2)):
                    act.dma_start(LAMR[:, n, :], v[l].rearrange("(a n) -> a n", a=1).broadcast_to([128, 64]))\
                       .then_inc(vec_in.sem, 16)
                act.dma_start(LAMC[:, 0:2], lam_d[l]).then_inc(vec_in.sem, 16)

                def conv_store(u):
                    kind, ct, q = UNITS[u]
                    t0, tn = CHUNKS[q]
                    act.wait_ge(conv_done.sem, conv_done.at(l, u + 1))
                    if kind == "hyena":
                        for n in range(2):
                            act.dma_start(hy_d[n, ct, :, t0:t0 + tn], CACC[:, n, :tn]).then_inc(conv_stored.sem, 16)
                    else:
                        act.dma_start(cf_d[ct, :, t0:t0 + tn], CACC[:, 0, :tn]).then_inc(conv_stored.sem, 16)

                def conv_load(u, n):
                    kind, ct, q = UNITS[u]
                    t0, tn = CHUNKS[q]
                    halo = 1 if kind == "hyena" else 15
                    lo = t0 - (halo if q == 1 else 0)
                    hi = t0 + tn + (halo if q == 0 else 0)
                    at = lo - (t0 - halo)
                    done = 3 * n
                    for p in range(2):
                        act.wait_ge(z_stored[p].sem, z_stored[p].at(l, 16 * ((done + 1 - p) // 2)))
                    act.wait_ge(conv_done.sem, conv_done.at(l, u))
                    tiles = (ct, 2 + ct, 4 + ct) if kind == "hyena" else (6 + ct, 8 + ct)
                    dst = HYIN if kind == "hyena" else CFIN
                    for x, tile in enumerate(tiles):
                        act.dma_start(dst[:, x, at:at + hi - lo], z_d[tile, :, lo:hi]).then_inc(conv_in.sem, 16)

                for n in range(ZT):
                    for q, (t0, tn) in enumerate(CHUNKS):
                        u = 3 * n + q
                        if q < 2:
                            act.wait_ge(z_psum.sem, z_psum.at(l, 2 * n + q + 1))
                        else:
                            act.wait_ge(blk_used.sem, blk_used.at(l, n + 1))
                        act.wait_ge(z_stored[u % 2].sem, z_stored[u % 2].at(l, 16 * (u // 2)))
                        S.activation(ZST[:, u % 2, :tn], PS[:, 3 * (n % 2) + q, :tn], ACT.Copy).then_inc(z_evac.sem, 1)
                        act.wait_ge(z_evac.sem, z_evac.at(l, u + 1))
                        act.dma_start(z_d[n, :, t0:t0 + tn], ZST[:, u % 2, :tn]).then_inc(z_stored[u % 2].sem, 16)
                    if n in UNIT_AT:
                        u = UNIT_AT.index(n)
                        if u:
                            conv_store(u - 1)
                        conv_load(u, n)
                        if UNITS[u][0] == "conformer":
                            t0, tn = CHUNKS[UNITS[u][2]]
                            act.wait_ge(conv_in.sem, conv_in.at(l, 6 * 48 + (u - 5) * 32))
                            act.wait_ge(pads_ready.sem, pads_ready.at(l, u - 5))
                            S.activation(CFIN[:, 1, :tn + 30], CFIN[:, 1, :tn + 30], ACT.Sigmoid)\
                             .then_inc(glu_done.sem, 1)
                conv_store(11)

                act.wait_ge(blk_used.sem, blk_used.at(l, B_FWD))
                act.wait_ge(conv_stored.sem, conv_stored.at(l, 288))
                for dst, src in ((HW1[0:33, 0], hf_w1[l]), (HW1[0:33, 1], hf_w1[l]), (HW2[0:64, 0], hf_w2[l]),
                                 (HW2[0:64, 1], hf_w2[l]), (HW3[0:64, :], hf_w3[l]),
                                 (FEAT[0:33, :], feats_d)):
                    act.dma_start(dst, src).then_inc(hf_in.sem, 16)
                for ct in range(2):
                    act.dma_start(UIN[:, ct, :], hy_d[0, ct]).then_inc(u_in.sem, 16)
                for n, (src, dst) in enumerate(((ARG, HID1), (ARG, HID2))):
                    act.wait_ge(hf_arg.sem, hf_arg.at(l, n + 1))
                    S.activation(dst[0:64, :], src[0:64, :], ACT.Sin).then_inc(hf_sin.sem, 1)
                for t in range(TT):
                    if t == 0:
                        for t2 in range(2):
                            act.dma_start(DEC[:, t2, :], decay_d[t2 * 128:(t2 + 1) * 128]).then_inc(dec_in[t2].sem, 16)
                    act.wait_ge(m_sum.sem, m_sum.at(l, t + 1))
                    if t + 2 < TT:
                        act.dma_start(DEC[:, t % 2, :], decay_d[(t + 2) * 128:(t + 3) * 128])\
                           .then_inc(dec_in[t % 2].sem, 16)
                    S.activation(MH[:, t, 0:768].rearrange("p (a n) -> p a n", a=3)[:, 0:3:2, :], FPM[:], ACT.Copy)\
                     .then_inc(m_hi.sem, 1)
                    act.wait_ge(u_psum.sem, u_psum.at(l, t + 1))
                    S.activation(MH[:, t, 256:512], PS[:, 2 + t % 2, 0:256], ACT.Copy).then_inc(u_hi.sem, 1)
                for j in range(TT):
                    b0 = 2 * (j % 2)
                    if j < ST:
                        act.wait_ge(blk_used.sem, blk_used.at(l, B_FWD + 2 * j + 2))
                    elif j == ST:
                        act.wait_ge(dft_psum.sem, dft_psum.at(l, 1))
                    else:
                        act.wait_ge(blk_used.sem, blk_used.at(l, B_INV))
                    if j:
                        act.wait_ge(f_sum.sem, f_sum.at(l, j))
                    S.activation(GS[:, 0, :], PS[:, b0, 0:256], ACT.Copy, scale=WF[:, j:j + 1])
                    S.activation(GS[:, 1, :], PS[:, b0 + 1, 256:512], ACT.Copy, scale=WF[:, j:j + 1])\
                     .then_inc(g_scaled.sem, 1)
                    act.wait_ge(f_sum.sem, f_sum.at(l, j + 1))
                    S.activation(FH[:, j] if j < ST else FPH[:, j - ST], YF[:], ACT.Copy).then_inc(f_hi.sem, 1)
                n = 0
                for ct in range(2):
                    for q, (t0, tn) in enumerate(CHUNKS):
                        act.wait_ge(blk_used.sem, blk_used.at(l, B_OUT))
                        act.wait_ge(old_read.sem, old_read.at(l, n))
                        for x in range(2):
                            act.dma_start(OLD[:, x, :tn], hy_d[x, ct, :, t0:t0 + tn]).then_inc(old_in.sem, 16)
                        act.wait_ge(hy_done.sem, hy_done.at(l, n + 1))
                        act.dma_start(y_d[ct, :, t0:t0 + tn], OY[:, :tn]).then_inc(hy_stored.sem, 16)
                        n += 1

                act.wait_ge(lam_ready.sem, lam_ready.at(l, 1))
                S.activation(LAMS[:, 2:4], LAMS[:, 0:2], ACT.Exp).then_inc(lam_exp.sem, 1)
                with act.Fori(0, HEADS) as h:
                    act.wait_ge(prep_turned.sem, prep_turned.at(l, 1) + h)
                    act.wait_ge(kv_stored.sem, kv_stored.at(l, 0) + h * 32)
                    S.activation(KO[:].rearrange("p t n -> p (t n)"), PS[:, 0, 256:512], ACT.Copy)
                    S.activation(VO[:].rearrange("p t n -> p (t n)"), PSF[:, 512 + 1024:512 + 1280], ACT.Copy)\
                     .then_inc(kv_copied.sem, 1)
                    S.activation(KR[:, 0:PAST], PS[:, 0, 0:PAST], ACT.Copy).then_inc(kc_placed.sem, 1)
                    act.wait_ge(kv_copied.sem, kv_copied.at(l, 1) + h)
                    for dst, src in ((new_k, KO), (new_v, VO)):
                        act.dma_start(dst[0, l].rearrange("(t p) m d -> p t (m d)", p=128)[:, :, bass.ts(h, 128)],
                                      src[:]).then_inc(kv_stored.sem, 16)
                    S.activation(V2[:, 0:2, 0:128], CKV[:, 1], ACT.Copy)
                    S.activation(V2[:, 2:TT + 2, 0:128], PSF[:, 512:512 + T].rearrange("p (t n) -> p t n", t=TT),
                                 ACT.Copy).then_inc(v_hi.sem, 1)
                    act.wait_ge(head_in.sem, head_in.at(l, 80) + h * 80)
                    for n in range(4):
                        src = (QR, KR)[n // 2]
                        t0 = 512 * (n % 2) + (0, PAST)[n // 2]
                        if n:
                            act.wait_ge(rope_swapped.sem, rope_swapped.at(l, n) + h * 4)
                        S.activation(ZHL[:, 0, :], src[:, t0:t0 + 512], ACT.Copy).then_inc(rope_hi.sem, 1)
                    act.wait_ge(rope_done.sem, rope_done.at(l, 4) + h * 4)
                    act.wait_ge(kc_placed.sem, kc_placed.at(l, 1) + h)
                    for m in range(2):
                        own, other = slice(64 * m, 64 * m + 64), slice(64 - 64 * m, 128 - 64 * m)
                        S.activation(QQ[own, m, :], QR[own, :], ACT.Copy).then_inc(qk_hi.sem, 1)
                        S.activation(KH[own, m, :], KR[own, :], ACT.Copy).then_inc(qk_hi.sem, 1)
                        S.activation(KH[other, m, :], KR[own, :], ACT.Copy).then_inc(qk_hi.sem, 1)

                    n_at = 0

                    def exps(t):
                        k0, kn = ITEMS[t]
                        for m in range(2):
                            act.wait_ge(smax.sem, smax.at(l, 2 * t + m + 1) + h * 2 * TT)
                            if t:
                                act.wait_ge(mixed.sem, mixed.at(l, t) + h * TT)
                            S.activation(PB[:, m, :kn], PSF[:, 1536 * m:1536 * m + kn], ACT.Exp,
                                         bias=STAT[:, t % 2, m:m + 1], scale=SCALE,
                                         accum_out=STAT[:, t % 2, 2 + m:3 + m]).then_inc(probs.sem, 1)

                    exps(0)
                    for t in range(TT):
                        k0, kn = ITEMS[t]
                        for r, g0 in enumerate(range(0, kn // 128, 4)):
                            gn = min(4, kn // 128 - g0)
                            act.wait_ge(at_psum.sem, at_psum.at(l, n_at + 1) + h * (ST * 3 + PT))
                            if t and r == 0:
                                act.wait_ge(pv_psum.sem, pv_psum.at(l, t) + h * TT)
                            S.activation(ATH[:, g0 * 128:(g0 + gn) * 128], PS[:, 6 + r % 2, 0:gn * 128], ACT.Copy)\
                             .then_inc(at_hi.sem, 1)
                            n_at += 1
                        if t + 1 < TT:
                            exps(t + 1)
                        act.wait_ge(pv_psum.sem, pv_psum.at(l, t + 1) + h * TT)
                        if t:
                            act.wait_ge(o_ready.sem, o_ready.at(l, t) + h * TT)
                        S.activation(O2[:], PS[:, 7, 128:256], ACT.Copy, scale=STAT[:, t % 2, 4:5])\
                         .then_inc(o_part.sem, 1)
                    act.wait_ge(o_ready.sem, o_ready.at(l, TT) + h * TT)
                    A.loop(h, TT - 1, HEADS)
                    for t in range(TT):
                        ins = S.activation(O2[:], OB[:, t, :], ACT.Square, accum_out=SSQ[:, t:t + 1])
                        if t < TT - 1:
                            A.link(ins)
                    ins.then_inc(ssq_done.sem, 1)
                    act.wait_ge(ssq_done.sem, ssq_done.at(l, 1) + h)
                    S.activation(RRS[:], SSQ[:], ACT.Sqrt, scale=1 / 128, bias=EPSC[:, 0:1]).then_inc(sd_head.sem, 1)
                    act.wait_ge(o_turned.sem, o_turned.at(l, 1) + h)
                    S.activation(AB[:], PSF[:, 0:T], ACT.Copy, scale=VEC[:, V_SUB:V_SUB + 1]).then_inc(o_placed.sem, 1)
                    act.wait_ge(o_placed.sem, o_placed.at(l, 1) + h)
                    act.dma_start(y_d[h + 4], AB[:]).then_inc(yat_stored.sem, 16)
                A.end_loop()

                n = 0
                for q, (t0, tn) in enumerate(CHUNKS):
                    act.wait_ge(cf_in.sem, cf_in.at(l, 32 * (q + 1)))
                    if q:
                        act.wait_ge(cf_norm.sem, cf_norm.at(l, q))
                    S.activation(CFS[:, :, :tn], CFU[:, :, :tn], ACT.Square).then_inc(cf_sq.sem, 1)
                    for j in (0, 1, 4, 5, 6, 7):
                        act.wait_ge(y_in[n % 2].sem, y_in[n % 2].at(l, 16 * (n // 2 + 1)))
                        S.activation(HH[:, j, t0:t0 + tn], YIN[:, n % 2, :tn], ACT.Copy).then_inc(y_hi.sem, 1)
                        n += 1
                    act.wait_ge(cf_var.sem, cf_var.at(l, q + 1))
                    S.activation(RS[:, :tn], RS[:, :tn], ACT.Sqrt, bias=EPSC[:, 0:1]).then_inc(cf_sd.sem, 1)
                    act.wait_ge(cf_norm.sem, cf_norm.at(l, q + 1))
                    for ct in range(2):
                        ins = S.activation(CFY[:, ct, :tn], CFY[:, ct, :tn], ACT.Silu,
                                           scale=VEC[:, V_CFG + ct:V_CFG + ct + 1],
                                           bias=VEC[:, V_CFBB + ct:V_CFBB + ct + 1])
                    ins.then_inc(cf_silu.sem, 1)
                    act.wait_ge(cf_silu.sem, cf_silu.at(l, q + 1))
                    for ct in range(2):
                        S.activation(HH[:, 2 + ct, t0:t0 + tn], CFY[:, ct, :tn], ACT.Copy).then_inc(y_hi.sem, 1)

                def squares(which, buf):
                    for n in range(24):
                        q, j = (n % 3, n // 3) if which == 0 else (n // 8, n % 8)
                        t0, tn = CHUNKS[q]
                        if which == 0:
                            act.wait_ge(o_evac.sem, o_evac.at(l, n + 1))
                        else:
                            act.wait_ge(m2_evac.sem, m2_evac.at(l, 24 * (GROUPS - 1) + n + 1))
                        act.wait_ge(sq_added.sem, sq_added.at(l, 24 * which + n - 1))
                        S.activation(buf[:, n % 2, :tn], XT[:, j, t0:t0 + tn], ACT.Square).then_inc(sq_ready.sem, 1)

                squares(0, SQO)
                norm(l, 0)

                def hidden(g0, q, i):
                    t0, tn = CHUNKS[q]
                    for e in range(2):
                        u = 2 * (3 * g0 + q) + e
                        if q < 2:
                            act.wait_ge(m1_psum.sem, m1_psum.at(l, 4 * g0 + 2 * q + e + 1) + i * 4)
                        else:
                            act.wait_ge(blk_used.sem, blk_used.at(l, B_MLP + 4 * g0 + e + 1) + i * 4)
                        act.wait_ge(hid_ready.sem, hid_ready.at(l, u - 1) + i * 6)
                        S.activation(RB[:, e, :tn], PS[:, e, :tn], ACT.Relu).then_inc(relu_done.sem, 1)
                        act.wait_ge(relu_done.sem, relu_done.at(l, u + 1) + i * 6)
                        if q == 0:
                            act.wait_ge(m2_psum.sem, m2_psum.at(l, 23 * g0 - 15) + i * 23)
                        elif q == 1:
                            act.wait_ge(m2_psum.sem, m2_psum.at(l, 23 * g0 - 7) + i * 23)
                        else:
                            act.wait_ge(blk_used.sem, blk_used.at(l, B_MLP + 4 * g0) + i * 4)
                        S.activation(hidden_hi(q)[:, e, :tn], RB[:, e, :tn], ACT.Square).then_inc(hid_hi.sem, 1)

                act.wait_ge(kv_stored.sem, kv_stored.at(l, HEADS * 32))
                with act.Fori(0, GROUPS) as g:
                    for q in range(3):
                        hidden(0, q, g)
                squares(1, SQM)
                norm(l, 1)
                A.end_layer()

            for t in range(TT):
                act.wait_ge(y_turned.sem, t + 1)
                if t >= 2:
                    act.wait_ge(y_stored[t % 2].sem, 16 * (t // 2))
                for half in range(2):
                    ins = S.activation(XIN[:, t % 2, 512 * half:512 * half + 512], PS[:, 2 * (t % 2) + half, :],
                                       ACT.Copy, scale=1 / ALPHA)
                ins.then_inc(y_placed.sem, 1)
                act.wait_ge(y_placed.sem, t + 1)
                dst = y_sample[0, t * 128:(t + 1) * 128, :] if t < ST else \
                    y_prompt[0, (t - ST) * 128:(t - ST + 1) * 128, :]
                act.dma_start(dst, XIN[:, t % 2]).then_inc(y_stored[t % 2].sem, 16)
            for p in range(2):
                act.wait_ge(y_stored[p].sem, 16 * TT // 2)
            act.wait_ge(kv_stored.sem, kv_stored.at(DEPTH - 1, HEADS * 32))

        @block.vector
        def _(dve):
            V = nc.vector
            C = Chain(dve, v_chain, V_STEPS, V_BEFORE)

            V.memset(ONES[:], 1 / 1024)
            V.memset(EPSC[:], EPS)
            C.link(V.memset(AD0[:], 0.0))
            dve.wait_ge(row_turned.sem, 1)
            V.tensor_copy(CRAW[:], PS[:, 6, 0:16])
            V.tensor_copy(SWAP[:], SWAPF[:])
            V.tensor_copy(B0[:], PS[:, 6, 16:48]).then_inc(row_placed.sem, 1)
            dve.wait_ge(row_placed.sem, 1)
            dve.wait_ge(ada_used.sem, 34)
            for v in range(2):
                C.link(V.tensor_tensor(AD0[:, 0:DEPTH, :, v], PS[:, 7, 0:64].rearrange("p (l t v) -> p l t v", l=2, v=2)
                                       [:, :, :, v], B0[:].rearrange("p (l t) -> p l t", l=2), ALU.add))
            C.link(V.tensor_scalar(AD0[:, 0:DEPTH, 8:16, :], AD0[:, 0:DEPTH, 8:16, :], 1.0, 1 / ALPHA,
                                   ALU.add, ALU.mult))
            V.memset(MODT[:, 0, 0:2], 0.0).then_inc(const_done.sem, 1)
            dve.wait_ge(const_done.sem, 1)
            dve.wait_ge(x_placed.sem, TT)

            def lo_of_h(l, j, q, n, scale, bias, tmp):
                t0, tn = CHUNKS[q]
                C.link(V.tensor_scalar(tmp[:, :tn], XT[:, j, t0:t0 + tn], scale, bias, ALU.mult, ALU.add))
                dve.wait_ge(hh_ready.sem, n + 1 if l is None else hh_ready.at(l, n + 1))
                ins = V.tensor_tensor(HL[:, j, t0:t0 + tn], tmp[:, :tn], HH[:, j, t0:t0 + tn].bitcast(F32), ALU.subtract)
                if j == KT - 1:
                    ins.then_inc(h_ready.sem, 1)
                    dve.wait_ge(h_ready.sem, q + 1 if l is None else h_ready.at(l, n // 8 + 1))
                else:
                    C.link(ins)

            for q in range(3):
                v = COND[q]
                for j in range(KT):
                    lo_of_h(None, j, q, 8 * q + j, AD0[:, 0, 8 + j, v:v + 1], AD0[:, 0, j, v:v + 1], MODT[:, 0, :])

            def norm(l, which):
                acc = (ACC1, ACC2)[which]
                for q, (t0, tn) in enumerate(CHUNKS):
                    v, bank = COND[q], (6, 0, 2)[q]
                    k = 3 * which + q
                    dve.wait_ge(stats.sem, stats.at(l, k + 1))
                    C.link(V.tensor_copy(MU[:, :tn], PS[:, bank, :tn]))
                    C.link(V.tensor_tensor(LT[:, :tn], MU[:, :tn], MU[:, :tn], ALU.mult))
                    V.tensor_tensor(RS[:, :tn], PS[:, bank + 1, :tn], LT[:, :tn], ALU.subtract).then_inc(var_ready.sem, 1)
                    dve.wait_ge(sd_ready.sem, sd_ready.at(l, k + 1))
                    C.link(V.reciprocal(RS[:, :tn], RS[:, :tn]))
                    for j in range(KT):
                        n = 8 * k + j
                        x = XT[:, j, t0:t0 + tn]
                        if j:
                            dve.wait_ge(xn_ready.sem, xn_ready.at(l, n))
                        C.link(V.tensor_tensor(LT[:, :tn], x, MU[:, :tn], ALU.subtract))
                        V.tensor_tensor(x, LT[:, :tn], RS[:, :tn], ALU.mult).then_inc(xn_ready.sem, 1)
                        if j:
                            finish(l, which, q, j - 1, v)
                    finish(l, which, q, KT - 1, v)

            def finish(l, which, q, j, v):
                n = 8 * (3 * which + q) + j
                dve.wait_ge(xs_ready.sem, xs_ready.at(l, n + 1))
                if which:
                    scale = AD0[:, bass.ds(l + 1, 1), 8 + j, v:v + 1].rearrange("p a b -> p (a b)")
                    bias = AD0[:, bass.ds(l + 1, 1), j, v:v + 1].rearrange("p a b -> p (a b)")
                else:
                    scale, bias = ADA[:, A_SC2 + j, v:v + 1], ADA[:, A_SH2 + j, v:v + 1]
                lo_of_h(l, j, q, n, scale, bias, LT2)

            with dve.Fori(0, DEPTH) as l:
                C.layer(l)
                dve.wait_ge(vec_turned.sem, vec_turned.at(l, 1))
                C.link(V.tensor_copy(VEC[:], PS[:, 6, 0:ROWS_A + ROWS_B]))
                C.link(V.tensor_scalar(LNV[:], VEC[:, V_LN:V_LN + 32], ALPHA, None, ALU.mult))
                C.link(V.tensor_tensor(LAMR[:, 0:4:2, :], LAMR[:, 0:4:2, :], LAMR[:, 1:4:2, :], ALU.mult))
                V.tensor_reduce(LAMS[:, 0:2], LAMR[:, 0:4:2, :], AX_X, ALU.add).then_inc(lam_ready.sem, 1)

                for u, (kind, ct, q) in enumerate(UNITS):
                    t0, tn = CHUNKS[q]
                    if kind == "hyena":
                        buf, halo, width, parts = HYIN, 1, tn + 2, 3
                    else:
                        buf, halo, width, parts = CFIN, 15, tn + 30, 2
                    pads = []
                    if q != 1:
                        pads.append(buf[:, 0:parts, 0:halo])
                    if q != 0:
                        pads.append(buf[:, 0:parts, halo + tn:width])
                    for n, pad in enumerate(pads):
                        ins = V.memset(pad, 0.0)
                        if n < len(pads) - 1 or kind == "hyena":
                            C.link(ins)
                    if kind == "conformer":
                        ins.then_inc(pads_ready.sem, 1)
                        dve.wait_ge(glu_done.sem, glu_done.at(l, u - 5))
                    else:
                        dve.wait_ge(conv_in.sem, conv_in.at(l, 48 * (u + 1)))
                    stored = 32 * u if u <= 6 else 192 + 16 * (u - 6)
                    dve.wait_ge(conv_stored.sem, conv_stored.at(l, stored))
                    if kind == "hyena":
                        def conv(x, dst):
                            col = 2 * x + ct
                            C.link(V.tensor_scalar(dst, HYIN[:, x, 0:tn], VEC[:, V_HYW + col:V_HYW + col + 1],
                                                   VEC[:, V_HYB + col:V_HYB + col + 1], ALU.mult, ALU.add))
                            for k in (1, 2):
                                w = V_HYW + 6 * k + col
                                C.link(V.scalar_tensor_tensor(dst, HYIN[:, x, k:k + tn], VEC[:, w:w + 1], dst,
                                                              ALU.mult, ALU.add))
                        conv(1, CACC[:, 0, :tn])
                        conv(2, CACC[:, 1, :tn])
                        C.link(V.tensor_tensor(CACC[:, 0, :tn], CACC[:, 0, :tn], CACC[:, 1, :tn], ALU.mult))
                        conv(0, CACC[:, 1, :tn])
                    else:
                        C.link(V.tensor_tensor(CFIN[:, 0, :width], CFIN[:, 0, :width], CFIN[:, 1, :width], ALU.mult))
                        dst = CACC[:, 0, :tn]
                        C.link(V.tensor_scalar(dst, CFIN[:, 0, 0:tn], VEC[:, V_CFW + ct:V_CFW + ct + 1],
                                               VEC[:, V_CFB + ct:V_CFB + ct + 1], ALU.mult, ALU.add))
                        for k in range(1, 31):
                            w = V_CFW + 2 * k + ct
                            C.link(V.scalar_tensor_tensor(dst, CFIN[:, 0, k:k + tn], VEC[:, w:w + 1], dst,
                                                          ALU.mult, ALU.add))
                    V.memset(STAT[:, 0, 7:8], 0.0).then_inc(conv_done.sem, 1)
                    dve.wait_ge(conv_done.sem, conv_done.at(l, u + 1))

                dve.wait_ge(ada_used.sem, ada_used.at(l, 32))
                for v in range(2):
                    C.link(V.tensor_tensor(ADA[:, :, v], PS[:, 7, 0:64].rearrange("p (t v) -> p t v", v=2)[:, :, v],
                                           VEC[:, V_BADA:V_BADA + 32], ALU.add))
                C.link(V.tensor_scalar(ADA[:, A_SC2:A_SC2 + 8, :], ADA[:, A_SC2:A_SC2 + 8, :], 1.0, 1 / ALPHA,
                                       ALU.add, ALU.mult))

                for n in range(2):
                    for q, (t0, tn) in enumerate(CHUNKS):
                        dve.wait_ge(hf_psum.sem, hf_psum.at(l, 3 * n + q + 1))
                        if n:
                            dve.wait_ge(hf_sin.sem, hf_sin.at(l, 1))
                        b = (0, 2)[n]
                        C.link(V.tensor_scalar(ARG[0:64, t0:t0 + tn], PS[0:64, 3 * n + q, :tn], HFV[0:64, b:b + 1],
                                               HFV[0:64, 1:2], ALU.add, ALU.mult))
                    C.link(V.tensor_scalar(RND[0:64, :], ARG[0:64, :], 1 / TWO_PI, ROUND, ALU.mult, ALU.add))
                    C.link(V.tensor_scalar(RND[0:64, :], RND[0:64, :], ROUND, -TWO_PI, ALU.subtract, ALU.mult))
                    C.link(V.tensor_tensor(ARG[0:64, :], ARG[0:64, :], RND[0:64, :], ALU.add))
                    V.tensor_scalar(ARG[0:64, :], ARG[0:64, :], PI_BELOW, -PI_BELOW, ALU.min, ALU.max)\
                     .then_inc(hf_arg.sem, 1)
                for t in range(TT):
                    dve.wait_ge(hft_psum.sem, hft_psum.at(l, t + 1))
                    dve.wait_ge(dec_in[t % 2].sem, dec_in[t % 2].at(l, 16 * (t // 2 + 1)))
                    V.tensor_tensor(FB[:], PS[:, t % 2, :], DEC[:, t % 2, :], ALU.mult).then_inc(hft_read.sem, 1)
                    dve.wait_ge(hft_read.sem, hft_read.at(l, t + 1))
                    if t:
                        dve.wait_ge(m_hi.sem, m_hi.at(l, t))
                    C.link(V.tensor_tensor(FPM[:, 0, :], FB[:, 0:256], FB[:, 256:512], ALU.add))
                    V.tensor_tensor(FPM[:, 1, :], FB[:, 0:256], FB[:, 256:512], ALU.subtract).then_inc(m_sum.sem, 1)
                    dve.wait_ge(m_hi.sem, m_hi.at(l, t + 1))
                    V.tensor_tensor(ML[:, t, :].rearrange("p (a n) -> p a n", a=3)[:, 0:3:2, :], FPM[:],
                                    MH[:, t, :].rearrange("p (a n) -> p a n", a=3)[:, 0:3:2, :].bitcast(F32),
                                    ALU.subtract).then_inc(filt_ready.sem, 1)
                    dve.wait_ge(filt_ready.sem, filt_ready.at(l, t + 1))
                    dve.wait_ge(u_hi.sem, u_hi.at(l, t + 1))
                    V.tensor_tensor(ML[:, t, 256:512], PS[:, 2 + t % 2, 0:256], MH[:, t, 256:512].bitcast(F32),
                                    ALU.subtract).then_inc(u_ready.sem, 1)
                for j in range(TT):
                    b0 = 2 * (j % 2)
                    dve.wait_ge(g_scaled.sem, g_scaled.at(l, j + 1))
                    if j:
                        dve.wait_ge(f_hi.sem, f_hi.at(l, j))
                    uc, us = PS[:, b0, 256:512], PS[:, b0 + 1, 0:256]
                    V.tensor_tensor(PR[:, 0, :], uc, GS[:, 0, :], ALU.mult)
                    V.tensor_tensor(PR[:, 1, :], us, GS[:, 0, :], ALU.mult)
                    V.tensor_tensor(PR2[:, 0, :], us, GS[:, 1, :], ALU.mult)
                    C.link(V.tensor_tensor(PR2[:, 1, :], uc, GS[:, 1, :], ALU.mult))
                    C.link(V.tensor_tensor(YF[:, 0, :], PR[:, 0, :], PR2[:, 0, :], ALU.subtract))
                    V.tensor_tensor(YF[:, 1, :], PR[:, 1, :], PR2[:, 1, :], ALU.add).then_inc(f_sum.sem, 1)
                    dve.wait_ge(f_hi.sem, f_hi.at(l, j + 1))
                    fh = FH[:, j] if j < ST else FPH[:, j - ST]
                    fl = FL[:, j] if j < ST else FPL[:, j - ST]
                    V.tensor_tensor(fl, YF[:], fh.bitcast(F32), ALU.subtract).then_inc(f_ready.sem, 1)
                    dve.wait_ge(f_ready.sem, f_ready.at(l, j + 1))
                n = 0
                for ct in range(2):
                    for q, (t0, tn) in enumerate(CHUNKS):
                        dve.wait_ge(old_in.sem, old_in.at(l, 32 * (n + 1)))
                        y = PS[:, 4 + 2 * ct + q, :tn] if q < 2 else PS[:, ct, :tn]
                        dve.wait_ge(hy_stored.sem, hy_stored.at(l, 16 * n))
                        C.link(V.scalar_tensor_tensor(OLD[:, 0, :tn], OLD[:, 0, :tn], VEC[:, V_BIAS + ct:V_BIAS + ct + 1],
                                                      y, ALU.mult, ALU.add))
                        V.tensor_tensor(OY[:, :tn], OLD[:, 0, :tn], OLD[:, 1, :tn], ALU.mult).then_inc(hy_done.sem, 1)
                        dve.wait_ge(hy_done.sem, hy_done.at(l, n + 1))
                        V.memset(STAT[:, 0, 7:8], 0.0).then_inc(old_read.sem, 1)
                        dve.wait_ge(old_read.sem, old_read.at(l, n + 1))
                        n += 1

                dve.wait_ge(at_tab.sem, at_tab.at(l, 16))
                dve.wait_ge(lam_exp.sem, lam_exp.at(l, 1))
                C.link(V.tensor_tensor(LAMS[:, 0:1], LAMS[:, 3:4], LAMS[:, 2:3], ALU.subtract))
                V.tensor_tensor(LAMC[:, 2:3], LAMS[:, 0:1], LAMC[:, 0:1], ALU.subtract).then_inc(lam_known.sem, 1)
                with dve.Fori(0, HEADS) as h:
                    C.loop(h, V_HEAD, HEADS)
                    dve.wait_ge(lam_known.sem, lam_known.at(l, 1))
                    dve.wait_ge(v_hi.sem, v_hi.at(l, 1) + h)
                    V.tensor_tensor(V2[:, 0:2, 128:256], CKV[:, 1], V2[:, 0:2, 0:128].bitcast(F32), ALU.subtract)
                    V.tensor_tensor(V2[:, 2:TT + 2, 128:256], PSF[:, 512:512 + T].rearrange("p (t n) -> p t n", t=TT),
                                    V2[:, 2:TT + 2, 0:128].bitcast(F32), ALU.subtract).then_inc(v_split.sem, 1)
                    dve.wait_ge(v_split.sem, v_split.at(l, 1) + h)
                    for n in range(4):
                        src = (QR, KR)[n // 2]
                        t0 = 512 * (n % 2) + (0, PAST)[n // 2]
                        tab = slice(512 * (n % 2), 512 * (n % 2) + 512)
                        dve.wait_ge(rope_hi.sem, rope_hi.at(l, n + 1) + h * 4)
                        V.tensor_tensor(ZHL[:, 1, :], src[:, t0:t0 + 512], ZHL[:, 0, :].bitcast(F32), ALU.subtract)\
                         .then_inc(rope_lo.sem, 1)
                        dve.wait_ge(rope_lo.sem, rope_lo.at(l, n + 1) + h * 4)
                        C.link(V.tensor_tensor(src[:, t0:t0 + 512], src[:, t0:t0 + 512], ROPE[:, 0, tab], ALU.mult))
                        dve.wait_ge(rope_swapped.sem, rope_swapped.at(l, n + 1) + h * 4)
                        C.link(V.tensor_tensor(RT[:], PS[:, 4 + n % 2, :], ROPE[:, 1, tab], ALU.mult))
                        V.tensor_tensor(src[:, t0:t0 + 512], src[:, t0:t0 + 512], RT[:], ALU.add).then_inc(rope_done.sem, 1)
                        dve.wait_ge(rope_done.sem, rope_done.at(l, n + 1) + h * 4)
                    dve.wait_ge(kc_placed.sem, kc_placed.at(l, 1) + h)
                    for m in range(2):
                        own, other = slice(64 * m, 64 * m + 64), slice(64 - 64 * m, 128 - 64 * m)
                        dve.wait_ge(qk_hi.sem, qk_hi.at(l, 3 * m + 2) + h * 6)
                        V.tensor_tensor(QQ[other, m, :], QR[own, :], QQ[own, m, :].bitcast(F32), ALU.subtract)
                        V.tensor_tensor(KL[own, m, :], KR[own, :], KH[own, m, :].bitcast(F32), ALU.subtract)
                        C.link(V.tensor_tensor(KL[other, m, :], KR[own, :], KH[own, m, :].bitcast(F32), ALU.subtract))
                    dve.wait_ge(qk_hi.sem, qk_hi.at(l, 6) + h * 6)
                    V.memset(STAT[:, 0, 7:8], 0.0).then_inc(prep_done.sem, 1)
                    dve.wait_ge(prep_done.sem, prep_done.at(l, 1) + h)
                    V.memset(STAT[:, 0, 7:8], 0.0).then_inc(head_raw_free.sem, 1)
                    dve.wait_ge(head_raw_free.sem, head_raw_free.at(l, 1) + h)

                    n_at = 0

                    def maxima(t):
                        k0, kn = ITEMS[t]
                        for m in range(2):
                            dve.wait_ge(s_psum.sem, s_psum.at(l, 2 * t + m + 1) + h * 2 * TT)
                            C.link(V.tensor_reduce(STAT[:, t % 2, 6 + m:7 + m], PSF[:, 1536 * m:1536 * m + kn],
                                                   AX_X, ALU.max))
                            V.tensor_scalar(STAT[:, t % 2, m:m + 1], STAT[:, t % 2, 6 + m:7 + m], -SCALE, None,
                                            ALU.mult).then_inc(smax.sem, 1)

                    maxima(0)
                    for t in range(TT):
                        k0, kn = ITEMS[t]
                        st_ = STAT[:, t % 2, :]
                        dve.wait_ge(probs.sem, probs.at(l, 2 * t + 2) + h * 2 * TT)
                        C.link(V.reciprocal(st_[:, 4:6], st_[:, 2:4]))
                        C.link(V.scalar_tensor_tensor(st_[:, 6:7], st_[:, 2:3], LAMC[:, 2:3], st_[:, 5:6],
                                                      ALU.mult, ALU.mult))
                        if t:
                            dve.wait_ge(at_psum.sem, at_psum.at(l, n_at) + h * (ST * 3 + PT))
                        else:
                            dve.wait_ge(yat_stored.sem, yat_stored.at(l, 0) + h * 16)
                        V.scalar_tensor_tensor(AB[:, :kn], PB[:, 1, :kn], st_[:, 6:7], PB[:, 0, :kn],
                                               ALU.mult, ALU.add).then_inc(mixed.sem, 1)
                        if t + 1 < TT:
                            maxima(t + 1)
                        for r, g0 in enumerate(range(0, kn // 128, 4)):
                            gn = min(4, kn // 128 - g0)
                            cols = slice(g0 * 128, (g0 + gn) * 128)
                            dve.wait_ge(at_hi.sem, at_hi.at(l, n_at + 1) + h * (ST * 3 + PT))
                            V.tensor_tensor(ATL[:, cols], PS[:, 6 + r % 2, 0:gn * 128], ATH[:, cols].bitcast(F32),
                                            ALU.subtract).then_inc(at_lo.sem, 1)
                            n_at += 1
                        dve.wait_ge(o_part.sem, o_part.at(l, t + 1) + h * TT)
                        V.scalar_tensor_tensor(OB[:, t, :], PS[:, 7, 0:128], st_[:, 4:5], O2[:], ALU.mult, ALU.add)\
                         .then_inc(o_ready.sem, 1)
                    dve.wait_ge(sd_head.sem, sd_head.at(l, 1) + h)
                    C.link(V.reciprocal(RRS[:], RRS[:]))
                    C.link(V.tensor_scalar(RRS[:], RRS[:], LAMC[:, 1:2], None, ALU.mult))
                    V.tensor_tensor(OB[:], OB[:], RRS[:].rearrange("p (t a) -> p t a", a=1).broadcast_to([128, TT, 128]),
                                    ALU.mult).then_inc(o_normed.sem, 1)
                C.end_loop()

                n = 0
                for q, (t0, tn) in enumerate(CHUNKS):
                    for j in (0, 1, 4, 5, 6, 7):
                        dve.wait_ge(y_hi.sem, y_hi.at(l, 8 * q + n % 6 + 1))
                        V.tensor_tensor(HL[:, j, t0:t0 + tn], YIN[:, n % 2, :tn], HH[:, j, t0:t0 + tn].bitcast(F32),
                                        ALU.subtract).then_inc(y_lo.sem, 1)
                        n += 1
                    dve.wait_ge(cf_stats.sem, cf_stats.at(l, q + 1))
                    C.link(V.tensor_scalar(MU[:, :tn], PS[:, 6, :tn], 4.0, None, ALU.mult))
                    C.link(V.tensor_tensor(LT[:, :tn], MU[:, :tn], MU[:, :tn], ALU.mult))
                    V.scalar_tensor_tensor(RS[:, :tn], PS[:, 7, :tn], 4.0, LT[:, :tn], ALU.mult, ALU.subtract)\
                     .then_inc(cf_var.sem, 1)
                    dve.wait_ge(cf_sd.sem, cf_sd.at(l, q + 1))
                    C.link(V.reciprocal(RS[:, :tn], RS[:, :tn]))
                    for ct in range(2):
                        C.link(V.tensor_tensor(LT[:, :tn], CFU[:, ct, :tn], MU[:, :tn], ALU.subtract))
                        ins = V.tensor_tensor(CFY[:, ct, :tn], LT[:, :tn], RS[:, :tn], ALU.mult)
                        if ct == 0:
                            C.link(ins)
                    ins.then_inc(cf_norm.sem, 1)
                    for ct in range(2):
                        dve.wait_ge(y_hi.sem, y_hi.at(l, 8 * q + 7 + ct))
                        V.tensor_tensor(HL[:, 2 + ct, t0:t0 + tn], CFY[:, ct, :tn],
                                        HH[:, 2 + ct, t0:t0 + tn].bitcast(F32), ALU.subtract).then_inc(y_lo.sem, 1)

                def add_sums(which, n, j, q, buf):
                    t0, tn = CHUNKS[q]
                    acc = (ACC1, ACC2)[which]
                    for x in range(2):
                        if x:
                            dve.wait_ge(sq_ready.sem, sq_ready.at(l, 24 * which + n + 1))
                        src = buf[:, n % 2, :tn] if x else XT[:, j, t0:t0 + tn]
                        dst = acc[:, x, t0:t0 + tn]
                        ins = V.tensor_copy(dst, src) if j == 0 else V.tensor_tensor(dst, dst, src, ALU.add)
                        if x:
                            ins.then_inc(sq_added.sem, 1)
                            dve.wait_ge(sq_added.sem, sq_added.at(l, 24 * which + n + 1))
                        else:
                            C.link(ins)
                    if j == KT - 1:
                        V.memset(STAT[:, 0, 7:8], 0.0).then_inc(acc_ready.sem, 1)
                        dve.wait_ge(acc_ready.sem, acc_ready.at(l, 3 * which + q + 1))

                for n in range(24):
                    q, j = n % 3, n // 3
                    t0, tn = CHUNKS[q]
                    if q < 2:
                        dve.wait_ge(o_psum.sem, o_psum.at(l, 2 * j + q + 1))
                    else:
                        dve.wait_ge(blk_used.sem, blk_used.at(l, B_OUT + j + 1))
                    x = XT[:, j, t0:t0 + tn]
                    V.scalar_tensor_tensor(x, PS[:, 3 * (j % 2) + q, :tn], ADA[:, A_G1 + j, COND[q]:COND[q] + 1], x,
                                           ALU.mult, ALU.add).then_inc(o_evac.sem, 1)
                    dve.wait_ge(o_evac.sem, o_evac.at(l, n + 1))
                    add_sums(0, n, j, q, SQO)
                norm(l, 0)

                def hidden(g, q):
                    t0, tn = CHUNKS[q]
                    for e in range(2):
                        u = 2 * q + e
                        dve.wait_ge(relu_done.sem, relu_done.at(l, u + 1) + g * 6)
                        V.tensor_tensor(SB2[:, e, :tn], RB[:, e, :tn], RB[:, e, :tn], ALU.mult).then_inc(sq_kept.sem, 1)
                        dve.wait_ge(sq_kept.sem, sq_kept.at(l, u + 1) + g * 6)
                        dve.wait_ge(hid_hi.sem, hid_hi.at(l, u + 1) + g * 6)
                        V.tensor_tensor(hidden_lo(q)[:, e, :tn], SB2[:, e, :tn], hidden_hi(q)[:, e, :tn].bitcast(F32),
                                        ALU.subtract).then_inc(hid_ready.sem, 1)

                def down(g, q, back):
                    t0, tn = CHUNKS[q]
                    for j in range(KT):
                        m = 8 * (q - 3 * back) + j
                        if q == 2 and j == KT - 1:
                            dve.wait_ge(blk_used.sem, blk_used.at(l, B_MLP + 4 * (1 - back)) + g * 4)
                        else:
                            dve.wait_ge(m2_psum.sem, m2_psum.at(l, 8 * q + j + 1 - 23 * back) + g * 23)
                        x = XT[:, j, t0:t0 + tn]
                        ins = V.scalar_tensor_tensor(x, PS[:, 2 + m % 6, :tn], ADA[:, A_G2 + j, COND[q]:COND[q] + 1], x,
                                                     ALU.mult, ALU.add)
                        ins.then_inc(m2_evac.sem, 1)

                def group(g, first=False):
                    hidden(g, 0)
                    if not first:
                        down(g, 2, 1)
                    hidden(g, 1)
                    down(g, 0, 0)
                    hidden(g, 2)
                    down(g, 1, 0)

                group(0, True)
                with dve.Fori(1, GROUPS - 1) as g:
                    group(g)
                g = GROUPS - 1
                hidden(g, 0)
                down(g, 2, 1)
                hidden(g, 1)
                down(g, 0, 0)
                dve.wait_ge(m2_evac.sem, m2_evac.at(l, 24 * g + 8))
                for j in range(KT):
                    add_sums(1, j, j, 0, SQM)
                hidden(g, 2)
                down(g, 1, 0)
                dve.wait_ge(m2_evac.sem, m2_evac.at(l, 24 * g + 16))
                for j in range(KT):
                    add_sums(1, 8 + j, j, 1, SQM)
                down(g, 2, 0)
                dve.wait_ge(m2_evac.sem, m2_evac.at(l, 24 * g + 24))
                for j in range(KT):
                    add_sums(1, 16 + j, j, 2, SQM)
                norm(l, 1)
                C.end_layer()


def bass_hyena_conformer_diffattn_dit(nc, ins, consts, outs):
    program(nc, ins, consts, outs)


_INS = ['x_prompt', 'x_sample', 'cache_k', 'cache_v', 'c', 'c_ctx', 'w_ada', 'b_ada', 'w_in',
        'hy_conv_w', 'hy_conv_b', 'hf_w1', 'hf_b1', 'hf_freq', 'hf_w2', 'hf_b2', 'hf_w3', 'hy_bias',
        'cf_conv_w', 'cf_conv_b', 'cf_ln_g', 'cf_ln_b', 'lam_q1', 'lam_k1', 'lam_q2', 'lam_k2',
        'subln_g', 'w_out', 'ln1_g', 'ln1_b', 'w_mlp1', 'w_mlp2', 'ln2_g', 'ln2_b']
_OUTS = [(1, 256, 1024), (1, 1024, 1024), (1, 2, 256, 8, 64), (1, 2, 256, 4, 128)]


def _constants():
    import numpy as np
    ident = np.eye(128)
    d = np.arange(128)
    partner = np.where(d % 32 < 16, d + 16, d - 16)
    swap = np.zeros((128, 128))
    swap[partner, d] = 1.0
    tok = np.arange(1024)
    f32 = np.float32
    inv = (f32(10000.0) ** (-(np.arange(0, 32, 2, dtype=f32)) / f32(32))).astype(f32)
    pos = np.where(((d // 32) % 2 == 0)[:, None], (tok // 64)[None, :], (tok % 64)[None, :]).astype(f32)
    ang = (pos * inv[d % 16][:, None]).astype(f32).astype(np.float64)
    sign = np.where(d % 32 < 16, -1.0, 1.0)[:, None]
    rope = np.stack([np.cos(ang), sign * np.sin(ang)], 1)
    feats, decay = [], []
    deltas = np.abs(np.linspace(math.log(1e-2) / 0.3, math.log(1e-2) / 1.5, 256))
    for n in (1024, 256):
        t = np.linspace(0.0, 1.0, n)[:, None]
        w = (2.0 * math.pi / n) * np.arange(n)[:, None]
        fr = np.linspace(1e-4, 15, 16)[None, :]
        feats.append(np.concatenate([t, np.cos(fr * w), -np.sin(fr * w)], -1))
        dec = np.exp(-t * deltas[None, :])
        back = dec.copy()
        back[0] = 0.0
        decay.append(np.concatenate([dec, back], 1))

    def dft(n):
        a = 2 * math.pi * ((np.arange(n)[:, None] * np.arange(n)[None, :]) % (2 * n - 1)) / (2 * n - 1)
        return np.stack([np.cos(a), np.sin(a)])

    small = dft(256).reshape(2, 2, 128, 256).transpose(2, 1, 0, 3).reshape(128, 1024)
    weight = np.full((128, 10), 2.0)
    weight[:, :8] /= 2047
    weight[:, 8:] /= 511
    weight[0, 0] /= 2
    weight[0, 8] /= 2
    lam = [0.8 - 0.6 * math.exp(-0.3 * k) for k in range(2)]
    lam = np.broadcast_to(np.array([[v, 1 - v] for v in lam])[:, None, :], (2, 128, 2))
    out = [ident, swap, rope, np.concatenate(feats).T, np.concatenate(decay), dft(1024), small, weight, lam]
    return [np.ascontiguousarray(a, dtype=f32) for a in out]


def kernel(**inputs):
    import numpy as _np
    import concourse.bacc as _bacc
    from concourse import mybir as _mybir
    from concourse.bass_utils import run_bass_kernel_spmd as _run

    nc = _bacc.Bacc("TRN2", target_bir_lowering=False, num_devices=1)
    arrays = {}

    def external(name, a):
        a = _np.ascontiguousarray(a)
        arrays[name] = a
        return nc.dram_tensor(name, a.shape, _mybir.dt.from_np(a.dtype), kind="ExternalInput").ap()

    ins = [external(f"in_{n}_dram", inputs[n]) for n in _INS]
    consts = [external(f"const_{i}_dram", a) for i, a in enumerate(_constants())]
    outs = [nc.dram_tensor(f"out_{i}_dram", s, _mybir.dt.from_np(_np.dtype("float32")), kind="ExternalOutput").ap()
            for i, s in enumerate(_OUTS)]
    bass_hyena_conformer_diffattn_dit(nc, ins, consts, outs)
    r = _run(nc, [arrays], core_ids=[0])
    return tuple(r.results[0][f"out_{i}_dram"] for i in range(len(_OUTS)))
```

```python
import math
from contextlib import ExitStack

import concourse.bass as bass
from concourse import mybir

F32 = mybir.dt.float32
F32R = mybir.dt.float32r
ALU = mybir.AluOpType
ACT = mybir.ActivationFunctionType
AX_X = mybir.AxisListType.X

DEPTH = 2
D = 1024
KT = D // 128
LS, LP = 1024, 256
T = LS + LP
TT = T // 128
ST, PT = LS // 128, LP // 128
PAST = 256
CHUNKS = [(0, 512), (512, 512), (1024, 256)]
COND = [0, 0, 1]
ZT = 22
HEADS = 4
FF_T = 32
GROUPS = FF_T // 2
RING = 6
ALPHA = (2 * DEPTH) ** 0.25
EPS = 1e-5
SCALE = 64 ** -0.5
TWO_PI = 2 * math.pi
ROUND = 1.5 * 2 ** 23
PI_BELOW = 3.1415925

B_IN, B_FWD, B_INV, B_OUT, B_MLP, BLOCKS = 0, 24, 42, 60, 68, 132
LEFT_OUT = {21: 2, 40: 1, 58: 1}
REAL = [b for b in range(BLOCKS) if b not in (22, 23, 41, 59)]
RAW_OF = {b: r for r, b in enumerate(REAL)}

V_BADA, V_LN, V_HYW, V_HYB, V_BIAS, ROWS_A = 0, 32, 64, 82, 88, 90
V_CFW, V_CFB, V_CFG, V_CFBB, V_SUB, ROWS_B = 90, 152, 154, 156, 158, 69
LN_G = [V_LN, V_LN + 16]
LN_B = [V_LN + 8, V_LN + 24]
A_G1, A_SH2, A_SC2, A_G2 = 0, 8, 16, 24

KEYS = PAST + T
S_KEYS = PAST + LS
ITEMS = [(0, S_KEYS)] * ST + [(S_KEYS, LP)] * PT

ROUNDS = ST * 3 + PT


def rounds(t):
    nk = ITEMS[t][1] // 128
    return [(g, min(4, nk - g)) for g in range(0, nk, 4)]


def first_round(t):
    return sum(len(rounds(i)) for i in range(t))


UNITS = [("hyena", c, q) for c in range(2) for q in range(3)] + \
        [("conformer", c, q) for c in range(2) for q in range(3)]
A_BEFORE, A_STEPS = 0, HEADS * (TT - 1)
V_BEFORE, V_STEPS, V_HEAD = 28, 546, 24
UNIT_AT = [6, 7, 8, 9, 10, 11, 12, 13, 15, 16, 18, 19]


class Signal:

    def __init__(self, sem, per_layer, start=0):
        self.sem, self.per_layer, self.start = sem, per_layer, start

    def at(self, l, k):
        return l * self.per_layer + (k + self.start)


class Chain:

    def __init__(self, engine, sem, per_layer, before):
        self.engine, self.sem, self.per_layer, self.before = engine, sem, per_layer, before
        self.n, self.l, self.i, self.per_i, self.trips, self.at_start = 0, None, None, 0, 0, 0

    def link(self, ins):
        self.n += 1
        ins.then_inc(self.sem, 1)
        value = self.n if self.l is None else self.l * self.per_layer + (self.n + self.before)
        if self.i is not None:
            value = value + self.i * self.per_i
        self.engine.wait_ge(self.sem, value)

    def layer(self, l):
        assert self.n == self.before, self.n
        self.l, self.n = l, 0

    def loop(self, i, per_i, trips):
        self.i, self.per_i, self.trips, self.at_start = i, per_i, trips, self.n

    def end_loop(self):
        assert self.n - self.at_start == self.per_i, self.n - self.at_start
        self.n, self.i = self.at_start + self.per_i * self.trips, None

    def end_layer(self):
        assert self.n == self.per_layer, self.n


def program(nc, ins, consts, outs):
    x_prompt, x_sample, cache_k, cache_v, c, c_ctx, w_ada, b_ada, w_in, hy_conv_w, hy_conv_b, \
        hf_w1, hf_b1, hf_freq, hf_w2, hf_b2, hf_w3, hy_bias, cf_conv_w, cf_conv_b, cf_ln_g, \
        cf_ln_b, lam_q1, lam_k1, lam_q2, lam_k2, subln_g, w_out, ln1_g, ln1_b, w_mlp1, w_mlp2, \
        ln2_g, ln2_b = ins
    ident_d, swap_d, rope_d, feats_d, decay_d, dft_d, dftp_d, weight_d, lam_d = consts
    y_prompt, y_sample, new_k, new_v = outs

    z_d = nc.dram_tensor("z_scratch", (ZT, 128, T), F32, kind="Internal").ap()
    hy_d = nc.dram_tensor("hyena_scratch", (2, 2, 128, T), F32, kind="Internal").ap()
    cf_d = nc.dram_tensor("conformer_scratch", (2, 128, T), F32, kind="Internal").ap()
    y_d = nc.dram_tensor("mixed_scratch", (KT, 128, T), F32, kind="Internal").ap()

    base = (nc.sbuf_base + 63) // 64 * 64

    def place(name, shape, dtype, offset):
        return nc.alloc_sbuf_tensor_at(name, shape, dtype, offset=offset)

    class Stack:
        def __init__(self, at, end):
            self.at, self.end = at, end

        def take(self, name, shape, dtype=F32):
            n = 4
            for s in shape[1:]:
                n *= s
            t = place(name, shape, dtype, self.at)
            self.at += (n + 31) // 32 * 32
            assert self.at <= self.end, (name, self.at - self.end)
            return t

    XT_O = base
    WS = XT_O + KT * T * 4
    HID_O = WS + 2 * KT * T * 4
    ADW_O = HID_O + 16384
    RING_O = ADW_O + 8192
    RAW_O = RING_O + 2 * RING * 4096
    SMALL_O = RAW_O + 8192
    XT = place("XT", [128, KT, T], F32, XT_O)
    HH = place("HH", [128, KT, T], F32R, WS)
    HL = place("HL", [128, KT, T], F32R, WS + KT * T * 4)
    ADW = place("ADW", [128, 2, 8, 128], F32, ADW_O)
    RH = place("RH", [128, RING, 1024], F32R, RING_O)
    RL = place("RL", [128, RING, 1024], F32R, RING_O + RING * 4096)
    RAW = place("RAW", [128, 2, 1024], F32, RAW_O)

    small = Stack(SMALL_O, nc.sbuf_usable_end)
    IDENT = small.take("IDENT", [128, 128])
    SWAPF = small.take("SWAPF", [128, 128])
    SWAP = small.take("SWAP", [128, 128], F32R)
    ONES = small.take("ONES", [128, 128])
    VEC = small.take("VEC", [128, ROWS_A + ROWS_B])
    LNV = small.take("LNV", [128, 32])
    ADA = small.take("ADA", [128, 32, 2])
    AD0 = small.take("AD0", [128, DEPTH + 1, 16, 2])
    CONDS = small.take("CONDS", [128, 16])
    EPSC = small.take("EPSC", [128, 1])
    ONE = small.take("ONE", [128, 1])
    WF = small.take("WF", [128, TT])
    HFV = small.take("HFV", [128, 4])
    LAMS = small.take("LAMS", [128, 4])
    LAMC = small.take("LAMC", [128, 4])
    STAT = small.take("STAT", [128, 4, 8])
    HB2_O = small.at
    VROW = small.take("VROW", [128, 128])
    VROWB = small.take("VROWB", [128, 128])
    LAMR = small.take("LAMR", [128, 4, 64])
    KO = small.take("KO", [128, 2, 128])
    VO = small.take("VO", [128, 2, 128])

    st = Stack(HID_O, ADW_O)
    XIN = st.take("XIN", [128, 2, 1024])
    CROW = st.take("CROW", [128, 128])
    BROW = st.take("BROW", [128, 128])
    B0 = st.take("B0", [128, 32])
    CRAW = st.take("CRAW", [128, 16])
    MODT = st.take("MODT", [128, 2, 512])
    st = Stack(HID_O, ADW_O)
    ZST = st.take("ZST", [128, 2, 512])
    HYIN = place("HYIN", [128, 3, 514], F32, st.at)
    CFIN = place("CFIN", [128, 2, 542], F32, st.at)
    st.at += 6176
    CACC = st.take("CACC", [128, 2, 512])
    st = Stack(WS, RING_O)
    MH = st.take("MH", [128, TT, 768], F32R)
    ML = st.take("ML", [128, TT, 768], F32R)
    FH = st.take("FH", [128, ST, 2, 256], F32R)
    FL = st.take("FL", [128, ST, 2, 256], F32R)
    GS = st.take("GS", [128, 2, 256])
    PR = st.take("PR", [128, 2, 256])
    PR2 = st.take("PR2", [128, 2, 256])
    YF = st.take("YF", [128, 2, 256])
    FPH = place("FPH", [128, PT, 2, 256], F32R, WS)
    FPL = place("FPL", [128, PT, 2, 256], F32R, WS + 4096)
    OLD = place("OLD", [128, 2, 512], F32, WS + 8192)
    OY = place("OY", [128, 512], F32, WS + 12288)
    st2 = Stack(WS + 2 * TT * 768 * 4, RING_O)
    FEAT = st2.take("FEAT", [128, T])
    HID1 = st2.take("HID1", [128, T])
    HID2 = st2.take("HID2", [128, T])
    ARG = st2.take("ARG", [128, T])
    RND = place("RND", [128, T], F32, WS)
    HW1 = place("HW1", [128, 2, 64], F32, WS + 6144)
    HW2 = place("HW2", [128, 2, 64], F32, WS + 6656)
    HW3 = st2.take("HW3", [128, 512])
    DEC = st2.take("DEC", [128, 2, 512])
    FB = st2.take("FB", [128, 512])
    FPM = st2.take("FPM", [128, 2, 256])
    UIN = st2.take("UIN", [128, 2, T])
    st = Stack(WS, SMALL_O)
    KH = st.take("KH", [128, 2, KEYS], F32R)
    KL = st.take("KL", [128, 2, KEYS], F32R)
    QQ = st.take("QQ", [128, 2, T], F32R)
    V2 = st.take("V2", [128, TT + 2, 256], F32R)
    PB = st.take("PB", [128, 2, 2, S_KEYS])
    AB = st.take("AB", [128, S_KEYS])
    ATH = st.take("ATH", [128, 2, S_KEYS], F32R)
    ATL = st.take("ATL", [128, 2, S_KEYS], F32R)
    OB = st.take("OB", [128, TT, 128])
    KR = st.take("KR", [128, KEYS])
    QR = st.take("QR", [128, T])
    VR = place("VR", [128, T], F32, st.at)
    st.at += 5120
    CKV = place("CKV", [128, 2, 2, 128], F32, st.at)
    st.at += 2048
    ROPE = st.take("ROPE", [128, 2, LS])
    O2 = st.take("O2", [128, 128])
    SSQ = st.take("SSQ", [128, TT])
    RRS = st.take("RRS", [128, TT])
    ZH = st.take("ZH", [128, 2, LS], F32R)
    ZL = st.take("ZL", [128, 2, LS], F32R)
    RT = st.take("RT", [128, LS])
    OT = st.take("OT", [128, T])
    SQJ = st.take("SQJ", [128, 128])
    st = Stack(HID_O, RING_O)
    YIN = st.take("YIN", [128, 2, 512])
    SQO = place("SQO", [128, 2, 512], F32, HID_O)
    st.at = HID_O + 4096
    ACC1 = st.take("ACC1", [128, 2, T])
    CFU = place("CFU", [128, 2, 512], F32, HID_O + 4096)
    CFS = place("CFS", [128, 2, 512], F32, HID_O + 8192)
    CFY = place("CFY", [128, 2, 512], F32, HID_O + 12288)
    MU = place("MU", [128, 512], F32, ADW_O)
    RS = place("RS", [128, 512], F32, ADW_O + 2048)
    LT = place("LT", [128, 512], F32, ADW_O + 4096)
    MR = place("MR", [128, 2, T], F32, HID_O + 4096)
    LTR = place("LTR", [128, 2, 512], F32, ADW_O + 4096)
    HT = place("HT", [128, 2, 512], F32, HID_O)
    HSB = place("HSB", [128, 2, KT, 2], F32, HID_O + 14336)
    HBH = place("HBH", [128, 2, 2, 512], F32R, HID_O)
    HBL = place("HBL", [128, 2, 2, 512], F32R, HID_O + 8192)
    HB2H = place("HB2H", [128, 2, 256], F32R, HB2_O)
    HB2L = place("HB2L", [128, 2, 256], F32R, HB2_O + 2048)
    RB = place("RB", [128, 2, 512], F32, ADW_O)
    SB2 = place("SB2", [128, 2, 512], F32, ADW_O + 4096)
    ACC2 = place("ACC2", [128, 2, T], F32, WS + KT * T * 4)
    SQM = place("SQM", [128, 2, 512], F32, ADW_O)

    def hidden_hi(q):
        return HBH[:, q] if q < 2 else HB2H[:]

    def hidden_lo(q):
        return HBL[:, q] if q < 2 else HB2L[:]

    nc.disable_value_cache = True
    with ExitStack() as ctx:
        PS = ctx.enter_context(nc.psum_tensor("PS", [128, 8, 512], F32))
        PSF = PS[:, :, :].rearrange("p b n -> p (b n)")

        def signal(name, per_layer=0, start=0):
            return Signal(ctx.enter_context(nc.semaphore(name)), per_layer, start)

        raw_in = [signal(f"raw_in{p}", 64 * 16) for p in range(2)]
        hi_split = signal("hi_split", len(REAL))
        blk_ready = signal("blk_ready", BLOCKS, BLOCKS)
        blk_used = signal("blk_used", BLOCKS, RING)
        ada_in = [signal(f"ada_in{p}", 16 * 16, 16 * 16) for p in range(2)]
        ada_used = signal("ada_used", 32, 34)
        const_in = signal("const_in")
        const_done = signal("const_done")
        one_ready = signal("one_ready")
        x_in = [signal(f"x_in{p}") for p in range(2)]
        x_turned = signal("x_turned")
        x_placed = signal("x_placed")
        row_turned = signal("row_turned")
        row_placed = signal("row_placed")
        silu_done = signal("silu_done")
        vec_in = signal("vec_in", 21 * 16)
        vec_turned = signal("vec_turned", 1)
        vec_ready = signal("vec_ready", 1)
        xn_ready = signal("xn_ready", 48)
        xs_ready = signal("xs_ready", 48, 1)
        hh_ready = signal("hh_ready", 48, 24)
        h_ready = signal("h_ready", 48, 24)
        mod_ready = signal("mod_ready", 2)
        var_ready = signal("var_ready", 6, 6)
        sd_ready = signal("sd_ready", 6)
        acc_ready = signal("acc_ready", 6)
        stats = signal("stats", 6)
        z_psum = signal("z_psum", 44)
        z_evac = signal("z_evac", 66, 6)
        z_stored = [signal(f"z_stored{p}", 33 * 16, 16) for p in range(2)]
        conv_in = signal("conv_in", 480)
        conv_done = signal("conv_done", 12, 1)
        conv_stored = signal("conv_stored", 288, 16)
        glu_done = signal("glu_done", 6)
        hf_in = signal("hf_in", 6 * 16)
        hf_psum = signal("hf_psum", 6)
        hf_read = signal("hf_read", 6)
        hf_arg = signal("hf_arg", 2)
        hf_sin = signal("hf_sin", 2)
        dec_in = [signal(f"dec_in{p}", 5 * 16) for p in range(2)]
        hft_psum = signal("hft_psum", TT)
        hft_read = signal("hft_read", TT, 1)
        dec_read = signal("dec_read", TT, 2)
        m_sum = signal("m_sum", TT)
        m_hi = signal("m_hi", TT)
        filt_ready = signal("filt_ready", TT)
        u_in = signal("u_in", 32)
        u_psum = signal("u_psum", TT)
        u_hi = signal("u_hi", TT)
        u_ready = signal("u_ready", TT, 2)
        dft_psum = signal("dft_psum", 1)
        g_scaled = signal("g_scaled", TT)
        f_sum = signal("f_sum", TT)
        f_hi = signal("f_hi", TT)
        f_ready = signal("f_ready", TT)
        inv_done = signal("inv_done", 0)
        old_in = signal("old_in", 6 * 32)
        old_read = signal("old_read", 6, 1)
        hy_done = signal("hy_done", 6)
        hy_stored = signal("hy_stored", 6 * 16, 16)
        at_tab = signal("at_tab", 16)
        lam_ready = signal("lam_ready", 1)
        lam_known = signal("lam_known", 1)
        head_in = signal("head_in", HEADS * 5 * 16)
        qk_split = signal("qk_split", HEADS, 1)
        kl_split = signal("kl_split", HEADS * 2, 2)
        prep_turned = signal("prep_turned", HEADS)
        kc_placed = signal("kc_placed", HEADS)
        v_hi = signal("v_hi", HEADS)
        v_split = signal("v_split", HEADS)
        rope_hi = signal("rope_hi", HEADS * 2)
        rope_lo = signal("rope_lo", HEADS * 2)
        rope_cos = signal("rope_cos", HEADS * 2)
        rope_swapped = signal("rope_swapped", HEADS * 2, 2)
        rope_done = signal("rope_done", HEADS * 2)
        qk_hi = signal("qk_hi", HEADS * 6)
        s_psum = signal("s_psum", HEADS * TT * 2)
        smax = signal("smax", HEADS * TT * 2)
        probs = signal("probs", HEADS * TT * 2)
        mixed = signal("mixed", HEADS * TT)
        at_psum = signal("at_psum", HEADS * ROUNDS)
        at_hi = signal("at_hi", HEADS * ROUNDS)
        at_lo = signal("at_lo", HEADS * ROUNDS)
        pv_psum = signal("pv_psum", HEADS * TT)
        o_part = signal("o_part", HEADS * TT)
        o_ready = signal("o_ready", HEADS * TT)
        ssq_done = signal("ssq_done", HEADS)
        sd_head = signal("sd_head", HEADS)
        o_normed = signal("o_normed", HEADS)
        o_turned = signal("o_turned", HEADS)
        o_placed = signal("o_placed", HEADS, 1)
        kv_copied = signal("kv_copied", HEADS)
        kv_stored = signal("kv_stored", HEADS * 32, 32)
        yat_stored = signal("yat_stored", HEADS * 16, 16)
        y_in = [signal(f"y_in{p}", 9 * 16) for p in range(2)]
        y_hi = signal("y_hi", 24)
        y_lo = signal("y_lo", 24, 2)
        cf_in = signal("cf_in", 6 * 16)
        cf_sq = signal("cf_sq", 3)
        cf_stats = signal("cf_stats", 3)
        cf_var = signal("cf_var", 3)
        cf_sd = signal("cf_sd", 3)
        cf_norm = signal("cf_norm", 3)
        cf_silu = signal("cf_silu", 3)
        o_psum = signal("o_psum", 16)
        o_evac = signal("o_evac", 24, 6)
        sq_ready = signal("sq_ready", 48)
        sq_added = signal("sq_added", 48, 2)
        m1_psum = signal("m1_psum", GROUPS * 4)
        relu_done = signal("relu_done", GROUPS * 6)
        hid_hi = signal("hid_hi", GROUPS * 6)
        hid_ready = signal("hid_ready", GROUPS * 6, 2)
        m2_psum = signal("m2_psum", GROUPS * 23, 16)
        m2_evac = signal("m2_evac", GROUPS * 24, 6)
        y_turned = signal("y_turned")
        y_placed = signal("y_placed")
        y_stored = [signal(f"y_stored{p}") for p in range(2)]
        pads_ready = signal("pads_ready", 6)
        sq_kept = signal("sq_kept", GROUPS * 6)
        lam_exp = signal("lam_exp", 1)
        v_chain = ctx.enter_context(nc.semaphore("v_chain"))
        a_chain = ctx.enter_context(nc.semaphore("a_chain"))

        block = ctx.enter_context(nc.Block())

        def column_block(w, l, j):
            return w[l].rearrange("(k p) n -> p k n", p=128)[:, :, bass.ts(j, 128)]

        def raw_view(p):
            return RAW[:, p, :].rearrange("p (k n) -> p k n", k=8)

        def dft_columns(part, j):
            return dft_d[part].rearrange("(k p) n -> p k n", p=128)[:, :, j * 128:(j + 1) * 128]

        def dft_rows(part, j):
            return dft_d[part, j * 128:(j + 1) * 128, :]

        @block.sync
        def _(sp):
            def load_block(l, b, i, source, view3):
                r = RAW_OF[b]
                p = r % 2
                if r >= 2:
                    before = REAL[r - 2] + 1
                else:
                    before = REAL[r - 2] + 1 - BLOCKS
                sp.wait_ge(blk_ready.sem, blk_ready.at(l, before) + i * RING)
                sp.dma_start(raw_view(p) if view3 else RAW[:, p, :], source).then_inc(raw_in[p].sem, 16)

            def load_ada(l, a, t):
                sp.wait_ge(ada_used.sem, ada_used.at(l, a - 1))
                sp.dma_start(ADW[:, a % 2], column_block(w_ada, l, t)).then_inc(ada_in[a % 2].sem, 16)

            for n, (dst, src) in enumerate([(IDENT[:], ident_d), (SWAPF[:], swap_d), (WF[:], weight_d),
                                            (CROW[0:8, :], c.rearrange("a (k p) -> (a k) p", p=128)),
                                            (CROW[8:16, :], c_ctx.rearrange("(k p) -> k p", p=128)),
                                            (BROW[0:16, :], b_ada[0, 0:2048].rearrange("(k p) -> k p", p=128)),
                                            (BROW[16:32, :], b_ada[1, 0:2048].rearrange("(k p) -> k p", p=128))]):
                sp.dma_start(dst, src).then_inc(const_in.sem, 16)
            for t in range(TT):
                if t >= 2:
                    sp.wait_ge(x_turned.sem, t - 1)
                src = x_sample[0, t * 128:(t + 1) * 128, :] if t < ST else \
                    x_prompt[0, (t - ST) * 128:(t - ST + 1) * 128, :]
                sp.dma_start(XIN[:, t % 2], src).then_inc(x_in[t % 2].sem, 16)
            for a in range(32):
                sp.wait_ge(ada_used.sem, a + 1)
                sp.dma_start(ADW[:, a % 2], column_block(w_ada, a // 16, a % 16)).then_inc(ada_in[a % 2].sem, 16)

            with sp.Fori(0, DEPTH) as l:
                sp.wait_ge(blk_used.sem, blk_used.at(l, 0))
                rows_a = [(V_BADA, b_ada[l].rearrange("(r p) -> r p", p=128)[16:48]),
                          (V_LN, ln1_g[l].rearrange("(r p) -> r p", p=128)),
                          (V_LN + 8, ln1_b[l].rearrange("(r p) -> r p", p=128)),
                          (V_LN + 16, ln2_g[l].rearrange("(r p) -> r p", p=128)),
                          (V_LN + 24, ln2_b[l].rearrange("(r p) -> r p", p=128)),
                          (V_HYW, hy_conv_w[l].rearrange("k (r p) -> (k r) p", p=128)),
                          (V_HYB, hy_conv_b[l].rearrange("(r p) -> r p", p=128)),
                          (V_BIAS, hy_bias[l].rearrange("(r p) -> r p", p=128))]
                rows_b = [(0, cf_conv_w[l].rearrange("k (r p) -> (k r) p", p=128)),
                          (62, cf_conv_b[l].rearrange("(r p) -> r p", p=128)),
                          (64, cf_ln_g[l].rearrange("(r p) -> r p", p=128)),
                          (66, cf_ln_b[l].rearrange("(r p) -> r p", p=128)),
                          (68, subln_g[l].rearrange("(r p) -> r p", p=128))]
                for dst, rows in ((VROW, rows_a), (VROWB, rows_b)):
                    for r, src in rows:
                        sp.dma_start(dst[r:r + src.shape[0], :], src).then_inc(vec_in.sem, 16)
                for n, v in enumerate((hf_b1, hf_freq, hf_b2)):
                    sp.dma_start(HFV[0:64, n:n + 1], v[l].rearrange("(p a) -> p a", a=1)).then_inc(vec_in.sem, 16)
                for n, v in enumerate((lam_q1, lam_k1, lam_q2, lam_k2)):
                    sp.dma_start(LAMR[:, n, :], v[l].rearrange("(a n) -> a n", a=1).broadcast_to([128, 64]))\
                       .then_inc(vec_in.sem, 16)
                sp.dma_start(LAMC[:, 0:2], lam_d[l]).then_inc(vec_in.sem, 16)

                with sp.Fori(0, 2) as i:
                    for q in range(6):
                        load_block(l, B_IN + q, i, column_block(w_in, l, i * 6 + q), True)
                        if q == 0:
                            sp.wait_ge(h_ready.sem, h_ready.at(l, 0))
                        for e in range(2):
                            a = 2 * q + e
                            sp.wait_ge(ada_used.sem, ada_used.at(l, a - 1) + i * 12)
                            sp.dma_start(ADW[:, a % 2], column_block(w_ada, l, i * 12 + (16 + a)))\
                              .then_inc(ada_in[a % 2].sem, 16)
                for q in range(12, ZT):
                    load_block(l, B_IN + q, 0, column_block(w_in, l, q), True)
                    if q < 16:
                        for e in range(2):
                            load_ada(l, 2 * q + e, 16 + 2 * q + e)
                for j in range(ST):
                    for part in range(2):
                        load_block(l, B_FWD + 2 * j + part, 0, dft_columns(part, j), True)
                load_block(l, B_FWD + 16, 0, dftp_d, False)
                for j in range(ST):
                    for part in range(2):
                        load_block(l, B_INV + 2 * j + part, 0, dft_rows(part, j), False)
                load_block(l, B_INV + 16, 0, dftp_d, False)

                for p in range(2):
                    sp.wait_ge(z_stored[p].sem, z_stored[p].at(l, 33 * 16))
                sp.wait_ge(hy_stored.sem, hy_stored.at(l, 6 * 16))
                sp.dma_start(ROPE[:], rope_d).then_inc(at_tab.sem, 16)
                with sp.Fori(0, HEADS) as h:
                    sp.wait_ge(qk_split.sem, qk_split.at(l, 0) + h)
                    sp.wait_ge(kl_split.sem, kl_split.at(l, 0) + h * 2)
                    sp.dma_start(KR[:, PAST:KEYS], z_d[h + 14]).then_inc(head_in.sem, 16)
                    sp.dma_start(QR[:], z_d[h + 10]).then_inc(head_in.sem, 16)
                    sp.dma_start(VR[:], z_d[h + 18]).then_inc(head_in.sem, 16)
                    sp.dma_start(CKV[:, 0], cache_k[0, l].rearrange("(t p) m d -> p t (m d)", p=128)
                                 [:, :, bass.ts(h, 128)]).then_inc(head_in.sem, 16)
                    sp.dma_start(CKV[:, 1], cache_v[0, l].rearrange("(t p) m d -> p t (m d)", p=128)
                                 [:, :, bass.ts(h, 128)]).then_inc(head_in.sem, 16)
                sp.wait_ge(yat_stored.sem, yat_stored.at(l, HEADS * 16))
                n = 0
                for q, (t0, tn) in enumerate(CHUNKS):
                    if q:
                        sp.wait_ge(cf_norm.sem, cf_norm.at(l, q))
                    for ct in range(2):
                        sp.dma_start(CFU[:, ct, :tn], cf_d[ct, :, t0:t0 + tn]).then_inc(cf_in.sem, 16)
                    for j in (0, 1, 4, 5, 6, 7):
                        before = 8 * ((n - 2) // 6) + (n - 2) % 6 + 1 if n >= 2 else 0
                        sp.wait_ge(y_lo.sem, y_lo.at(l, before))
                        sp.dma_start(YIN[:, n % 2, :tn], y_d[j, :, t0:t0 + tn]).then_inc(y_in[n % 2].sem, 16)
                        n += 1
                for q in range(8):
                    load_block(l, B_OUT + q, 0, column_block(w_out, l, q), True)
                with sp.Fori(0, GROUPS) as g:
                    for e in range(4):
                        b = B_MLP + e
                        p = RAW_OF[b] % 2
                        sp.wait_ge(blk_ready.sem, blk_ready.at(l, b - 1) + g * 4)
                        if e < 2:
                            sp.dma_start(raw_view(p), column_block(w_mlp1, l, g * 2 + e)).then_inc(raw_in[p].sem, 16)
                        else:
                            sp.dma_start(RAW[:, p, :], w_mlp2[l].rearrange("(j p) n -> j p n", p=128)[g * 2 + (e - 2)])\
                              .then_inc(raw_in[p].sem, 16)

        @block.gpsimd
        def _(pool):
            for freed in [blk_ready, blk_used, z_evac, *z_stored, conv_done, conv_stored, var_ready,
                          hft_read, dec_read, u_ready, old_read, hy_stored, xs_ready, qk_split, kl_split, o_placed, rope_swapped,
                          kv_stored, yat_stored, y_lo, o_evac, sq_added, hid_ready, m2_psum, m2_evac]:
                pool.sem_inc(freed.sem, freed.start)
            pool.sem_inc(ada_used.sem, 2)
            nc.gpsimd.memset(ONE[:], 1.0).then_inc(one_ready.sem, 1)
            pool.wait_ge(one_ready.sem, 1)

            def split(l, b, i, per_i):
                r, s = RAW_OF[b], b % RING
                p = r % 2
                pool.wait_ge(raw_in[p].sem, raw_in[p].at(l, 16 * (r // 2 + 1)) + i * (8 * per_i))
                pool.wait_ge(blk_used.sem, blk_used.at(l, b - RING + 1) + i * per_i)
                nc.gpsimd.tensor_tensor(RH[:, s, :], RAW[:, p, :], ONE[:].broadcast_to([128, 1024]), ALU.mult).then_inc(hi_split.sem, 1)
                pool.wait_ge(hi_split.sem, hi_split.at(l, r + 1) + i * per_i)
                nc.gpsimd.tensor_tensor(RL[:, s, :], RAW[:, p, :], RH[:, s, :].bitcast(F32), ALU.subtract)\
                  .then_inc(blk_ready.sem, 1 + LEFT_OUT.get(b, 0))

            with pool.Fori(0, DEPTH) as l:
                with pool.Fori(0, 2) as i:
                    for q in range(6):
                        split(l, B_IN + q, i, 6)
                for b in REAL[12:RAW_OF[B_OUT]]:
                    split(l, b, 0, 4)
                with pool.Fori(0, HEADS) as h:
                    for n, src in enumerate((QR[:], KR[:, PAST:PAST + LS])):
                        if n == 0:
                            pool.wait_ge(at_tab.sem, at_tab.at(l, 16))
                            pool.wait_ge(head_in.sem, head_in.at(l, 80) + h * 80)
                        pool.wait_ge(rope_swapped.sem, rope_swapped.at(l, n - 1) + h * 2)
                        nc.gpsimd.tensor_tensor(ZH[:, n], src[:, 0:LS], ONE[:].broadcast_to([128, LS]), ALU.mult)\
                            .then_inc(rope_hi.sem, 1)
                        pool.wait_ge(rope_hi.sem, rope_hi.at(l, n + 1) + h * 2)
                        nc.gpsimd.tensor_tensor(ZL[:, n], src[:, 0:LS], ZH[:, n].bitcast(F32), ALU.subtract)\
                            .then_inc(rope_lo.sem, 1)
                        pool.wait_ge(rope_lo.sem, rope_lo.at(l, n + 1) + h * 2)
                        nc.gpsimd.tensor_tensor(src[:, 0:LS], src[:, 0:LS], ROPE[:, 0, :], ALU.mult)\
                            .then_inc(rope_cos.sem, 1)
                    for m in range(2):
                        own = slice(64 * m, 64 * m + 64)
                        pool.wait_ge(qk_hi.sem, qk_hi.at(l, m + 1) + h * 6)
                        nc.gpsimd.tensor_tensor(KL[own, m, :], KR[own, :], KH[own, m, :].bitcast(F32), ALU.subtract)\
                            .then_inc(kl_split.sem, 1)
                for b in REAL[RAW_OF[B_OUT]:RAW_OF[B_MLP] + 4]:
                    split(l, b, 0, 4)
                with pool.Fori(0, 5) as i:
                    for q in range(12):
                        split(l, B_MLP + 4 + q, i, 12)
                for n in range(24):
                    q, j = n // 8, n % 8
                    t0, tn = CHUNKS[q]
                    dst = ACC2[:, 1, t0:t0 + tn]
                    pool.wait_ge(sq_ready.sem, sq_ready.at(l, 24 + n + 1))
                    if j == 0:
                        ins = nc.gpsimd.tensor_tensor(dst, SQM[:, n % 2, :tn], ONE[:].broadcast_to([128, tn]), ALU.mult)
                    else:
                        pool.wait_ge(sq_added.sem, sq_added.at(l, 24 + n))
                        ins = nc.gpsimd.tensor_tensor(dst, dst, SQM[:, n % 2, :tn], ALU.add)
                    ins.then_inc(sq_added.sem, 1)

        @block.tensor
        def _(pe):
            def weights_ready(l, b, i=0, per_i=0):
                pe.wait_ge(blk_ready.sem, blk_ready.at(l, b + 1) + i * per_i)

            def column_product(out, s, hi, lo, beside=None):
                for n, (w, m) in enumerate(((RH, hi), (RH, lo), (RL, hi))):
                    for k in range(KT):
                        mm = pe.matmul(out, w[:, s, k * 128:(k + 1) * 128], m(k),
                                       start=(n == 0 and k == 0), stop=(n == 2 and k == KT - 1))
                        if n == 1 and beside is not None:
                            beside(k)
                return mm

            pe.wait_ge(const_in.sem, 7 * 16)
            pe.transpose(PS[:, 6, 0:16], CROW[0:16, :], IDENT[0:16, 0:16])
            pe.transpose(PS[:, 6, 16:48], BROW[0:32, :], IDENT[0:32, 0:32]).then_inc(row_turned.sem, 1)
            for t in range(TT):
                pe.wait_ge(x_in[t % 2].sem, 16 * (t // 2 + 1))
                if t >= 2:
                    pe.wait_ge(x_placed.sem, t - 1)
                for j in range(KT):
                    mm = pe.transpose(PSF[:, (t % 2) * 1024 + j * 128:(t % 2) * 1024 + (j + 1) * 128],
                                      XIN[:, t % 2, j * 128:(j + 1) * 128], IDENT[:])
                mm.then_inc(x_turned.sem, 1)
            pe.wait_ge(silu_done.sem, 1)

            def ada_tile(a, col):
                cv = CONDS[:, :].rearrange("p (v k) -> p k v", v=2)
                for k in range(KT):
                    mm = pe.matmul(PS[:, 7, 2 * col:2 * col + 2], ADW[:, a % 2, k, :], cv[:, k, :],
                                   start=(k == 0), stop=(k == KT - 1))
                mm.then_inc(ada_used.sem, 1)

            for a in range(32):
                pe.wait_ge(ada_in[a % 2].sem, 16 * (a // 2 + 1))
                ada_tile(a, a)

            with pe.Fori(0, DEPTH) as l:
                def z_tile(n, i, per_i):
                    s, p = n % RING, n % 2
                    weights_ready(l, B_IN + n, i, per_i)
                    for q, (t0, tn) in enumerate(CHUNKS):
                        if n == 0:
                            pe.wait_ge(h_ready.sem, h_ready.at(l, 8 * (q - 2)))
                            pe.wait_ge(var_ready.sem, var_ready.at(l, -1))
                        pe.wait_ge(z_evac.sem, z_evac.at(l, 3 * n + q - 5) + i * (3 * per_i))
                        a = 2 * n + q
                        with_ada = q < 2 and n < 16
                        if with_ada:
                            pe.wait_ge(ada_in[q].sem, ada_in[q].at(l, 16 * (n + 1)) + i * (16 * per_i))

                        def ada(k):
                            m = pe.matmul(PS[:, 7, bass.ds(i * (4 * per_i) + 2 * a, 2) if per_i else
                                             slice(2 * a, 2 * a + 2)],
                                          ADW[:, q, k, :], CONDS[:, :].rearrange("p (v k) -> p k v", v=2)[:, k, :],
                                          start=(k == 0), stop=(k == KT - 1))
                            if k == KT - 1:
                                m.then_inc(ada_used.sem, 1)

                        mm = column_product(PS[:, 3 * p + q, 0:tn], s, lambda k: HH[:, k, t0:t0 + tn],
                                            lambda k: HL[:, k, t0:t0 + tn], ada if with_ada else None)
                        if q < 2:
                            mm.then_inc(z_psum.sem, 1)
                    mm.then_inc(blk_used.sem, 1 + LEFT_OUT.get(n, 0))

                def vectors():
                    pe.wait_ge(h_ready.sem, h_ready.at(l, -16))
                    pe.wait_ge(vec_in.sem, vec_in.at(l, 16 * 21))
                    pe.transpose(PS[:, 6, 0:ROWS_A], VROW[0:ROWS_A, :], IDENT[0:ROWS_A, 0:ROWS_A])
                    pe.transpose(PS[:, 6, ROWS_A:ROWS_A + ROWS_B], VROWB[0:ROWS_B, :],
                                 IDENT[0:ROWS_B, 0:ROWS_B]).then_inc(vec_turned.sem, 1)

                vectors()
                with pe.Fori(0, 2) as i:
                    for n in range(6):
                        z_tile(n, i, 6)
                for n in range(12, ZT):
                    z_tile(n, 0, 0)

                pe.wait_ge(hf_in.sem, hf_in.at(l, 6 * 16))
                pe.wait_ge(z_evac.sem, z_evac.at(l, 66))
                for layer_no, (w, kk, src) in enumerate(((HW1, 33, FEAT), (HW2, 64, HID1))):
                    if layer_no:
                        pe.wait_ge(hf_sin.sem, hf_sin.at(l, 1))
                    for q, (t0, tn) in enumerate(CHUNKS):
                        pe.matmul(PS[:, 3 * layer_no + q, 0:tn], w[0:kk].rearrange("p a n -> p (a n)"), src[0:kk, t0:t0 + tn],
                                  start=True, stop=True).then_inc(hf_psum.sem, 1)
                pe.wait_ge(hf_sin.sem, hf_sin.at(l, 2))
                pe.wait_ge(u_in.sem, u_in.at(l, 32))
                for t in range(TT):
                    pe.wait_ge(hft_read.sem, hft_read.at(l, max(t - 1, 0)))
                    pe.matmul(PS[:, t % 2, :], HID2[0:64, t * 128:(t + 1) * 128], HW3[0:64, :],
                              start=True, stop=True).then_inc(hft_psum.sem, 1)
                    pe.wait_ge(u_ready.sem, u_ready.at(l, t - 1))
                    for ct in range(2):
                        mm = pe.transpose(PS[:, 2 + t % 2, ct * 128:(ct + 1) * 128],
                                          UIN[:, ct, t * 128:(t + 1) * 128], IDENT[:])
                    mm.then_inc(u_psum.sem, 1)
                pe.wait_ge(filt_ready.sem, filt_ready.at(l, TT))
                pe.wait_ge(u_ready.sem, u_ready.at(l, TT))
                for j in range(ST):
                    for part in range(2):
                        b = B_FWD + 2 * j + part
                        weights_ready(l, b)
                        if j >= 2:
                            pe.wait_ge(f_sum.sem, f_sum.at(l, j - 1))
                        c0 = 256 * part
                        column_product(PS[:, 2 * (j % 2) + part, :], b % RING,
                                       lambda k: MH[:, k, c0:c0 + 512], lambda k: ML[:, k, c0:c0 + 512])\
                            .then_inc(blk_used.sem, 1)
                b = B_FWD + 16
                weights_ready(l, b)
                pblk = [W[:, b % RING, :].rearrange("p (t n) -> p t n", t=2) for W in (RH, RL)]
                for j in range(PT):
                    pe.wait_ge(f_sum.sem, f_sum.at(l, ST + j - 1))
                    for part in range(2):
                        c0, f0 = 256 * part, 256 * part + 128 * j
                        for n, (w, m) in enumerate(((pblk[0], MH), (pblk[0], ML), (pblk[1], MH))):
                            for k in range(PT):
                                mm = pe.matmul(PS[:, 2 * (j % 2) + part, :], w[:, k, f0:f0 + 128],
                                               m[:, ST + k, c0:c0 + 512],
                                               start=(n == 0 and k == 0), stop=(n == 2 and k == 1))
                    if j == 0:
                        mm.then_inc(dft_psum.sem, 1)
                mm.then_inc(blk_used.sem, 2)
                for j in range(ST):
                    for part in range(2):
                        b = B_INV + 2 * j + part
                        weights_ready(l, b)
                        if part == 0:
                            pe.wait_ge(f_ready.sem, f_ready.at(l, j + 1))
                        for ct in range(2):
                            for n, (f, w) in enumerate(((FH, RH), (FH, RL), (FL, RH))):
                                for q in range(2):
                                    mm = pe.matmul(PS[:, 4 + 2 * ct + q, :], f[:, j, part, ct * 128:(ct + 1) * 128],
                                                   w[:, b % RING, q * 512:(q + 1) * 512],
                                                   start=(j == 0 and part == 0 and n == 0),
                                                   stop=(j == ST - 1 and part == 1 and n == 2))
                        mm.then_inc(blk_used.sem, 1)
                b = B_INV + 16
                weights_ready(l, b)
                pe.wait_ge(f_ready.sem, f_ready.at(l, TT))
                pblk = [W[:, b % RING, :].rearrange("p (t n) -> p t n", t=2) for W in (RH, RL)]
                for ct in range(2):
                    for j in range(PT):
                        for part in range(2):
                            for n, (f, w) in enumerate(((FPH, pblk[0]), (FPH, pblk[1]), (FPL, pblk[0]))):
                                mm = pe.matmul(PS[:, ct, 0:256], f[:, j, part, ct * 128:(ct + 1) * 128],
                                               w[:, j, 256 * part:256 * part + 256],
                                               start=(j == 0 and part == 0 and n == 0),
                                               stop=(j == 1 and part == 1 and n == 2))
                mm.then_inc(blk_used.sem, 2)

                def swaps(h):
                    for n in range(2):
                        pe.wait_ge(rope_lo.sem, rope_lo.at(l, n + 1) + h * 2)
                        for q in range(2):
                            cols = slice(512 * q, 512 * q + 512)
                            pe.matmul(PS[:, 1 + 3 * n + q, :], SWAP[:], ZH[:, n, cols], start=True, stop=False)
                            mm = pe.matmul(PS[:, 1 + 3 * n + q, :], SWAP[:], ZL[:, n, cols], start=False, stop=True)
                        mm.then_inc(rope_swapped.sem, 1)

                def turn_inputs(h):
                    pe.wait_ge(rope_done.sem, rope_done.at(l, 2) + h * 2)
                    for t in range(2):
                        pe.transpose(PS[:, 0, t * 128:(t + 1) * 128], CKV[:, 0, t, :], IDENT[:])
                        pe.transpose(PS[:, 0, 256 + t * 128:256 + (t + 1) * 128],
                                     KR[:, S_KEYS + t * 128:S_KEYS + (t + 1) * 128], IDENT[:])
                    for t in range(TT):
                        mm = pe.transpose(PSF[:, 512 + t * 128:512 + (t + 1) * 128],
                                          VR[:, t * 128:(t + 1) * 128], IDENT[:])
                    mm.then_inc(prep_turned.sem, 1)

                def head(h, last):
                    pe.wait_ge(qk_split.sem, qk_split.at(l, 1) + h)
                    pe.wait_ge(kl_split.sem, kl_split.at(l, 2) + h * 2)
                    pe.wait_ge(o_placed.sem, o_placed.at(l, 0) + h)

                    def scores(t):
                        k0, kn = ITEMS[t]
                        for m in range(2):
                            if t:
                                pe.wait_ge(probs.sem, probs.at(l, 2 * t - 1 + m) + h * (2 * TT))
                            pieces = [(o, min(512, kn - o)) for o in range(0, kn, 512)]
                            for o, w in pieces:
                                for x, kk in enumerate((KH, KL)):
                                    mm = pe.matmul(PSF[:, 1536 * m + o:1536 * m + o + w],
                                                   QQ[:, m, t * 128:(t + 1) * 128],
                                                   kk[:, m, k0 + o:k0 + o + w], start=(x == 0), stop=(x == 1))
                            mm.then_inc(s_psum.sem, 1)

                    def turn(t, which):
                        for r, (g0, gn) in enumerate(rounds(t)):
                            if r not in which:
                                continue
                            if r == 0:
                                pe.wait_ge(mixed.sem, mixed.at(l, t + 1) + h * TT)
                            if r == 1 and t > 1:
                                pe.wait_ge(o_ready.sem, o_ready.at(l, t - 1) + h * TT)
                            elif r != 1 and (r or t):
                                pe.wait_ge(at_lo.sem, at_lo.at(l, first_round(t) + (1 if r else 0)) + h * ROUNDS)
                            for e in range(gn):
                                mm = pe.transpose(PS[:, 6 + r % 2, e * 128:(e + 1) * 128],
                                                  AB[:, (g0 + e) * 128:(g0 + e + 1) * 128], IDENT[:])
                            mm.then_inc(at_psum.sem, 1)

                    def values(t, seen):
                        k0, kn = ITEMS[t]
                        pe.wait_ge(at_lo.sem, at_lo.at(l, seen) + h * ROUNDS)
                        if t:
                            pe.wait_ge(o_ready.sem, o_ready.at(l, t) + h * TT)
                        nk = kn // 128
                        for k in range(nk):
                            kt = k0 // 128 + k
                            pe.matmul(PS[:, 7, 0:256], ATH[:, t % 2, k * 128:(k + 1) * 128], V2[:, kt, :],
                                      start=(k == 0), stop=False)
                            mm = pe.matmul(PS[:, 7, 0:128], ATL[:, t % 2, k * 128:(k + 1) * 128],
                                           V2[:, kt, 0:128], start=False, stop=(k == nk - 1))
                        mm.then_inc(pv_psum.sem, 1)

                    scores(0)
                    scores(1)
                    for t in range(TT):
                        turn(t, (0, 1))
                        if t + 2 < TT:
                            scores(t + 2)
                        turn(t, (2,))
                        if t == ST and not last:
                            swaps(h + 1)
                        if t:
                            values(t - 1, first_round(t) + (2 if len(rounds(t)) > 1 else 0))
                    values(TT - 1, ROUNDS)
                    if not last:
                        turn_inputs(h + 1)
                    pe.wait_ge(o_normed.sem, o_normed.at(l, 1) + h)
                    for t in range(TT):
                        mm = pe.transpose(PSF[:, 2048 + t * 128:2048 + (t + 1) * 128], OB[:, t, :], IDENT[:])
                    mm.then_inc(o_turned.sem, 1)

                pe.wait_ge(hy_done.sem, hy_done.at(l, 6))
                swaps(0)
                turn_inputs(0)
                with pe.Fori(0, HEADS - 1) as h:
                    head(h, False)
                head(HEADS - 1, True)
                pe.wait_ge(o_placed.sem, o_placed.at(l, HEADS))

                for q, (t0, tn) in enumerate(CHUNKS):
                    pe.wait_ge(cf_sq.sem, cf_sq.at(l, q + 1))
                    pe.wait_ge(cf_in.sem, cf_in.at(l, 32 * (q + 1)))
                    for n, src in enumerate((CFU, CFS)):
                        for ct in range(2):
                            mm = pe.matmul(PS[:, 6 + n, 0:tn], ONES[:], src[:, ct, 0:tn], start=(ct == 0), stop=(ct == 1))
                    mm.then_inc(cf_stats.sem, 1)

                for n in range(KT):
                    b = B_OUT + n
                    weights_ready(l, b)
                    for q, (t0, tn) in enumerate(CHUNKS):
                        if n == 0:
                            pe.wait_ge(y_lo.sem, y_lo.at(l, 8 * (q + 1)))
                        pe.wait_ge(o_evac.sem, o_evac.at(l, 3 * n + q - 5))
                        mm = column_product(PS[:, 3 * (n % 2) + q, 0:tn], b % RING,
                                            lambda k: HH[:, k, t0:t0 + tn], lambda k: HL[:, k, t0:t0 + tn])
                        if q < 2:
                            mm.then_inc(o_psum.sem, 1)
                    mm.then_inc(blk_used.sem, 1)

                def norm_sums(which, q, bank):
                    t0, tn = CHUNKS[q]
                    pe.wait_ge(acc_ready.sem, acc_ready.at(l, 3 * which + q + 1))
                    if which:
                        pe.wait_ge(sq_added.sem, sq_added.at(l, 24 + 8 * (q + 1)))
                    for n in range(2):
                        mm = pe.matmul(PS[:, bank + n, 0:tn], ONES[:], (ACC1, ACC2)[which][:, n, t0:t0 + tn],
                                       start=True, stop=True)
                    mm.then_inc(stats.sem, 1)

                for q in range(3):
                    norm_sums(0, q, (6, 0, 2)[q])

                def up(g0, q, i):
                    t0, tn = CHUNKS[q]
                    for e in range(2):
                        b = B_MLP + 4 * g0 + e
                        if q == 0:
                            weights_ready(l, b, i, 12)
                        if e == 0:
                            pe.wait_ge(hid_ready.sem, hid_ready.at(l, 2 * (3 * g0 + q)) + i * 18)
                        mm = column_product(PS[:, e, 0:tn], b % RING,
                                            lambda k: HH[:, k, t0:t0 + tn], lambda k: HL[:, k, t0:t0 + tn])
                        if q < 2:
                            mm.then_inc(m1_psum.sem, 1)
                        else:
                            mm.then_inc(blk_used.sem, 1)

                def down(g0, q, i):
                    t0, tn = CHUNKS[q]
                    b = B_MLP + 4 * g0 + 2
                    if q == 0:
                        weights_ready(l, b + 1, i, 12)
                    pe.wait_ge(hid_ready.sem, hid_ready.at(l, 2 * (3 * g0 + q) + 2) + i * 18)
                    for j in range(KT):
                        m = 8 * (3 * g0 + q) + j
                        pe.wait_ge(m2_evac.sem, m2_evac.at(l, m - 5) + i * 72)
                        for n, (w, x) in enumerate(((RH, hidden_hi(q)), (RH, hidden_lo(q)), (RL, hidden_hi(q)))):
                            for e in range(2):
                                mm = pe.matmul(PS[:, 2 + m % 6, 0:tn], w[:, (b + e) % RING, j * 128:(j + 1) * 128],
                                               x[:, e, 0:tn], start=(n == 0 and e == 0),
                                               stop=(n == 2 and e == 1))
                        if q == 2 and j == KT - 1:
                            mm.then_inc(blk_used.sem, 2)
                        else:
                            mm.then_inc(m2_psum.sem, 1)

                for q in range(3):
                    pe.wait_ge(h_ready.sem, h_ready.at(l, 8 * (q + 1)))
                    pe.wait_ge(var_ready.sem, var_ready.at(l, min(q + 2, 3)))
                    up(0, q, 0)
                    if q:
                        down(0, q - 1, 0)
                with pe.Fori(0, 5) as i:
                    for g in range(1, 4):
                        up(g, 0, i)
                        down(g - 1, 2, i)
                        up(g, 1, i)
                        down(g, 0, i)
                        up(g, 2, i)
                        down(g, 1, i)
                pe.wait_ge(hid_ready.sem, hid_ready.at(l, 6 * GROUPS))
                norm_sums(1, 0, 0)
                down(GROUPS - 1, 2, 0)
                pe.wait_ge(m2_evac.sem, m2_evac.at(l, 24 * GROUPS))
                norm_sums(1, 1, 2)
                norm_sums(1, 2, 4)

            pe.wait_ge(h_ready.sem, h_ready.at(DEPTH - 1, 48))
            pe.wait_ge(xs_ready.sem, xs_ready.at(DEPTH - 1, 48))
            for t in range(TT):
                if t >= 2:
                    pe.wait_ge(y_placed.sem, t - 1)
                for j in range(KT):
                    mm = pe.transpose(PSF[:, (t % 2) * 1024 + j * 128:(t % 2) * 1024 + (j + 1) * 128],
                                      XT[:, j, t * 128:(t + 1) * 128], IDENT[:])
                mm.then_inc(y_turned.sem, 1)

        @block.scalar
        def _(act):
            A = Chain(act, a_chain, A_STEPS, A_BEFORE)
            S = nc.scalar

            act.wait_ge(row_placed.sem, 1)
            S.activation(CONDS[:], CRAW[:], ACT.Silu).then_inc(silu_done.sem, 1)
            for t in range(TT):
                act.wait_ge(x_turned.sem, t + 1)
                for half in range(2):
                    ins = S.activation(XT[:, 4 * half:4 * half + 4, t * 128:(t + 1) * 128],
                                       PS[:, 2 * (t % 2) + half, :].rearrange("p (j n) -> p j n", j=4),
                                       ACT.Copy, scale=ALPHA)
                ins.then_inc(x_placed.sem, 1)

            def hi_of_h(j, q, scale, bias):
                t0, tn = CHUNKS[q]
                S.activation(HH[:, j, t0:t0 + tn], XT[:, j, t0:t0 + tn], ACT.Identity, scale=scale, bias=bias)\
                    .then_inc(hh_ready.sem, 1)

            act.wait_ge(const_done.sem, 1)
            act.wait_ge(x_placed.sem, TT)
            for q in range(3):
                v = COND[q]
                for j in range(KT):
                    hi_of_h(j, q, AD0[:, 0, 8 + j, v:v + 1], AD0[:, 0, j, v:v + 1])

            def gain(l, n, j, t0, tn):
                x, at = XT[:, j, t0:t0 + tn], 16 * (n // 24) + j
                act.wait_ge(hh_ready.sem, hh_ready.at(l, n + 1))
                S.activation(x, x, ACT.Identity, scale=LNV[:, at:at + 1], bias=LNV[:, at + 8:at + 9])\
                 .then_inc(xs_ready.sem, 1)

            def norm(l, which):
                for q, (t0, tn) in enumerate(CHUNKS):
                    act.wait_ge(var_ready.sem, var_ready.at(l, 3 * which + q + 1))
                    S.activation(MR[:, 1, t0:t0 + tn], MR[:, 1, t0:t0 + tn], ACT.Sqrt).then_inc(sd_ready.sem, 1)
                for q, (t0, tn) in enumerate(CHUNKS):
                    v = COND[q]
                    for j in range(KT):
                        n = 8 * (3 * which + q) + j
                        x = XT[:, j, t0:t0 + tn]
                        scale, bias = HSB[:, 0, j, v:v + 1], HSB[:, 1, j, v:v + 1]
                        act.wait_ge(xn_ready.sem, xn_ready.at(l, n + 1))
                        S.activation(HH[:, j, t0:t0 + tn], x, ACT.Identity, scale=scale, bias=bias)
                        act.wait_ge(h_ready.sem, h_ready.at(l, n - 1))
                        S.activation(HT[:, n % 2, :tn], x, ACT.Identity, scale=scale, bias=bias)\
                         .then_inc(hh_ready.sem, 1)
                        if which == 0:
                            gain(l, n, j, t0, tn)
                if which:
                    for q, (t0, tn) in enumerate(CHUNKS):
                        for j in range(KT):
                            gain(l, 8 * (3 + q) + j, j, t0, tn)

            with act.Fori(0, DEPTH) as l:
                A.layer(l)
                def conv_store(u):
                    kind, ct, q = UNITS[u]
                    t0, tn = CHUNKS[q]
                    act.wait_ge(conv_done.sem, conv_done.at(l, u + 1))
                    if kind == "hyena":
                        for n in range(2):
                            act.dma_start(hy_d[n, ct, :, t0:t0 + tn], CACC[:, n, :tn]).then_inc(conv_stored.sem, 16)
                    else:
                        act.dma_start(cf_d[ct, :, t0:t0 + tn], CACC[:, 0, :tn]).then_inc(conv_stored.sem, 16)

                def conv_load(u, n):
                    kind, ct, q = UNITS[u]
                    t0, tn = CHUNKS[q]
                    halo = 1 if kind == "hyena" else 15
                    lo = t0 - (halo if q == 1 else 0)
                    hi = t0 + tn + (halo if q == 0 else 0)
                    at = lo - (t0 - halo)
                    done = 3 * n
                    for p in range(2):
                        act.wait_ge(z_stored[p].sem, z_stored[p].at(l, 16 * ((done + 1 - p) // 2)))
                    act.wait_ge(conv_done.sem, conv_done.at(l, u))
                    tiles = (ct, 2 + ct, 4 + ct) if kind == "hyena" else (6 + ct, 8 + ct)
                    dst = HYIN if kind == "hyena" else CFIN
                    for x, tile in enumerate(tiles):
                        act.dma_start(dst[:, x, at:at + hi - lo], z_d[tile, :, lo:hi]).then_inc(conv_in.sem, 16)

                act.wait_ge(h_ready.sem, h_ready.at(l, 0))
                for n in range(ZT):
                    for q, (t0, tn) in enumerate(CHUNKS):
                        u = 3 * n + q
                        if q < 2:
                            act.wait_ge(z_psum.sem, z_psum.at(l, 2 * n + q + 1))
                        else:
                            act.wait_ge(blk_used.sem, blk_used.at(l, n + 1))
                        act.wait_ge(z_stored[u % 2].sem, z_stored[u % 2].at(l, 16 * (u // 2)))
                        S.activation(ZST[:, u % 2, :tn], PS[:, 3 * (n % 2) + q, :tn], ACT.Copy).then_inc(z_evac.sem, 1)
                        act.wait_ge(z_evac.sem, z_evac.at(l, u + 1))
                        act.dma_start(z_d[n, :, t0:t0 + tn], ZST[:, u % 2, :tn]).then_inc(z_stored[u % 2].sem, 16)
                    if n in UNIT_AT:
                        u = UNIT_AT.index(n)
                        if u:
                            conv_store(u - 1)
                        conv_load(u, n)
                        if UNITS[u][0] == "conformer":
                            t0, tn = CHUNKS[UNITS[u][2]]
                            act.wait_ge(conv_in.sem, conv_in.at(l, 6 * 48 + (u - 5) * 32))
                            act.wait_ge(pads_ready.sem, pads_ready.at(l, u - 5))
                            S.activation(CFIN[:, 1, :tn + 30], CFIN[:, 1, :tn + 30], ACT.Sigmoid)\
                             .then_inc(glu_done.sem, 1)
                conv_store(11)

                act.wait_ge(blk_used.sem, blk_used.at(l, B_FWD))
                act.wait_ge(conv_stored.sem, conv_stored.at(l, 288))
                for dst, src in ((HW1[0:33, 0], hf_w1[l]), (HW1[0:33, 1], hf_w1[l]), (HW2[0:64, 0], hf_w2[l]),
                                 (HW2[0:64, 1], hf_w2[l]), (HW3[0:64, :], hf_w3[l]),
                                 (FEAT[0:33, :], feats_d)):
                    act.dma_start(dst, src).then_inc(hf_in.sem, 16)
                for ct in range(2):
                    act.dma_start(UIN[:, ct, :], hy_d[0, ct]).then_inc(u_in.sem, 16)
                for n, (src, dst) in enumerate(((ARG, HID1), (ARG, HID2))):
                    act.wait_ge(hf_arg.sem, hf_arg.at(l, n + 1))
                    S.activation(dst[0:64, :], src[0:64, :], ACT.Sin).then_inc(hf_sin.sem, 1)
                for t in range(TT):
                    if t == 0:
                        for t2 in range(2):
                            act.dma_start(DEC[:, t2, :], decay_d[t2 * 128:(t2 + 1) * 128]).then_inc(dec_in[t2].sem, 16)
                    act.wait_ge(m_sum.sem, m_sum.at(l, t + 1))
                    if t + 2 < TT:
                        act.dma_start(DEC[:, t % 2, :], decay_d[(t + 2) * 128:(t + 3) * 128])\
                           .then_inc(dec_in[t % 2].sem, 16)
                    S.activation(MH[:, t, 0:768].rearrange("p (a n) -> p a n", a=3)[:, 0:3:2, :], FPM[:], ACT.Copy)\
                     .then_inc(m_hi.sem, 1)
                    act.wait_ge(u_psum.sem, u_psum.at(l, t + 1))
                    S.activation(MH[:, t, 256:512], PS[:, 2 + t % 2, 0:256], ACT.Copy).then_inc(u_hi.sem, 1)
                for j in range(TT):
                    b0 = 2 * (j % 2)
                    if j < ST:
                        act.wait_ge(blk_used.sem, blk_used.at(l, B_FWD + 2 * j + 2))
                    elif j == ST:
                        act.wait_ge(dft_psum.sem, dft_psum.at(l, 1))
                    else:
                        act.wait_ge(blk_used.sem, blk_used.at(l, B_INV))
                    if j:
                        act.wait_ge(f_sum.sem, f_sum.at(l, j))
                    S.activation(GS[:, 0, :], PS[:, b0, 0:256], ACT.Copy, scale=WF[:, j:j + 1])
                    S.activation(GS[:, 1, :], PS[:, b0 + 1, 256:512], ACT.Copy, scale=WF[:, j:j + 1])\
                     .then_inc(g_scaled.sem, 1)
                    act.wait_ge(f_sum.sem, f_sum.at(l, j + 1))
                    S.activation(FH[:, j] if j < ST else FPH[:, j - ST], YF[:], ACT.Copy).then_inc(f_hi.sem, 1)
                n = 0
                for ct in range(2):
                    for q, (t0, tn) in enumerate(CHUNKS):
                        act.wait_ge(blk_used.sem, blk_used.at(l, B_OUT))
                        act.wait_ge(old_read.sem, old_read.at(l, n))
                        for x in range(2):
                            act.dma_start(OLD[:, x, :tn], hy_d[x, ct, :, t0:t0 + tn]).then_inc(old_in.sem, 16)
                        act.wait_ge(hy_done.sem, hy_done.at(l, n + 1))
                        act.dma_start(y_d[ct, :, t0:t0 + tn], OY[:, :tn]).then_inc(hy_stored.sem, 16)
                        n += 1

                act.wait_ge(lam_ready.sem, lam_ready.at(l, 1))
                S.activation(LAMS[:, 2:4], LAMS[:, 0:2], ACT.Exp).then_inc(lam_exp.sem, 1)
                def split_inputs(h):
                    act.wait_ge(prep_turned.sem, prep_turned.at(l, 1) + h)
                    act.wait_ge(kv_stored.sem, kv_stored.at(l, 0) + h * 32)
                    S.activation(KR[:, 0:PAST], PS[:, 0, 0:PAST], ACT.Copy).then_inc(kc_placed.sem, 1)
                    S.activation(KO[:].rearrange("p t n -> p (t n)"), PS[:, 0, 256:512], ACT.Copy)
                    S.activation(VO[:].rearrange("p t n -> p (t n)"), PSF[:, 512 + 1024:512 + 1280], ACT.Copy)\
                     .then_inc(kv_copied.sem, 1)
                    S.activation(V2[:, 0:2, 0:128], CKV[:, 1], ACT.Copy)
                    S.activation(V2[:, 2:TT + 2, 0:128], PSF[:, 512:512 + T].rearrange("p (t n) -> p t n", t=TT),
                                 ACT.Copy).then_inc(v_hi.sem, 1)
                    act.wait_ge(rope_done.sem, rope_done.at(l, 2) + h * 2)
                    act.wait_ge(kc_placed.sem, kc_placed.at(l, 1) + h)
                    for src, dst, scale, flip in ((KR, KH, 1.0, False), (KR, KH, 1.0, True), (QR, QQ, SCALE, False)):
                        for m in range(2):
                            own = slice(64 * m, 64 * m + 64)
                            to = slice(64 - 64 * m, 128 - 64 * m) if flip else own
                            S.activation(dst[to, m, :], src[own, :], ACT.Copy, scale=scale).then_inc(qk_hi.sem, 1)
                    act.wait_ge(kv_copied.sem, kv_copied.at(l, 1) + h)
                    for dst, src in ((new_k, KO), (new_v, VO)):
                        act.dma_start(dst[0, l].rearrange("(t p) m d -> p t (m d)", p=128)
                                      [:, :, h * 128:h * 128 + 128] if isinstance(h, int) else
                                      dst[0, l].rearrange("(t p) m d -> p t (m d)", p=128)[:, :, bass.ts(h, 128)],
                                      src[:]).then_inc(kv_stored.sem, 16)

                def head(h, last):
                    def exps(t, m):
                        k0, kn = ITEMS[t]
                        act.wait_ge(smax.sem, smax.at(l, 2 * t + m + 1) + h * 2 * TT)
                        if t > 1:
                            act.wait_ge(mixed.sem, mixed.at(l, t - 1) + h * TT)
                        S.activation(PB[:, t % 2, m, :kn], PSF[:, 1536 * m:1536 * m + kn], ACT.Exp,
                                     bias=STAT[:, t % 4, m:m + 1],
                                     accum_out=STAT[:, t % 4, 2 + m:3 + m]).then_inc(probs.sem, 1)

                    def hi_of_round(t, r):
                        g0, gn = rounds(t)[r]
                        act.wait_ge(at_psum.sem, at_psum.at(l, first_round(t) + r + 1) + h * ROUNDS)
                        if t > 1 and r == 0:
                            act.wait_ge(pv_psum.sem, pv_psum.at(l, t - 1) + h * TT)
                        S.activation(ATH[:, t % 2, g0 * 128:(g0 + gn) * 128], PS[:, 6 + r % 2, 0:gn * 128],
                                     ACT.Copy).then_inc(at_hi.sem, 1)

                    def part_of_output(t):
                        act.wait_ge(pv_psum.sem, pv_psum.at(l, t + 1) + h * TT)
                        if t:
                            act.wait_ge(o_ready.sem, o_ready.at(l, t) + h * TT)
                        S.activation(O2[:], PS[:, 7, 128:256], ACT.Copy, scale=STAT[:, t % 4, 4:5])\
                         .then_inc(o_part.sem, 1)

                    def square(t):
                        act.wait_ge(o_ready.sem, o_ready.at(l, t + 1) + h * TT)
                        ins = S.activation(SQJ[:], OB[:, t, :], ACT.Square, accum_out=SSQ[:, t:t + 1])
                        if t < TT - 1:
                            A.link(ins)
                        else:
                            ins.then_inc(ssq_done.sem, 1)

                    for t in range(2):
                        for m in range(2):
                            exps(t, m)
                    for t in range(TT):
                        for r in range(len(rounds(t))):
                            hi_of_round(t, r)
                        if t + 2 < TT:
                            exps(t + 2, 0)
                            exps(t + 2, 1)
                        if t:
                            part_of_output(t - 1)
                        if t > 1:
                            square(t - 2)
                    part_of_output(TT - 1)
                    square(TT - 2)
                    square(TT - 1)
                    if not last:
                        split_inputs(h + 1)
                    act.wait_ge(ssq_done.sem, ssq_done.at(l, 1) + h)
                    S.activation(RRS[:], SSQ[:], ACT.Sqrt, scale=1 / 128, bias=EPSC[:, 0:1]).then_inc(sd_head.sem, 1)
                    act.wait_ge(o_turned.sem, o_turned.at(l, 1) + h)
                    act.wait_ge(yat_stored.sem, yat_stored.at(l, 0) + h * 16)
                    S.activation(OT[:], PSF[:, 2048:2048 + T], ACT.Copy, scale=VEC[:, V_SUB:V_SUB + 1])\
                     .then_inc(o_placed.sem, 1)
                    act.wait_ge(o_placed.sem, o_placed.at(l, 1) + h)
                    act.dma_start(y_d[h + 4], OT[:]).then_inc(yat_stored.sem, 16)

                split_inputs(0)
                with act.Fori(0, HEADS - 1) as h:
                    A.loop(h, TT - 1, HEADS - 1)
                    head(h, False)
                A.end_loop()
                head(HEADS - 1, True)

                n = 0
                for q, (t0, tn) in enumerate(CHUNKS):
                    act.wait_ge(cf_in.sem, cf_in.at(l, 32 * (q + 1)))
                    if q:
                        act.wait_ge(cf_norm.sem, cf_norm.at(l, q))
                    S.activation(CFS[:, :, :tn], CFU[:, :, :tn], ACT.Square).then_inc(cf_sq.sem, 1)
                    for j in (0, 1, 4, 5, 6, 7):
                        act.wait_ge(y_in[n % 2].sem, y_in[n % 2].at(l, 16 * (n // 2 + 1)))
                        S.activation(HH[:, j, t0:t0 + tn], YIN[:, n % 2, :tn], ACT.Copy).then_inc(y_hi.sem, 1)
                        n += 1
                    act.wait_ge(cf_var.sem, cf_var.at(l, q + 1))
                    S.activation(RS[:, :tn], RS[:, :tn], ACT.Sqrt, bias=EPSC[:, 0:1]).then_inc(cf_sd.sem, 1)
                    act.wait_ge(cf_norm.sem, cf_norm.at(l, q + 1))
                    for ct in range(2):
                        ins = S.activation(CFY[:, ct, :tn], CFY[:, ct, :tn], ACT.Silu,
                                           scale=VEC[:, V_CFG + ct:V_CFG + ct + 1],
                                           bias=VEC[:, V_CFBB + ct:V_CFBB + ct + 1])
                    ins.then_inc(cf_silu.sem, 1)
                    act.wait_ge(cf_silu.sem, cf_silu.at(l, q + 1))
                    for ct in range(2):
                        S.activation(HH[:, 2 + ct, t0:t0 + tn], CFY[:, ct, :tn], ACT.Copy).then_inc(y_hi.sem, 1)

                def squares(which, buf):
                    for n in range(24):
                        q, j = (n % 3, n // 3) if which == 0 else (n // 8, n % 8)
                        t0, tn = CHUNKS[q]
                        if which == 0:
                            act.wait_ge(o_evac.sem, o_evac.at(l, n + 1))
                        else:
                            act.wait_ge(m2_evac.sem, m2_evac.at(l, 24 * (GROUPS - 1) + n + 1))
                        act.wait_ge(sq_added.sem, sq_added.at(l, 24 * which + n - 1))
                        S.activation(buf[:, n % 2, :tn], XT[:, j, t0:t0 + tn], ACT.Square).then_inc(sq_ready.sem, 1)

                squares(0, SQO)
                norm(l, 0)

                def hidden(g0, q, i):
                    t0, tn = CHUNKS[q]
                    for e in range(2):
                        u = 2 * (3 * g0 + q) + e
                        if q < 2:
                            act.wait_ge(m1_psum.sem, m1_psum.at(l, 4 * g0 + 2 * q + e + 1) + i * 4)
                        else:
                            act.wait_ge(blk_used.sem, blk_used.at(l, B_MLP + 4 * g0 + e + 1) + i * 4)
                        act.wait_ge(hid_ready.sem, hid_ready.at(l, u - 1) + i * 6)
                        S.activation(RB[:, e, :tn], PS[:, e, :tn], ACT.Relu).then_inc(relu_done.sem, 1)
                        act.wait_ge(relu_done.sem, relu_done.at(l, u + 1) + i * 6)
                        if q == 0:
                            act.wait_ge(m2_psum.sem, m2_psum.at(l, 23 * g0 - 15) + i * 23)
                        elif q == 1:
                            act.wait_ge(m2_psum.sem, m2_psum.at(l, 23 * g0 - 7) + i * 23)
                        else:
                            act.wait_ge(blk_used.sem, blk_used.at(l, B_MLP + 4 * g0) + i * 4)
                        S.activation(hidden_hi(q)[:, e, :tn], RB[:, e, :tn], ACT.Square).then_inc(hid_hi.sem, 1)

                act.wait_ge(kv_stored.sem, kv_stored.at(l, HEADS * 32))
                act.wait_ge(h_ready.sem, h_ready.at(l, 24))
                with act.Fori(0, GROUPS) as g:
                    for q in range(3):
                        hidden(0, q, g)
                act.wait_ge(hid_ready.sem, hid_ready.at(l, 6 * GROUPS))
                squares(1, SQM)
                norm(l, 1)
                A.end_layer()

            for t in range(TT):
                act.wait_ge(y_turned.sem, t + 1)
                if t >= 2:
                    act.wait_ge(y_stored[t % 2].sem, 16 * (t // 2))
                for half in range(2):
                    ins = S.activation(XIN[:, t % 2, 512 * half:512 * half + 512], PS[:, 2 * (t % 2) + half, :],
                                       ACT.Copy, scale=1 / ALPHA)
                ins.then_inc(y_placed.sem, 1)
                act.wait_ge(y_placed.sem, t + 1)
                dst = y_sample[0, t * 128:(t + 1) * 128, :] if t < ST else \
                    y_prompt[0, (t - ST) * 128:(t - ST + 1) * 128, :]
                act.dma_start(dst, XIN[:, t % 2]).then_inc(y_stored[t % 2].sem, 16)
            for p in range(2):
                act.wait_ge(y_stored[p].sem, 16 * TT // 2)
            act.wait_ge(kv_stored.sem, kv_stored.at(DEPTH - 1, HEADS * 32))

        @block.vector
        def _(dve):
            V = nc.vector
            C = Chain(dve, v_chain, V_STEPS, V_BEFORE)

            V.memset(ONES[:], 1 / 1024)
            V.memset(EPSC[:], EPS)
            C.link(V.memset(AD0[:], 0.0))
            dve.wait_ge(row_turned.sem, 1)
            V.tensor_copy(CRAW[:], PS[:, 6, 0:16])
            V.tensor_copy(SWAP[:], SWAPF[:])
            V.tensor_copy(B0[:], PS[:, 6, 16:48]).then_inc(row_placed.sem, 1)
            dve.wait_ge(row_placed.sem, 1)
            dve.wait_ge(ada_used.sem, 34)
            for v in range(2):
                C.link(V.tensor_tensor(AD0[:, 0:DEPTH, :, v], PS[:, 7, 0:64].rearrange("p (l t v) -> p l t v", l=2, v=2)
                                       [:, :, :, v], B0[:].rearrange("p (l t) -> p l t", l=2), ALU.add))
            C.link(V.tensor_scalar(AD0[:, 0:DEPTH, 8:16, :], AD0[:, 0:DEPTH, 8:16, :], 1.0, 1 / ALPHA,
                                   ALU.add, ALU.mult))
            V.memset(MODT[:, 0, 0:2], 0.0).then_inc(const_done.sem, 1)
            dve.wait_ge(const_done.sem, 1)
            dve.wait_ge(x_placed.sem, TT)

            for q, (t0, tn) in enumerate(CHUNKS):
                v = COND[q]
                for j in range(KT):
                    n = 8 * q + j
                    C.link(V.tensor_scalar(MODT[:, n % 2, :tn], XT[:, j, t0:t0 + tn], AD0[:, 0, 8 + j, v:v + 1],
                                           AD0[:, 0, j, v:v + 1], ALU.mult, ALU.add))
                    dve.wait_ge(hh_ready.sem, n + 1)
                    V.tensor_tensor(HL[:, j, t0:t0 + tn], MODT[:, n % 2, :tn], HH[:, j, t0:t0 + tn].bitcast(F32),
                                    ALU.subtract).then_inc(h_ready.sem, 1)
                    if n:
                        dve.wait_ge(h_ready.sem, n)

            def norm(l, which, banks):
                if which:
                    sh, sc = [AD0[:, bass.ds(l + 1, 1), a:a + 8, :].rearrange("p a k v -> p (a k) v") for a in (0, 8)]
                else:
                    sh, sc = ADA[:, A_SH2:A_SH2 + 8, :], ADA[:, A_SC2:A_SC2 + 8, :]
                g, b = [LNV[:, 16 * which + a:16 * which + a + 8].rearrange("p (k a) -> p k a", a=1)
                        .broadcast_to([128, KT, 2]) for a in (0, 8)]
                C.link(V.tensor_tensor(HSB[:, 0], g, sc, ALU.mult))
                C.link(V.tensor_tensor(HSB[:, 1], b, sc, ALU.mult))
                V.tensor_tensor(HSB[:, 1], HSB[:, 1], sh, ALU.add).then_inc(mod_ready.sem, 1)
                for q, (t0, tn) in enumerate(CHUNKS):
                    mu, rs = MR[:, 0, t0:t0 + tn], MR[:, 1, t0:t0 + tn]
                    dve.wait_ge(stats.sem, stats.at(l, 3 * which + q + 1))
                    C.link(V.tensor_copy(mu, PS[:, banks[q], :tn]))
                    C.link(V.tensor_tensor(rs, mu, mu, ALU.mult))
                    V.scalar_tensor_tensor(rs, PS[:, banks[q] + 1, :tn], EPSC[:, 0:1], rs, ALU.add, ALU.subtract)\
                     .then_inc(var_ready.sem, 1)

                def lo(n, j, t0, tn):
                    dve.wait_ge(hh_ready.sem, hh_ready.at(l, n + 1))
                    V.tensor_tensor(HL[:, j, t0:t0 + tn], HT[:, n % 2, :tn], HH[:, j, t0:t0 + tn].bitcast(F32),
                                    ALU.subtract).then_inc(h_ready.sem, 1)

                for q, (t0, tn) in enumerate(CHUNKS):
                    dve.wait_ge(sd_ready.sem, sd_ready.at(l, 3 * which + q + 1))
                    C.link(V.reciprocal(MR[:, 1, t0:t0 + tn], MR[:, 1, t0:t0 + tn]))
                    for j in range(KT):
                        n = 8 * (3 * which + q) + j
                        x = XT[:, j, t0:t0 + tn]
                        if n % 24 > 1:
                            dve.wait_ge(xn_ready.sem, xn_ready.at(l, n - 1))
                        C.link(V.tensor_tensor(LTR[:, n % 2, :tn], x, MR[:, 0, t0:t0 + tn], ALU.subtract))
                        V.tensor_tensor(x, LTR[:, n % 2, :tn], MR[:, 1, t0:t0 + tn], ALU.mult).then_inc(xn_ready.sem, 1)
                        if j:
                            lo(n - 1, j - 1, t0, tn)
                    lo(n, KT - 1, t0, tn)

            with dve.Fori(0, DEPTH) as l:
                C.layer(l)
                dve.wait_ge(vec_turned.sem, vec_turned.at(l, 1))
                C.link(V.tensor_copy(VEC[:], PS[:, 6, 0:ROWS_A + ROWS_B]))
                dve.wait_ge(xs_ready.sem, xs_ready.at(l, 0))
                C.link(V.tensor_scalar(LNV[:], VEC[:, V_LN:V_LN + 32], ALPHA, None, ALU.mult))
                C.link(V.tensor_tensor(LAMR[:, 0:4:2, :], LAMR[:, 0:4:2, :], LAMR[:, 1:4:2, :], ALU.mult))
                V.tensor_reduce(LAMS[:, 0:2], LAMR[:, 0:4:2, :], AX_X, ALU.add).then_inc(lam_ready.sem, 1)

                for u, (kind, ct, q) in enumerate(UNITS):
                    t0, tn = CHUNKS[q]
                    if kind == "hyena":
                        buf, halo, width, parts = HYIN, 1, tn + 2, 3
                    else:
                        buf, halo, width, parts = CFIN, 15, tn + 30, 2
                    pads = []
                    if q != 1:
                        pads.append(buf[:, 0:parts, 0:halo])
                    if q != 0:
                        pads.append(buf[:, 0:parts, halo + tn:width])
                    for n, pad in enumerate(pads):
                        ins = V.memset(pad, 0.0)
                        if n < len(pads) - 1 or kind == "hyena":
                            C.link(ins)
                    if kind == "conformer":
                        ins.then_inc(pads_ready.sem, 1)
                        dve.wait_ge(glu_done.sem, glu_done.at(l, u - 5))
                    else:
                        dve.wait_ge(conv_in.sem, conv_in.at(l, 48 * (u + 1)))
                    stored = 32 * u if u <= 6 else 192 + 16 * (u - 6)
                    dve.wait_ge(conv_stored.sem, conv_stored.at(l, stored))
                    if kind == "hyena":
                        def conv(x, dst):
                            col = 2 * x + ct
                            C.link(V.tensor_scalar(dst, HYIN[:, x, 0:tn], VEC[:, V_HYW + col:V_HYW + col + 1],
                                                   VEC[:, V_HYB + col:V_HYB + col + 1], ALU.mult, ALU.add))
                            for k in (1, 2):
                                w = V_HYW + 6 * k + col
                                C.link(V.scalar_tensor_tensor(dst, HYIN[:, x, k:k + tn], VEC[:, w:w + 1], dst,
                                                              ALU.mult, ALU.add))
                        conv(1, CACC[:, 0, :tn])
                        conv(2, CACC[:, 1, :tn])
                        C.link(V.tensor_tensor(CACC[:, 0, :tn], CACC[:, 0, :tn], CACC[:, 1, :tn], ALU.mult))
                        conv(0, CACC[:, 1, :tn])
                    else:
                        C.link(V.tensor_tensor(CFIN[:, 0, :width], CFIN[:, 0, :width], CFIN[:, 1, :width], ALU.mult))
                        dst = CACC[:, 0, :tn]
                        C.link(V.tensor_scalar(dst, CFIN[:, 0, 0:tn], VEC[:, V_CFW + ct:V_CFW + ct + 1],
                                               VEC[:, V_CFB + ct:V_CFB + ct + 1], ALU.mult, ALU.add))
                        for k in range(1, 31):
                            w = V_CFW + 2 * k + ct
                            C.link(V.scalar_tensor_tensor(dst, CFIN[:, 0, k:k + tn], VEC[:, w:w + 1], dst,
                                                          ALU.mult, ALU.add))
                    V.memset(STAT[:, 0, 7:8], 0.0).then_inc(conv_done.sem, 1)
                    dve.wait_ge(conv_done.sem, conv_done.at(l, u + 1))

                dve.wait_ge(ada_used.sem, ada_used.at(l, 32))
                for v in range(2):
                    C.link(V.tensor_tensor(ADA[:, :, v], PS[:, 7, 0:64].rearrange("p (t v) -> p t v", v=2)[:, :, v],
                                           VEC[:, V_BADA:V_BADA + 32], ALU.add))
                C.link(V.tensor_scalar(ADA[:, A_SC2:A_SC2 + 8, :], ADA[:, A_SC2:A_SC2 + 8, :], 1.0, 1 / ALPHA,
                                       ALU.add, ALU.mult))

                for n in range(2):
                    for q, (t0, tn) in enumerate(CHUNKS):
                        dve.wait_ge(hf_psum.sem, hf_psum.at(l, 3 * n + q + 1))
                        if n:
                            dve.wait_ge(hf_sin.sem, hf_sin.at(l, 1))
                        b = (0, 2)[n]
                        C.link(V.tensor_scalar(ARG[0:64, t0:t0 + tn], PS[0:64, 3 * n + q, :tn], HFV[0:64, b:b + 1],
                                               HFV[0:64, 1:2], ALU.add, ALU.mult))
                    C.link(V.tensor_scalar(RND[0:64, :], ARG[0:64, :], 1 / TWO_PI, ROUND, ALU.mult, ALU.add))
                    C.link(V.tensor_scalar(RND[0:64, :], RND[0:64, :], ROUND, -TWO_PI, ALU.subtract, ALU.mult))
                    C.link(V.tensor_tensor(ARG[0:64, :], ARG[0:64, :], RND[0:64, :], ALU.add))
                    V.tensor_scalar(ARG[0:64, :], ARG[0:64, :], PI_BELOW, -PI_BELOW, ALU.min, ALU.max)\
                     .then_inc(hf_arg.sem, 1)
                for t in range(TT):
                    dve.wait_ge(hft_psum.sem, hft_psum.at(l, t + 1))
                    dve.wait_ge(dec_in[t % 2].sem, dec_in[t % 2].at(l, 16 * (t // 2 + 1)))
                    V.tensor_tensor(FB[:], PS[:, t % 2, :], DEC[:, t % 2, :], ALU.mult).then_inc(hft_read.sem, 1)
                    dve.wait_ge(hft_read.sem, hft_read.at(l, t + 1))
                    if t:
                        dve.wait_ge(m_hi.sem, m_hi.at(l, t))
                    C.link(V.tensor_tensor(FPM[:, 0, :], FB[:, 0:256], FB[:, 256:512], ALU.add))
                    V.tensor_tensor(FPM[:, 1, :], FB[:, 0:256], FB[:, 256:512], ALU.subtract).then_inc(m_sum.sem, 1)
                    dve.wait_ge(m_hi.sem, m_hi.at(l, t + 1))
                    V.tensor_tensor(ML[:, t, :].rearrange("p (a n) -> p a n", a=3)[:, 0:3:2, :], FPM[:],
                                    MH[:, t, :].rearrange("p (a n) -> p a n", a=3)[:, 0:3:2, :].bitcast(F32),
                                    ALU.subtract).then_inc(filt_ready.sem, 1)
                    dve.wait_ge(filt_ready.sem, filt_ready.at(l, t + 1))
                    dve.wait_ge(u_hi.sem, u_hi.at(l, t + 1))
                    V.tensor_tensor(ML[:, t, 256:512], PS[:, 2 + t % 2, 0:256], MH[:, t, 256:512].bitcast(F32),
                                    ALU.subtract).then_inc(u_ready.sem, 1)
                for j in range(TT):
                    b0 = 2 * (j % 2)
                    dve.wait_ge(g_scaled.sem, g_scaled.at(l, j + 1))
                    if j:
                        dve.wait_ge(f_hi.sem, f_hi.at(l, j))
                    uc, us = PS[:, b0, 256:512], PS[:, b0 + 1, 0:256]
                    V.tensor_tensor(PR[:, 0, :], uc, GS[:, 0, :], ALU.mult)
                    V.tensor_tensor(PR[:, 1, :], us, GS[:, 0, :], ALU.mult)
                    V.tensor_tensor(PR2[:, 0, :], us, GS[:, 1, :], ALU.mult)
                    C.link(V.tensor_tensor(PR2[:, 1, :], uc, GS[:, 1, :], ALU.mult))
                    C.link(V.tensor_tensor(YF[:, 0, :], PR[:, 0, :], PR2[:, 0, :], ALU.subtract))
                    V.tensor_tensor(YF[:, 1, :], PR[:, 1, :], PR2[:, 1, :], ALU.add).then_inc(f_sum.sem, 1)
                    dve.wait_ge(f_hi.sem, f_hi.at(l, j + 1))
                    fh = FH[:, j] if j < ST else FPH[:, j - ST]
                    fl = FL[:, j] if j < ST else FPL[:, j - ST]
                    V.tensor_tensor(fl, YF[:], fh.bitcast(F32), ALU.subtract).then_inc(f_ready.sem, 1)
                    dve.wait_ge(f_ready.sem, f_ready.at(l, j + 1))
                n = 0
                for ct in range(2):
                    for q, (t0, tn) in enumerate(CHUNKS):
                        dve.wait_ge(old_in.sem, old_in.at(l, 32 * (n + 1)))
                        y = PS[:, 4 + 2 * ct + q, :tn] if q < 2 else PS[:, ct, :tn]
                        dve.wait_ge(hy_stored.sem, hy_stored.at(l, 16 * n))
                        C.link(V.scalar_tensor_tensor(OLD[:, 0, :tn], OLD[:, 0, :tn], VEC[:, V_BIAS + ct:V_BIAS + ct + 1],
                                                      y, ALU.mult, ALU.add))
                        V.tensor_tensor(OY[:, :tn], OLD[:, 0, :tn], OLD[:, 1, :tn], ALU.mult).then_inc(hy_done.sem, 1)
                        dve.wait_ge(hy_done.sem, hy_done.at(l, n + 1))
                        V.memset(STAT[:, 0, 7:8], 0.0).then_inc(old_read.sem, 1)
                        dve.wait_ge(old_read.sem, old_read.at(l, n + 1))
                        n += 1

                dve.wait_ge(at_tab.sem, at_tab.at(l, 16))
                dve.wait_ge(lam_exp.sem, lam_exp.at(l, 1))
                C.link(V.tensor_tensor(LAMS[:, 0:1], LAMS[:, 3:4], LAMS[:, 2:3], ALU.subtract))
                V.tensor_tensor(LAMC[:, 2:3], LAMS[:, 0:1], LAMC[:, 0:1], ALU.subtract).then_inc(lam_known.sem, 1)
                def rotate(h):
                    for n, src in enumerate((QR[:], KR[:, PAST:PAST + LS])):
                        dve.wait_ge(rope_swapped.sem, rope_swapped.at(l, n + 1) + h * 2)
                        C.link(V.tensor_tensor(RT[:], PSF[:, 512 + 1536 * n:512 + 1536 * n + LS], ROPE[:, 1, :], ALU.mult))
                        dve.wait_ge(rope_cos.sem, rope_cos.at(l, n + 1) + h * 2)
                        V.tensor_tensor(src[:, 0:LS], src[:, 0:LS], RT[:], ALU.add).then_inc(rope_done.sem, 1)
                        dve.wait_ge(rope_done.sem, rope_done.at(l, n + 1) + h * 2)

                def split_inputs(h):
                    dve.wait_ge(v_hi.sem, v_hi.at(l, 1) + h)
                    V.tensor_tensor(V2[:, 0:2, 128:256], CKV[:, 1], V2[:, 0:2, 0:128].bitcast(F32), ALU.subtract)
                    V.tensor_tensor(V2[:, 2:TT + 2, 128:256], PSF[:, 512:512 + T].rearrange("p (t n) -> p t n", t=TT),
                                    V2[:, 2:TT + 2, 0:128].bitcast(F32), ALU.subtract).then_inc(v_split.sem, 1)
                    for m in range(2):
                        own, other = slice(64 * m, 64 * m + 64), slice(64 - 64 * m, 128 - 64 * m)
                        dve.wait_ge(qk_hi.sem, qk_hi.at(l, m + 1) + h * 6)
                        V.tensor_tensor(KL[other, m, :], KR[own, :], KH[own, m, :].bitcast(F32), ALU.subtract)
                    for m in range(2):
                        own, other = slice(64 * m, 64 * m + 64), slice(64 - 64 * m, 128 - 64 * m)
                        dve.wait_ge(qk_hi.sem, qk_hi.at(l, m + 5) + h * 6)
                        ins = V.scalar_tensor_tensor(QQ[other, m, :], QR[own, :], SCALE, QQ[own, m, :].bitcast(F32),
                                                     ALU.mult, ALU.subtract)
                    ins.then_inc(qk_split.sem, 1)

                def head(h, last):
                    dve.wait_ge(lam_known.sem, lam_known.at(l, 1))

                    def maxima(t):
                        k0, kn = ITEMS[t]
                        for m in range(2):
                            dve.wait_ge(s_psum.sem, s_psum.at(l, 2 * t + m + 1) + h * 2 * TT)
                            V.tensor_reduce(STAT[:, t % 4, m:m + 1], PSF[:, 1536 * m:1536 * m + kn],
                                            AX_X, ALU.max, negate=True).then_inc(smax.sem, 1)

                    def mix(t):
                        k0, kn = ITEMS[t]
                        st_ = STAT[:, t % 4, :]
                        dve.wait_ge(probs.sem, probs.at(l, 2 * t + 2) + h * 2 * TT)
                        C.link(V.reciprocal(st_[:, 4:6], st_[:, 2:4]))
                        C.link(V.scalar_tensor_tensor(st_[:, 6:7], st_[:, 2:3], LAMC[:, 2:3], st_[:, 5:6],
                                                      ALU.mult, ALU.mult))
                        if t:
                            dve.wait_ge(at_psum.sem, at_psum.at(l, first_round(t)) + h * ROUNDS)
                        V.scalar_tensor_tensor(AB[:, :kn], PB[:, t % 2, 1, :kn], st_[:, 6:7], PB[:, t % 2, 0, :kn],
                                               ALU.mult, ALU.add).then_inc(mixed.sem, 1)

                    def lo_of_round(t, r):
                        g0, gn = rounds(t)[r]
                        cols = slice(g0 * 128, (g0 + gn) * 128)
                        dve.wait_ge(at_hi.sem, at_hi.at(l, first_round(t) + r + 1) + h * ROUNDS)
                        V.tensor_tensor(ATL[:, t % 2, cols], PS[:, 6 + r % 2, 0:gn * 128],
                                        ATH[:, t % 2, cols].bitcast(F32), ALU.subtract).then_inc(at_lo.sem, 1)

                    def output(t):
                        dve.wait_ge(o_part.sem, o_part.at(l, t + 1) + h * TT)
                        V.scalar_tensor_tensor(OB[:, t, :], PS[:, 7, 0:128], STAT[:, t % 4, 4:5], O2[:],
                                               ALU.mult, ALU.add).then_inc(o_ready.sem, 1)

                    maxima(0)
                    maxima(1)
                    mix(0)
                    for t in range(TT):
                        for r in range(min(2, len(rounds(t)))):
                            lo_of_round(t, r)
                        if t + 2 < TT:
                            maxima(t + 2)
                        if t + 1 < TT:
                            mix(t + 1)
                        if len(rounds(t)) > 2:
                            lo_of_round(t, 2)
                        if t:
                            output(t - 1)
                        if t == ST and not last:
                            rotate(h + 1)
                    output(TT - 1)
                    if not last:
                        split_inputs(h + 1)
                    dve.wait_ge(sd_head.sem, sd_head.at(l, 1) + h)
                    C.link(V.reciprocal(RRS[:], RRS[:]))
                    C.link(V.tensor_scalar(RRS[:], RRS[:], LAMC[:, 1:2], None, ALU.mult))
                    V.tensor_tensor(OB[:], OB[:], RRS[:].rearrange("p (t a) -> p t a", a=1).broadcast_to([128, TT, 128]),
                                    ALU.mult).then_inc(o_normed.sem, 1)
                    dve.wait_ge(o_normed.sem, o_normed.at(l, 1) + h)

                rotate(0)
                split_inputs(0)
                with dve.Fori(0, HEADS - 1) as h:
                    C.loop(h, V_HEAD, HEADS - 1)
                    head(h, False)
                C.end_loop()
                head(HEADS - 1, True)

                n = 0
                for q, (t0, tn) in enumerate(CHUNKS):
                    for j in (0, 1, 4, 5, 6, 7):
                        dve.wait_ge(y_hi.sem, y_hi.at(l, 8 * q + n % 6 + 1))
                        V.tensor_tensor(HL[:, j, t0:t0 + tn], YIN[:, n % 2, :tn], HH[:, j, t0:t0 + tn].bitcast(F32),
                                        ALU.subtract).then_inc(y_lo.sem, 1)
                        n += 1
                    dve.wait_ge(cf_stats.sem, cf_stats.at(l, q + 1))
                    C.link(V.tensor_scalar(MU[:, :tn], PS[:, 6, :tn], 4.0, None, ALU.mult))
                    C.link(V.tensor_tensor(LT[:, :tn], MU[:, :tn], MU[:, :tn], ALU.mult))
                    V.scalar_tensor_tensor(RS[:, :tn], PS[:, 7, :tn], 4.0, LT[:, :tn], ALU.mult, ALU.subtract)\
                     .then_inc(cf_var.sem, 1)
                    dve.wait_ge(cf_sd.sem, cf_sd.at(l, q + 1))
                    C.link(V.reciprocal(RS[:, :tn], RS[:, :tn]))
                    for ct in range(2):
                        C.link(V.tensor_tensor(LT[:, :tn], CFU[:, ct, :tn], MU[:, :tn], ALU.subtract))
                        ins = V.tensor_tensor(CFY[:, ct, :tn], LT[:, :tn], RS[:, :tn], ALU.mult)
                        if ct == 0:
                            C.link(ins)
                    ins.then_inc(cf_norm.sem, 1)
                    for ct in range(2):
                        dve.wait_ge(y_hi.sem, y_hi.at(l, 8 * q + 7 + ct))
                        V.tensor_tensor(HL[:, 2 + ct, t0:t0 + tn], CFY[:, ct, :tn],
                                        HH[:, 2 + ct, t0:t0 + tn].bitcast(F32), ALU.subtract).then_inc(y_lo.sem, 1)

                def add_sums(n, j, q):
                    t0, tn = CHUNKS[q]
                    for x in range(2):
                        if x:
                            dve.wait_ge(sq_ready.sem, sq_ready.at(l, n + 1))
                        src = SQO[:, n % 2, :tn] if x else XT[:, j, t0:t0 + tn]
                        dst = ACC1[:, x, t0:t0 + tn]
                        ins = V.tensor_copy(dst, src) if j == 0 else V.tensor_tensor(dst, dst, src, ALU.add)
                        if x:
                            ins.then_inc(sq_added.sem, 1)
                            dve.wait_ge(sq_added.sem, sq_added.at(l, n + 1))
                        else:
                            C.link(ins)
                    if j == KT - 1:
                        V.memset(STAT[:, 0, 7:8], 0.0).then_inc(acc_ready.sem, 1)
                        dve.wait_ge(acc_ready.sem, acc_ready.at(l, q + 1))

                for n in range(24):
                    q, j = n % 3, n // 3
                    t0, tn = CHUNKS[q]
                    if q < 2:
                        dve.wait_ge(o_psum.sem, o_psum.at(l, 2 * j + q + 1))
                    else:
                        dve.wait_ge(blk_used.sem, blk_used.at(l, B_OUT + j + 1))
                    x = XT[:, j, t0:t0 + tn]
                    V.scalar_tensor_tensor(x, PS[:, 3 * (j % 2) + q, :tn], ADA[:, A_G1 + j, COND[q]:COND[q] + 1], x,
                                           ALU.mult, ALU.add).then_inc(o_evac.sem, 1)
                    dve.wait_ge(o_evac.sem, o_evac.at(l, n + 1))
                    add_sums(n, j, q)
                norm(l, 0, (6, 0, 2))

                def hidden(g, q):
                    t0, tn = CHUNKS[q]
                    for e in range(2):
                        u = 2 * q + e
                        dve.wait_ge(relu_done.sem, relu_done.at(l, u + 1) + g * 6)
                        V.tensor_tensor(SB2[:, e, :tn], RB[:, e, :tn], RB[:, e, :tn], ALU.mult).then_inc(sq_kept.sem, 1)
                        dve.wait_ge(sq_kept.sem, sq_kept.at(l, u + 1) + g * 6)
                        dve.wait_ge(hid_hi.sem, hid_hi.at(l, u + 1) + g * 6)
                        V.tensor_tensor(hidden_lo(q)[:, e, :tn], SB2[:, e, :tn], hidden_hi(q)[:, e, :tn].bitcast(F32),
                                        ALU.subtract).then_inc(hid_ready.sem, 1)

                def down(g, q, back, sums=False):
                    t0, tn = CHUNKS[q]
                    for j in range(KT):
                        m = 8 * (q - 3 * back) + j
                        if q == 2 and j == KT - 1:
                            dve.wait_ge(blk_used.sem, blk_used.at(l, B_MLP + 4 * (1 - back)) + g * 4)
                        else:
                            dve.wait_ge(m2_psum.sem, m2_psum.at(l, 8 * q + j + 1 - 23 * back) + g * 23)
                        x = XT[:, j, t0:t0 + tn]
                        V.scalar_tensor_tensor(x, PS[:, 2 + m % 6, :tn], ADA[:, A_G2 + j, COND[q]:COND[q] + 1], x,
                                               ALU.mult, ALU.add).then_inc(m2_evac.sem, 1)
                        if sums:
                            dve.wait_ge(m2_evac.sem, m2_evac.at(l, 24 * g + 8 * q + j + 1))
                            dst = ACC2[:, 0, t0:t0 + tn]
                            ins = V.tensor_copy(dst, x) if j == 0 else V.tensor_tensor(dst, dst, x, ALU.add)
                            if j < KT - 1:
                                C.link(ins)
                            else:
                                ins.then_inc(acc_ready.sem, 1)

                def group(g, first=False):
                    hidden(g, 0)
                    if not first:
                        down(g, 2, 1)
                    hidden(g, 1)
                    down(g, 0, 0)
                    hidden(g, 2)
                    down(g, 1, 0)

                group(0, True)
                with dve.Fori(1, GROUPS - 1) as g:
                    group(g)
                g = GROUPS - 1
                hidden(g, 0)
                down(g, 2, 1)
                hidden(g, 1)
                down(g, 0, 0, True)
                hidden(g, 2)
                down(g, 1, 0, True)
                down(g, 2, 0, True)
                norm(l, 1, (0, 2, 4))
                C.end_layer()


def bass_hyena_conformer_diffattn_dit(nc, ins, consts, outs):
    program(nc, ins, consts, outs)


_INS = ['x_prompt', 'x_sample', 'cache_k', 'cache_v', 'c', 'c_ctx', 'w_ada', 'b_ada', 'w_in',
        'hy_conv_w', 'hy_conv_b', 'hf_w1', 'hf_b1', 'hf_freq', 'hf_w2', 'hf_b2', 'hf_w3', 'hy_bias',
        'cf_conv_w', 'cf_conv_b', 'cf_ln_g', 'cf_ln_b', 'lam_q1', 'lam_k1', 'lam_q2', 'lam_k2',
        'subln_g', 'w_out', 'ln1_g', 'ln1_b', 'w_mlp1', 'w_mlp2', 'ln2_g', 'ln2_b']
_OUTS = [(1, 256, 1024), (1, 1024, 1024), (1, 2, 256, 8, 64), (1, 2, 256, 4, 128)]


def _constants():
    import numpy as np
    ident = np.eye(128)
    d = np.arange(128)
    partner = np.where(d % 32 < 16, d + 16, d - 16)
    swap = np.zeros((128, 128))
    swap[partner, d] = 1.0
    tok = np.arange(1024)
    f32 = np.float32
    inv = (f32(10000.0) ** (-(np.arange(0, 32, 2, dtype=f32)) / f32(32))).astype(f32)
    pos = np.where(((d // 32) % 2 == 0)[:, None], (tok // 64)[None, :], (tok % 64)[None, :]).astype(f32)
    ang = (pos * inv[d % 16][:, None]).astype(f32).astype(np.float64)
    sign = np.where(d % 32 < 16, -1.0, 1.0)[:, None]
    rope = np.stack([np.cos(ang), sign * np.sin(ang)], 1)
    feats, decay = [], []
    deltas = np.abs(np.linspace(math.log(1e-2) / 0.3, math.log(1e-2) / 1.5, 256))
    for n in (1024, 256):
        t = np.linspace(0.0, 1.0, n)[:, None]
        w = (2.0 * math.pi / n) * np.arange(n)[:, None]
        fr = np.linspace(1e-4, 15, 16)[None, :]
        feats.append(np.concatenate([t, np.cos(fr * w), -np.sin(fr * w)], -1))
        dec = np.exp(-t * deltas[None, :])
        back = dec.copy()
        back[0] = 0.0
        decay.append(np.concatenate([dec, back], 1))

    def dft(n):
        a = 2 * math.pi * ((np.arange(n)[:, None] * np.arange(n)[None, :]) % (2 * n - 1)) / (2 * n - 1)
        return np.stack([np.cos(a), np.sin(a)])

    small = dft(256).reshape(2, 2, 128, 256).transpose(2, 1, 0, 3).reshape(128, 1024)
    weight = np.full((128, 10), 2.0)
    weight[:, :8] /= 2047
    weight[:, 8:] /= 511
    weight[0, 0] /= 2
    weight[0, 8] /= 2
    lam = [0.8 - 0.6 * math.exp(-0.3 * k) for k in range(2)]
    lam = np.broadcast_to(np.array([[v, 1 - v] for v in lam])[:, None, :], (2, 128, 2))
    out = [ident, swap, rope, np.concatenate(feats).T, np.concatenate(decay), dft(1024), small, weight, lam]
    return [np.ascontiguousarray(a, dtype=f32) for a in out]


def kernel(**inputs):
    import numpy as _np
    import concourse.bacc as _bacc
    from concourse import mybir as _mybir
    from concourse.bass_utils import run_bass_kernel_spmd as _run

    nc = _bacc.Bacc("TRN2", target_bir_lowering=False, num_devices=1)
    arrays = {}

    def external(name, a):
        a = _np.ascontiguousarray(a)
        arrays[name] = a
        return nc.dram_tensor(name, a.shape, _mybir.dt.from_np(a.dtype), kind="ExternalInput").ap()

    ins = [external(f"in_{n}_dram", inputs[n]) for n in _INS]
    consts = [external(f"const_{i}_dram", a) for i, a in enumerate(_constants())]
    outs = [nc.dram_tensor(f"out_{i}_dram", s, _mybir.dt.from_np(_np.dtype("float32")), kind="ExternalOutput").ap()
            for i, s in enumerate(_OUTS)]
    bass_hyena_conformer_diffattn_dit(nc, ins, consts, outs)
    r = _run(nc, [arrays], core_ids=[0])
    return tuple(r.results[0][f"out_{i}_dram"] for i in range(len(_OUTS)))
```

```python
import math
from contextlib import ExitStack

import concourse.bass as bass
from concourse import mybir

F32 = mybir.dt.float32
F32R = mybir.dt.float32r
ALU = mybir.AluOpType
ACT = mybir.ActivationFunctionType
AX_X = mybir.AxisListType.X

DEPTH = 2
D = 1024
KT = D // 128
LS, LP = 1024, 256
T = LS + LP
TT = T // 128
ST, PT = LS // 128, LP // 128
PAST = 256
CHUNKS = [(0, 512), (512, 512), (1024, 256)]
COND = [0, 0, 1]
ZT = 22
HEADS = 4
FF_T = 32
GROUPS = FF_T // 2
RING = 6
ALPHA = (2 * DEPTH) ** 0.25
EPS = 1e-5
SCALE = 64 ** -0.5
TWO_PI = 2 * math.pi
ROUND = 1.5 * 2 ** 23
PI_BELOW = 3.1415925

B_IN, B_FWD, B_INV, B_OUT, B_MLP, BLOCKS = 0, 24, 42, 60, 68, 132
LEFT_OUT = {21: 2, 40: 1, 58: 1}
REAL = [b for b in range(BLOCKS) if b not in (22, 23, 41, 59)]
RAW_OF = {b: r for r, b in enumerate(REAL)}

V_BADA, V_LN, V_HYW, V_HYB, V_BIAS, ROWS_A = 0, 32, 64, 82, 88, 90
V_CFW, V_CFB, V_CFG, V_CFBB, V_SUB, ROWS_B = 90, 152, 154, 156, 158, 69
A_G1, A_SH2, A_SC2, A_G2 = 0, 8, 16, 24

KEYS = PAST + T
S_KEYS = PAST + LS
ITEMS = [(0, S_KEYS)] * ST + [(S_KEYS, LP)] * PT

ROUNDS = ST * 3 + PT


def rounds(t):
    nk = ITEMS[t][1] // 128
    return [(g, min(4, nk - g)) for g in range(0, nk, 4)]


def first_round(t):
    return sum(len(rounds(i)) for i in range(t))


HF_LOADS = 2 + 8 * DEPTH

UNITS = [("hyena", c, q) for c in range(2) for q in range(3)] + \
        [("conformer", c, q) for c in range(2) for q in range(3)]
A_BEFORE, A_STEPS = 0, HEADS * (TT - 1)
V_BEFORE, V_STEPS, V_HEAD = 72, 476, 24
UNIT_AT = [5, 5, 6, 7, 7, 8, 9, 11, 13, 14, 16, 18]


class Signal:

    def __init__(self, sem, per_layer, start=0):
        self.sem, self.per_layer, self.start = sem, per_layer, start

    def at(self, l, k):
        return l * self.per_layer + (k + self.start)


class Chain:

    def __init__(self, engine, sem, per_layer, before):
        self.engine, self.sem, self.per_layer, self.before = engine, sem, per_layer, before
        self.n, self.l, self.i, self.per_i, self.trips, self.at_start = 0, None, None, 0, 0, 0

    def link(self, ins):
        self.n += 1
        ins.then_inc(self.sem, 1)
        value = self.n if self.l is None else self.l * self.per_layer + (self.n + self.before)
        if self.i is not None:
            value = value + self.i * self.per_i
        self.engine.wait_ge(self.sem, value)

    def layer(self, l):
        assert self.n == self.before, self.n
        self.l, self.n = l, 0

    def loop(self, i, per_i, trips):
        self.i, self.per_i, self.trips, self.at_start = i, per_i, trips, self.n

    def end_loop(self):
        assert self.n - self.at_start == self.per_i, self.n - self.at_start
        self.n, self.i = self.at_start + self.per_i * self.trips, None

    def end_layer(self):
        assert self.n == self.per_layer, self.n


def program(nc, ins, consts, outs):
    x_prompt, x_sample, cache_k, cache_v, c, c_ctx, w_ada, b_ada, w_in, hy_conv_w, hy_conv_b, \
        hf_w1, hf_b1, hf_freq, hf_w2, hf_b2, hf_w3, hy_bias, cf_conv_w, cf_conv_b, cf_ln_g, \
        cf_ln_b, lam_q1, lam_k1, lam_q2, lam_k2, subln_g, w_out, ln1_g, ln1_b, w_mlp1, w_mlp2, \
        ln2_g, ln2_b = ins
    ident_d, swap_d, rope_d, feats_d, decay_d, dft_d, dftp_d, weight_d, lam_d = consts
    y_prompt, y_sample, new_k, new_v = outs

    z_d = nc.dram_tensor("z_scratch", (ZT, 128, T), F32, kind="Internal").ap()
    hy_d = nc.dram_tensor("hyena_scratch", (2, 2, 128, T), F32, kind="Internal").ap()
    cf_d = nc.dram_tensor("conformer_scratch", (2, 128, T), F32, kind="Internal").ap()
    filt_d = nc.dram_tensor("filter_scratch", (DEPTH, TT, 128, 512), F32, kind="Internal").ap()
    y_d = nc.dram_tensor("mixed_scratch", (KT, 128, T), F32, kind="Internal").ap()

    base = (nc.sbuf_base + 63) // 64 * 64

    def place(name, shape, dtype, offset):
        return nc.alloc_sbuf_tensor_at(name, shape, dtype, offset=offset)

    class Stack:
        def __init__(self, at, end):
            self.at, self.end = at, end

        def take(self, name, shape, dtype=F32):
            n = 4
            for s in shape[1:]:
                n *= s
            t = place(name, shape, dtype, self.at)
            self.at += (n + 31) // 32 * 32
            assert self.at <= self.end, (name, self.at - self.end)
            return t

    XT_O = base
    WS = XT_O + KT * T * 4
    HID_O = WS + 2 * KT * T * 4
    ADW_O = HID_O + 16384
    RING_O = ADW_O + 8192
    RAW_O = RING_O + 2 * RING * 4096
    SMALL_O = RAW_O + 8192
    XT = place("XT", [128, KT, T], F32, XT_O)
    HH = place("HH", [128, KT, T], F32R, WS)
    HL = place("HL", [128, KT, T], F32R, WS + KT * T * 4)
    ADW = place("ADW", [128, 2, 8, 128], F32, ADW_O)
    RH = place("RH", [128, RING, 1024], F32R, RING_O)
    RL = place("RL", [128, RING, 1024], F32R, RING_O + RING * 4096)
    RAW = place("RAW", [128, 2, 1024], F32, RAW_O)

    small = Stack(SMALL_O, nc.sbuf_usable_end)
    IDENT = small.take("IDENT", [128, 128])
    SWAPF = small.take("SWAPF", [128, 128])
    SWAP = small.take("SWAP", [128, 128], F32R)
    ONES = small.take("ONES", [128, 128])
    VEC = small.take("VEC", [128, ROWS_A + ROWS_B])
    LNV = small.take("LNV", [128, 32])
    ADA = small.take("ADA", [128, 32, 2])
    AD0 = small.take("AD0", [128, DEPTH + 1, 16, 2])
    CONDS = small.take("CONDS", [128, 16])
    EPSC = small.take("EPSC", [128, 1])
    ONE = small.take("ONE", [128, 1])
    WF = small.take("WF", [128, TT])
    HFV = small.take("HFV", [128, DEPTH, 4])
    LAMS = small.take("LAMS", [128, 4])
    LAMC = small.take("LAMC", [128, 4])
    STAT = small.take("STAT", [128, 4, 8])
    HB2_O = small.at
    VROW = small.take("VROW", [128, 128])
    VROWB = small.take("VROWB", [128, 128])
    LAMR = small.take("LAMR", [128, 4, 64])
    KO = small.take("KO", [128, 2, 128])
    VO = small.take("VO", [128, 2, 128])

    st = Stack(HID_O, ADW_O)
    XIN = st.take("XIN", [128, 2, 1024])
    CROW = st.take("CROW", [128, 128])
    BROW = st.take("BROW", [128, 128])
    B0 = st.take("B0", [128, 32])
    CRAW = st.take("CRAW", [128, 16])
    MODT = st.take("MODT", [128, 2, 512])
    st = Stack(WS, HID_O)
    FEAT = st.take("FEAT", [128, T])
    HID1 = st.take("HID1", [128, T])
    HID2 = st.take("HID2", [128, T])
    ARG = st.take("ARG", [128, T])
    RND = st.take("RND", [128, T])
    HW1 = st.take("HW1", [128, DEPTH, 2, 64])
    HW2 = st.take("HW2", [128, DEPTH, 2, 64])
    HW3 = st.take("HW3", [128, DEPTH, 512])
    DEC = st.take("DEC", [128, TT, 512])
    FB = st.take("FB", [128, 512])
    FOUT = st.take("FOUT", [128, 4, 2, 256])
    st = Stack(HID_O, ADW_O)
    ZST = st.take("ZST", [128, 2, 512])
    HYIN = place("HYIN", [128, 3, 514], F32, st.at)
    CFIN = place("CFIN", [128, 2, 542], F32, st.at)
    st.at += 6176
    CACC = st.take("CACC", [128, 2, 512])
    st = Stack(WS, RING_O)
    MH = st.take("MH", [128, TT, 768], F32R)
    ML = st.take("ML", [128, TT, 768], F32R)
    FH = st.take("FH", [128, ST, 2, 256], F32R)
    FL = st.take("FL", [128, ST, 2, 256], F32R)
    GS = st.take("GS", [128, 2, 256])
    PR = st.take("PR", [128, 2, 256])
    PR2 = st.take("PR2", [128, 2, 256])
    YF = st.take("YF", [128, 2, 256])
    FPH = place("FPH", [128, PT, 2, 256], F32R, WS)
    FPL = place("FPL", [128, PT, 2, 256], F32R, WS + 4096)
    OLD = place("OLD", [128, 2, 2, T], F32, WS + 8192)
    OY = place("OY", [128, 2, T], F32, WS + TT * 768 * 4)
    st2 = Stack(WS + 2 * TT * 768 * 4, RING_O)
    UIN = st2.take("UIN", [128, 2, T])
    FPM = st2.take("FPM", [128, TT, 2, 256])
    st = Stack(WS + 40960, WS + 2 * TT * 768 * 4)
    CFU = st.take("CFU", [128, 2, T])
    CFS = st.take("CFS", [128, 2, 512])
    MU = st.take("MU", [128, 512])
    RS = st.take("RS", [128, 512])
    LT = st.take("LT", [128, 512])
    st = Stack(WS, SMALL_O)
    KH = st.take("KH", [128, 2, KEYS], F32R)
    KL = st.take("KL", [128, 2, KEYS], F32R)
    QQ = st.take("QQ", [128, 2, T], F32R)
    V2 = st.take("V2", [128, TT + 2, 256], F32R)
    PB = st.take("PB", [128, 2, 2, S_KEYS])
    AB = st.take("AB", [128, S_KEYS])
    ATH = st.take("ATH", [128, 2, S_KEYS], F32R)
    ATL = st.take("ATL", [128, 2, S_KEYS], F32R)
    OB = st.take("OB", [128, TT, 128])
    KR = st.take("KR", [128, KEYS])
    QR = st.take("QR", [128, T])
    VR = place("VR", [128, T], F32, st.at)
    st.at += 5120
    CKV = place("CKV", [128, 2, 2, 128], F32, st.at)
    st.at += 2048
    ROPE = st.take("ROPE", [128, 2, LS])
    O2 = st.take("O2", [128, 128])
    SSQ = st.take("SSQ", [128, TT])
    RRS = st.take("RRS", [128, TT])
    ZH = st.take("ZH", [128, 2, LS], F32R)
    ZL = st.take("ZL", [128, 2, LS], F32R)
    RT = st.take("RT", [128, LS])
    OT = st.take("OT", [128, T])
    SQJ = st.take("SQJ", [128, 128])
    st = Stack(HID_O, RING_O)
    YIN = place("YIN", [128, 4, 512], F32, ADW_O)
    SQO = place("SQO", [128, 2, 512], F32, HID_O)
    st.at = HID_O + 4096
    ACC1 = st.take("ACC1", [128, 2, T])
    MR = place("MR", [128, 2, T], F32, HID_O + 4096)
    HT = place("HT", [128, 2, 512], F32, HID_O)
    HSB = place("HSB", [128, 2, KT, 2], F32, HID_O + 14336)
    HBH = place("HBH", [128, 2, 2, 512], F32R, HID_O)
    HBL = place("HBL", [128, 2, 2, 512], F32R, HID_O + 8192)
    HB2H = place("HB2H", [128, 2, 256], F32R, HB2_O)
    HB2L = place("HB2L", [128, 2, 256], F32R, HB2_O + 2048)
    RB = place("RB", [128, 2, 512], F32, ADW_O)
    SB2 = place("SB2", [128, 2, 512], F32, ADW_O + 4096)
    ACC2 = place("ACC2", [128, 2, T], F32, WS + KT * T * 4)
    SQM = place("SQM", [128, 2, 512], F32, ADW_O)

    def hidden_hi(q):
        return HBH[:, q] if q < 2 else HB2H[:]

    def hidden_lo(q):
        return HBL[:, q] if q < 2 else HB2L[:]

    nc.disable_value_cache = True
    with ExitStack() as ctx:
        PS = ctx.enter_context(nc.psum_tensor("PS", [128, 8, 512], F32))
        PSF = PS[:, :, :].rearrange("p b n -> p (b n)")

        def signal(name, per_layer=0, start=0):
            return Signal(ctx.enter_context(nc.semaphore(name)), per_layer, start)

        raw_in = [signal(f"raw_in{p}", 64 * 16) for p in range(2)]
        hi_split = signal("hi_split", len(REAL))
        blk_ready = signal("blk_ready", BLOCKS, BLOCKS)
        blk_used = signal("blk_used", BLOCKS, RING)
        ada_in = [signal(f"ada_in{p}", 16 * 16, 16 * 16) for p in range(2)]
        ada_used = signal("ada_used", 32, 34)
        const_in = signal("const_in")
        const_done = signal("const_done")
        one_ready = signal("one_ready")
        x_in = [signal(f"x_in{p}") for p in range(2)]
        x_turned = signal("x_turned")
        x_placed = signal("x_placed")
        row_turned = signal("row_turned")
        row_placed = signal("row_placed")
        silu_done = signal("silu_done")
        vec_in = signal("vec_in", 18 * 16)
        vec_turned = signal("vec_turned", 1)
        xn_ready = signal("xn_ready", 48)
        xs_ready = signal("xs_ready", 48, 1)
        hh_ready = signal("hh_ready", 48, 24)
        h_ready = signal("h_ready", 48, 24)
        mod_ready = signal("mod_ready", 2)
        var_ready = signal("var_ready", 6, 6)
        sd_ready = signal("sd_ready", 6)
        acc_ready = signal("acc_ready", 6)
        stats = signal("stats", 6)
        centred = signal("centred", 48)
        z_psum = signal("z_psum", 44)
        z_evac = signal("z_evac", 66, 6)
        z_stored = [signal(f"z_stored{p}", 33 * 16, 16) for p in range(2)]
        conv_in = signal("conv_in", 480)
        conv_done = signal("conv_done", 12, 1)
        conv_stored = signal("conv_stored", 288, 16)
        glu_done = signal("glu_done", 6)
        hf_in = signal("hf_in")
        hf_psum = signal("hf_psum")
        hf_arg = signal("hf_arg")
        hf_sin = signal("hf_sin")
        hft_psum = signal("hft_psum")
        hft_read = signal("hft_read")
        fout_ready = signal("fout_ready")
        fout_stored = [signal(f"fout_stored{p}") for p in range(4)]
        filt_in = [signal(f"filt_in{p}", 16) for p in range(TT // 2)]
        m_hi = signal("m_hi", TT)
        filt_ready = signal("filt_ready", TT)
        u_in = signal("u_in", 32)
        u_psum = signal("u_psum", TT)
        u_hi = signal("u_hi", TT)
        u_ready = signal("u_ready", TT, 2)
        dft_psum = signal("dft_psum", 1)
        g_scaled = signal("g_scaled", TT)
        f_sum = signal("f_sum", TT)
        f_hi = signal("f_hi", TT)
        f_ready = signal("f_ready", TT)
        old_in = signal("old_in", 4 * 16)
        hy_done = signal("hy_done", 6)
        hy_stored = signal("hy_stored", 4 * 16, 16)
        at_tab = signal("at_tab", 16)
        lam_ready = signal("lam_ready", 1)
        lam_known = signal("lam_known", 1)
        head_in = signal("head_in", HEADS * 5 * 16)
        qk_split = signal("qk_split", HEADS, 1)
        kl_split = signal("kl_split", HEADS * 2, 2)
        prep_turned = signal("prep_turned", HEADS)
        kc_placed = signal("kc_placed", HEADS)
        v_hi = signal("v_hi", HEADS)
        v_split = signal("v_split", HEADS)
        rope_hi = signal("rope_hi", HEADS * 2)
        rope_lo = signal("rope_lo", HEADS * 2)
        rope_cos = signal("rope_cos", HEADS * 2)
        rope_swapped = signal("rope_swapped", HEADS * 2, 2)
        rope_done = signal("rope_done", HEADS * 2)
        qk_hi = signal("qk_hi", HEADS * 6)
        s_psum = signal("s_psum", HEADS * TT * 2)
        smax = signal("smax", HEADS * TT * 2)
        probs = signal("probs", HEADS * TT * 2)
        mixed = signal("mixed", HEADS * TT)
        at_psum = signal("at_psum", HEADS * ROUNDS)
        at_hi = signal("at_hi", HEADS * ROUNDS)
        at_lo = signal("at_lo", HEADS * ROUNDS)
        pv_psum = signal("pv_psum", HEADS * TT)
        o_part = signal("o_part", HEADS * TT)
        o_ready = signal("o_ready", HEADS * TT)
        ssq_done = signal("ssq_done", HEADS)
        sd_head = signal("sd_head", HEADS)
        o_normed = signal("o_normed", HEADS)
        o_turned = signal("o_turned", HEADS)
        o_placed = signal("o_placed", HEADS, 1)
        kv_copied = signal("kv_copied", HEADS)
        kv_stored = signal("kv_stored", HEADS * 32, 32)
        yat_stored = signal("yat_stored", HEADS * 16, 16)
        y_in = [signal(f"y_in{p}", 6 * 16) for p in range(4)]
        y_hi = signal("y_hi", 24)
        y_lo = signal("y_lo", 24, 4)
        cf_in = signal("cf_in", 2 * 16)
        cf_sq = signal("cf_sq", 3)
        cf_stats = signal("cf_stats", 3)
        cf_var = signal("cf_var", 3)
        cf_sd = signal("cf_sd", 3)
        cf_norm = signal("cf_norm", 3)
        cf_silu = signal("cf_silu", 3)
        o_psum = signal("o_psum", 16)
        o_evac = signal("o_evac", 24, 6)
        sq_ready = signal("sq_ready", 48)
        sq_added = signal("sq_added", 48, 2)
        m1_psum = signal("m1_psum", GROUPS * 4)
        relu_done = signal("relu_done", GROUPS * 6)
        hid_hi = signal("hid_hi", GROUPS * 6)
        hid_ready = signal("hid_ready", GROUPS * 6, 2)
        m2_psum = signal("m2_psum", GROUPS * 23, 16)
        m2_evac = signal("m2_evac", GROUPS * 24, 6)
        y_turned = signal("y_turned")
        y_placed = signal("y_placed")
        y_stored = [signal(f"y_stored{p}") for p in range(2)]
        pads_ready = signal("pads_ready", 6)
        sq_kept = signal("sq_kept", GROUPS * 6)
        lam_exp = signal("lam_exp", 1)
        v_chain = ctx.enter_context(nc.semaphore("v_chain"))
        a_chain = ctx.enter_context(nc.semaphore("a_chain"))

        block = ctx.enter_context(nc.Block())

        def column_block(w, l, j):
            return w[l].rearrange("(k p) n -> p k n", p=128)[:, :, bass.ts(j, 128)]

        def raw_view(p):
            return RAW[:, p, :].rearrange("p (k n) -> p k n", k=8)

        def dft_columns(part, j):
            return dft_d[part].rearrange("(k p) n -> p k n", p=128)[:, :, j * 128:(j + 1) * 128]

        def dft_rows(part, j):
            return dft_d[part, j * 128:(j + 1) * 128, :]

        @block.sync
        def _(sp):
            def load_block(l, b, i, source, view3):
                r = RAW_OF[b]
                p = r % 2
                if r >= 2:
                    before = REAL[r - 2] + 1
                else:
                    before = REAL[r - 2] + 1 - BLOCKS
                sp.wait_ge(blk_ready.sem, blk_ready.at(l, before) + i * RING)
                sp.dma_start(raw_view(p) if view3 else RAW[:, p, :], source).then_inc(raw_in[p].sem, 16)

            def load_ada(l, a, t):
                sp.wait_ge(ada_used.sem, ada_used.at(l, a - 1))
                sp.dma_start(ADW[:, a % 2], column_block(w_ada, l, t)).then_inc(ada_in[a % 2].sem, 16)

            for n, (dst, src) in enumerate([(IDENT[:], ident_d), (SWAPF[:], swap_d), (WF[:], weight_d),
                                            (CROW[0:8, :], c.rearrange("a (k p) -> (a k) p", p=128)),
                                            (CROW[8:16, :], c_ctx.rearrange("(k p) -> k p", p=128)),
                                            (BROW[0:16, :], b_ada[0, 0:2048].rearrange("(k p) -> k p", p=128)),
                                            (BROW[16:32, :], b_ada[1, 0:2048].rearrange("(k p) -> k p", p=128))]):
                sp.dma_start(dst, src).then_inc(const_in.sem, 16)
            for t in range(TT):
                if t >= 2:
                    sp.wait_ge(x_turned.sem, t - 1)
                src = x_sample[0, t * 128:(t + 1) * 128, :] if t < ST else \
                    x_prompt[0, (t - ST) * 128:(t - ST + 1) * 128, :]
                sp.dma_start(XIN[:, t % 2], src).then_inc(x_in[t % 2].sem, 16)
            for a in range(32):
                sp.wait_ge(ada_used.sem, a + 1)
                sp.dma_start(ADW[:, a % 2], column_block(w_ada, a // 16, a % 16)).then_inc(ada_in[a % 2].sem, 16)

            with sp.Fori(0, DEPTH) as l:
                sp.wait_ge(blk_used.sem, blk_used.at(l, 0))
                rows_a = [(V_BADA, b_ada[l].rearrange("(r p) -> r p", p=128)[16:48]),
                          (V_LN, ln1_g[l].rearrange("(r p) -> r p", p=128)),
                          (V_LN + 8, ln1_b[l].rearrange("(r p) -> r p", p=128)),
                          (V_LN + 16, ln2_g[l].rearrange("(r p) -> r p", p=128)),
                          (V_LN + 24, ln2_b[l].rearrange("(r p) -> r p", p=128)),
                          (V_HYW, hy_conv_w[l].rearrange("k (r p) -> (k r) p", p=128)),
                          (V_HYB, hy_conv_b[l].rearrange("(r p) -> r p", p=128)),
                          (V_BIAS, hy_bias[l].rearrange("(r p) -> r p", p=128))]
                rows_b = [(0, cf_conv_w[l].rearrange("k (r p) -> (k r) p", p=128)),
                          (62, cf_conv_b[l].rearrange("(r p) -> r p", p=128)),
                          (64, cf_ln_g[l].rearrange("(r p) -> r p", p=128)),
                          (66, cf_ln_b[l].rearrange("(r p) -> r p", p=128)),
                          (68, subln_g[l].rearrange("(r p) -> r p", p=128))]
                for dst, rows in ((VROW, rows_a), (VROWB, rows_b)):
                    for r, src in rows:
                        sp.dma_start(dst[r:r + src.shape[0], :], src).then_inc(vec_in.sem, 16)
                for n, v in enumerate((lam_q1, lam_k1, lam_q2, lam_k2)):
                    sp.dma_start(LAMR[:, n, :], v[l].rearrange("(a n) -> a n", a=1).broadcast_to([128, 64]))\
                       .then_inc(vec_in.sem, 16)
                sp.dma_start(LAMC[:, 0:2], lam_d[l]).then_inc(vec_in.sem, 16)

                with sp.Fori(0, 2) as i:
                    for q in range(6):
                        load_block(l, B_IN + q, i, column_block(w_in, l, i * 6 + q), True)
                        if q == 0:
                            sp.wait_ge(h_ready.sem, h_ready.at(l, 0))
                        for e in range(2):
                            a = 2 * q + e
                            sp.wait_ge(ada_used.sem, ada_used.at(l, a - 1) + i * 12)
                            sp.dma_start(ADW[:, a % 2], column_block(w_ada, l, i * 12 + (16 + a)))\
                              .then_inc(ada_in[a % 2].sem, 16)
                for q in range(12, ZT):
                    load_block(l, B_IN + q, 0, column_block(w_in, l, q), True)
                    if q < 16:
                        for e in range(2):
                            load_ada(l, 2 * q + e, 16 + 2 * q + e)
                for j in range(ST):
                    for part in range(2):
                        load_block(l, B_FWD + 2 * j + part, 0, dft_columns(part, j), True)
                load_block(l, B_FWD + 16, 0, dftp_d, False)
                for j in range(ST):
                    for part in range(2):
                        load_block(l, B_INV + 2 * j + part, 0, dft_rows(part, j), False)
                load_block(l, B_INV + 16, 0, dftp_d, False)

                for p in range(2):
                    sp.wait_ge(z_stored[p].sem, z_stored[p].at(l, 33 * 16))
                sp.wait_ge(hy_stored.sem, hy_stored.at(l, 4 * 16))
                sp.dma_start(ROPE[:], rope_d).then_inc(at_tab.sem, 16)
                with sp.Fori(0, HEADS) as h:
                    sp.wait_ge(qk_split.sem, qk_split.at(l, 0) + h)
                    sp.wait_ge(kl_split.sem, kl_split.at(l, 0) + h * 2)
                    sp.dma_start(KR[:, PAST:KEYS], z_d[h + 14]).then_inc(head_in.sem, 16)
                    sp.dma_start(QR[:], z_d[h + 10]).then_inc(head_in.sem, 16)
                    sp.dma_start(VR[:], z_d[h + 18]).then_inc(head_in.sem, 16)
                    sp.dma_start(CKV[:, 0], cache_k[0, l].rearrange("(t p) m d -> p t (m d)", p=128)
                                 [:, :, bass.ts(h, 128)]).then_inc(head_in.sem, 16)
                    sp.dma_start(CKV[:, 1], cache_v[0, l].rearrange("(t p) m d -> p t (m d)", p=128)
                                 [:, :, bass.ts(h, 128)]).then_inc(head_in.sem, 16)
                sp.wait_ge(yat_stored.sem, yat_stored.at(l, HEADS * 16))
                for n in range(24):
                    q, j = n // 8, n % 8
                    t0, tn = CHUNKS[q]
                    sp.wait_ge(y_lo.sem, y_lo.at(l, n - 3))
                    sp.dma_start(YIN[:, n % 4, :tn], y_d[j, :, t0:t0 + tn]).then_inc(y_in[n % 4].sem, 16)
                    if n in (3, 7):
                        load_block(l, B_OUT + n // 4, 0, column_block(w_out, l, n // 4), True)
                for q in range(2, 8):
                    load_block(l, B_OUT + q, 0, column_block(w_out, l, q), True)
                with sp.Fori(0, GROUPS) as g:
                    for e in range(4):
                        b = B_MLP + e
                        p = RAW_OF[b] % 2
                        sp.wait_ge(blk_ready.sem, blk_ready.at(l, b - 1) + g * 4)
                        if e < 2:
                            sp.dma_start(raw_view(p), column_block(w_mlp1, l, g * 2 + e)).then_inc(raw_in[p].sem, 16)
                        else:
                            sp.dma_start(RAW[:, p, :], w_mlp2[l].rearrange("(j p) n -> j p n", p=128)[g * 2 + (e - 2)])\
                              .then_inc(raw_in[p].sem, 16)

        @block.gpsimd
        def _(pool):
            for freed in [blk_ready, blk_used, z_evac, *z_stored, conv_done, conv_stored, var_ready,
                          u_ready, hy_stored, xs_ready, qk_split, kl_split, o_placed, rope_swapped,
                          kv_stored, yat_stored, y_lo, o_evac, sq_added, hid_ready, m2_psum, m2_evac]:
                pool.sem_inc(freed.sem, freed.start)
            pool.sem_inc(ada_used.sem, 2)
            nc.gpsimd.memset(ONE[:], 1.0).then_inc(one_ready.sem, 1)
            pool.wait_ge(one_ready.sem, 1)

            def split(l, b, i, per_i):
                r, s = RAW_OF[b], b % RING
                p = r % 2
                pool.wait_ge(raw_in[p].sem, raw_in[p].at(l, 16 * (r // 2 + 1)) + i * (8 * per_i))
                pool.wait_ge(blk_used.sem, blk_used.at(l, b - RING + 1) + i * per_i)
                nc.gpsimd.tensor_tensor(RH[:, s, :], RAW[:, p, :], ONE[:].broadcast_to([128, 1024]), ALU.mult).then_inc(hi_split.sem, 1)
                pool.wait_ge(hi_split.sem, hi_split.at(l, r + 1) + i * per_i)
                nc.gpsimd.tensor_tensor(RL[:, s, :], RAW[:, p, :], RH[:, s, :].bitcast(F32), ALU.subtract)\
                  .then_inc(blk_ready.sem, 1 + LEFT_OUT.get(b, 0))

            def centre(l, which):
                for q, (t0, tn) in enumerate(CHUNKS):
                    pool.wait_ge(var_ready.sem, var_ready.at(l, 3 * which + q + 1))
                    for j in range(KT):
                        x = XT[:, j, t0:t0 + tn]
                        nc.gpsimd.tensor_tensor(x, x, MR[:, 0, t0:t0 + tn], ALU.subtract).then_inc(centred.sem, 1)

            with pool.Fori(0, DEPTH) as l:
                with pool.Fori(0, 2) as i:
                    for q in range(6):
                        split(l, B_IN + q, i, 6)
                for b in REAL[12:RAW_OF[B_OUT]]:
                    split(l, b, 0, 4)
                with pool.Fori(0, HEADS) as h:
                    for n, src in enumerate((QR[:], KR[:, PAST:PAST + LS])):
                        if n == 0:
                            pool.wait_ge(at_tab.sem, at_tab.at(l, 16))
                            pool.wait_ge(head_in.sem, head_in.at(l, 80) + h * 80)
                        pool.wait_ge(rope_swapped.sem, rope_swapped.at(l, n - 1) + h * 2)
                        nc.gpsimd.tensor_tensor(ZH[:, n], src[:, 0:LS], ONE[:].broadcast_to([128, LS]), ALU.mult)\
                            .then_inc(rope_hi.sem, 1)
                        pool.wait_ge(rope_hi.sem, rope_hi.at(l, n + 1) + h * 2)
                        nc.gpsimd.tensor_tensor(ZL[:, n], src[:, 0:LS], ZH[:, n].bitcast(F32), ALU.subtract)\
                            .then_inc(rope_lo.sem, 1)
                        pool.wait_ge(rope_lo.sem, rope_lo.at(l, n + 1) + h * 2)
                        nc.gpsimd.tensor_tensor(src[:, 0:LS], src[:, 0:LS], ROPE[:, 0, :], ALU.mult)\
                            .then_inc(rope_cos.sem, 1)
                    for m in range(2):
                        own = slice(64 * m, 64 * m + 64)
                        pool.wait_ge(qk_hi.sem, qk_hi.at(l, m + 1) + h * 6)
                        nc.gpsimd.tensor_tensor(KL[own, m, :], KR[own, :], KH[own, m, :].bitcast(F32), ALU.subtract)\
                            .then_inc(kl_split.sem, 1)
                for b in REAL[RAW_OF[B_OUT]:RAW_OF[B_MLP] + 4]:
                    split(l, b, 0, 4)
                centre(l, 0)
                with pool.Fori(0, 5) as i:
                    for q in range(12):
                        split(l, B_MLP + 4 + q, i, 12)
                for n in range(24):
                    q, j = n // 8, n % 8
                    t0, tn = CHUNKS[q]
                    dst = ACC2[:, 1, t0:t0 + tn]
                    pool.wait_ge(sq_ready.sem, sq_ready.at(l, 24 + n + 1))
                    if j == 0:
                        ins = nc.gpsimd.tensor_tensor(dst, SQM[:, n % 2, :tn], ONE[:].broadcast_to([128, tn]), ALU.mult)
                    else:
                        pool.wait_ge(sq_added.sem, sq_added.at(l, 24 + n))
                        ins = nc.gpsimd.tensor_tensor(dst, dst, SQM[:, n % 2, :tn], ALU.add)
                    ins.then_inc(sq_added.sem, 1)
                centre(l, 1)

        @block.tensor
        def _(pe):
            def weights_ready(l, b, i=0, per_i=0):
                pe.wait_ge(blk_ready.sem, blk_ready.at(l, b + 1) + i * per_i)

            def column_product(out, s, hi, lo, beside=None):
                for n, (w, m) in enumerate(((RH, hi), (RH, lo), (RL, hi))):
                    for k in range(KT):
                        mm = pe.matmul(out, w[:, s, k * 128:(k + 1) * 128], m(k),
                                       start=(n == 0 and k == 0), stop=(n == 2 and k == KT - 1))
                        if n == 1 and beside is not None:
                            beside(k)
                return mm

            pe.wait_ge(const_in.sem, 7 * 16)
            pe.transpose(PS[:, 6, 0:16], CROW[0:16, :], IDENT[0:16, 0:16])
            pe.transpose(PS[:, 6, 16:48], BROW[0:32, :], IDENT[0:32, 0:32]).then_inc(row_turned.sem, 1)
            for t in range(TT):
                pe.wait_ge(x_in[t % 2].sem, 16 * (t // 2 + 1))
                if t >= 2:
                    pe.wait_ge(x_placed.sem, t - 1)
                for j in range(KT):
                    mm = pe.transpose(PSF[:, (t % 2) * 1024 + j * 128:(t % 2) * 1024 + (j + 1) * 128],
                                      XIN[:, t % 2, j * 128:(j + 1) * 128], IDENT[:])
                mm.then_inc(x_turned.sem, 1)
            pe.wait_ge(silu_done.sem, 1)

            def ada_tile(a, col):
                cv = CONDS[:, :].rearrange("p (v k) -> p k v", v=2)
                for k in range(KT):
                    mm = pe.matmul(PS[:, 7, 2 * col:2 * col + 2], ADW[:, a % 2, k, :], cv[:, k, :],
                                   start=(k == 0), stop=(k == KT - 1))
                mm.then_inc(ada_used.sem, 1)

            a = 0

            def ada_tiles(a, n):
                for a in range(a, a + n):
                    pe.wait_ge(ada_in[a % 2].sem, 16 * (a // 2 + 1))
                    ada_tile(a, a)

            pe.wait_ge(hf_in.sem, HF_LOADS * 16)
            pe.wait_ge(x_placed.sem, TT)
            for l in range(DEPTH):
                for n, (w, kk, src) in enumerate(((HW1, 33, FEAT), (HW2, 64, HID1))):
                    if n:
                        pe.wait_ge(hf_sin.sem, 2 * l + 1)
                    elif l:
                        pe.wait_ge(hft_read.sem, TT * l)
                    for q, (t0, tn) in enumerate(CHUNKS):
                        pe.matmul(PS[:, 3 * n + q, 0:tn], w[0:kk, l].rearrange("p a n -> p (a n)"),
                                  src[0:kk, t0:t0 + tn], start=True, stop=True).then_inc(hf_psum.sem, 1)
                    ada_tiles(a, 3)
                    a += 3
                pe.wait_ge(hf_sin.sem, 2 * l + 2)
                for t in range(TT):
                    if TT * l + t > 1:
                        pe.wait_ge(hft_read.sem, TT * l + t - 1)
                    pe.matmul(PS[:, t % 2, :], HID2[0:64, t * 128:(t + 1) * 128], HW3[0:64, l, :],
                              start=True, stop=True).then_inc(hft_psum.sem, 1)
                    ada_tiles(a, 1)
                    a += 1

            with pe.Fori(0, DEPTH) as l:
                def z_tile(n, i, per_i):
                    s, p = n % RING, n % 2
                    weights_ready(l, B_IN + n, i, per_i)
                    for q, (t0, tn) in enumerate(CHUNKS):
                        if n == 0:
                            pe.wait_ge(h_ready.sem, h_ready.at(l, 8 * (q - 2)))
                            pe.wait_ge(var_ready.sem, var_ready.at(l, -1))
                        pe.wait_ge(z_evac.sem, z_evac.at(l, 3 * n + q - 5) + i * (3 * per_i))
                        a = 2 * n + q
                        with_ada = q < 2 and n < 16
                        if with_ada:
                            pe.wait_ge(ada_in[q].sem, ada_in[q].at(l, 16 * (n + 1)) + i * (16 * per_i))

                        def ada(k):
                            m = pe.matmul(PS[:, 7, bass.ds(i * (4 * per_i) + 2 * a, 2) if per_i else
                                             slice(2 * a, 2 * a + 2)],
                                          ADW[:, q, k, :], CONDS[:, :].rearrange("p (v k) -> p k v", v=2)[:, k, :],
                                          start=(k == 0), stop=(k == KT - 1))
                            if k == KT - 1:
                                m.then_inc(ada_used.sem, 1)

                        mm = column_product(PS[:, 3 * p + q, 0:tn], s, lambda k: HH[:, k, t0:t0 + tn],
                                            lambda k: HL[:, k, t0:t0 + tn], ada if with_ada else None)
                        if q < 2:
                            mm.then_inc(z_psum.sem, 1)
                    mm.then_inc(blk_used.sem, 1 + LEFT_OUT.get(n, 0))

                def vectors():
                    pe.wait_ge(h_ready.sem, h_ready.at(l, -16))
                    pe.wait_ge(vec_in.sem, vec_in.at(l, 16 * 18))
                    pe.transpose(PS[:, 6, 0:ROWS_A], VROW[0:ROWS_A, :], IDENT[0:ROWS_A, 0:ROWS_A])
                    pe.transpose(PS[:, 6, ROWS_A:ROWS_A + ROWS_B], VROWB[0:ROWS_B, :],
                                 IDENT[0:ROWS_B, 0:ROWS_B]).then_inc(vec_turned.sem, 1)

                vectors()
                with pe.Fori(0, 2) as i:
                    for n in range(6):
                        z_tile(n, i, 6)
                for n in range(12, ZT):
                    z_tile(n, 0, 0)

                pe.wait_ge(z_evac.sem, z_evac.at(l, 66))
                pe.wait_ge(u_in.sem, u_in.at(l, 32))
                for t in range(TT):
                    pe.wait_ge(u_ready.sem, u_ready.at(l, t - 1))
                    for ct in range(2):
                        mm = pe.transpose(PS[:, 2 + t % 2, ct * 128:(ct + 1) * 128],
                                          UIN[:, ct, t * 128:(t + 1) * 128], IDENT[:])
                    mm.then_inc(u_psum.sem, 1)
                pe.wait_ge(filt_ready.sem, filt_ready.at(l, TT))
                pe.wait_ge(u_ready.sem, u_ready.at(l, TT))
                for j in range(ST):
                    for part in range(2):
                        b = B_FWD + 2 * j + part
                        weights_ready(l, b)
                        if j >= 2:
                            pe.wait_ge(f_sum.sem, f_sum.at(l, j - 1))
                        c0 = 256 * part
                        column_product(PS[:, 2 * (j % 2) + part, :], b % RING,
                                       lambda k: MH[:, k, c0:c0 + 512], lambda k: ML[:, k, c0:c0 + 512])\
                            .then_inc(blk_used.sem, 1)
                b = B_FWD + 16
                weights_ready(l, b)
                pblk = [W[:, b % RING, :].rearrange("p (t n) -> p t n", t=2) for W in (RH, RL)]
                for j in range(PT):
                    pe.wait_ge(f_sum.sem, f_sum.at(l, ST + j - 1))
                    for part in range(2):
                        c0, f0 = 256 * part, 256 * part + 128 * j
                        for n, (w, m) in enumerate(((pblk[0], MH), (pblk[0], ML), (pblk[1], MH))):
                            for k in range(PT):
                                mm = pe.matmul(PS[:, 2 * (j % 2) + part, :], w[:, k, f0:f0 + 128],
                                               m[:, ST + k, c0:c0 + 512],
                                               start=(n == 0 and k == 0), stop=(n == 2 and k == 1))
                    if j == 0:
                        mm.then_inc(dft_psum.sem, 1)
                mm.then_inc(blk_used.sem, 2)
                def channel_sums(q):
                    tn = CHUNKS[q][1]
                    t0 = CHUNKS[q][0]
                    if q == 0:
                        pe.wait_ge(f_sum.sem, f_sum.at(l, TT))
                        pe.wait_ge(cf_in.sem, cf_in.at(l, 32))
                    else:
                        pe.wait_ge(cf_var.sem, cf_var.at(l, q))
                    pe.wait_ge(cf_sq.sem, cf_sq.at(l, q + 1))
                    for n in range(2):
                        for ct in range(2):
                            mm = pe.matmul(PS[:, 2 + n, 0:tn], ONES[:],
                                           CFS[:, ct, 0:tn] if n else CFU[:, ct, t0:t0 + tn],
                                           start=(ct == 0), stop=(ct == 1))
                    mm.then_inc(cf_stats.sem, 1)

                for j in range(ST):
                    for part in range(2):
                        b = B_INV + 2 * j + part
                        weights_ready(l, b)
                        if part == 0:
                            pe.wait_ge(f_ready.sem, f_ready.at(l, j + 1))
                        for ct in range(2):
                            for n, (f, w) in enumerate(((FH, RH), (FH, RL), (FL, RH))):
                                for q in range(2):
                                    mm = pe.matmul(PS[:, 4 + 2 * ct + q, :], f[:, j, part, ct * 128:(ct + 1) * 128],
                                                   w[:, b % RING, q * 512:(q + 1) * 512],
                                                   start=(j == 0 and part == 0 and n == 0),
                                                   stop=(j == ST - 1 and part == 1 and n == 2))
                        mm.then_inc(blk_used.sem, 1)
                    if j in (2, 4, 6):
                        channel_sums(j // 2 - 1)
                b = B_INV + 16
                weights_ready(l, b)
                pe.wait_ge(f_ready.sem, f_ready.at(l, TT))
                pblk = [W[:, b % RING, :].rearrange("p (t n) -> p t n", t=2) for W in (RH, RL)]
                for ct in range(2):
                    for j in range(PT):
                        for part in range(2):
                            for n, (f, w) in enumerate(((FPH, pblk[0]), (FPH, pblk[1]), (FPL, pblk[0]))):
                                mm = pe.matmul(PS[:, ct, 0:256], f[:, j, part, ct * 128:(ct + 1) * 128],
                                               w[:, j, 256 * part:256 * part + 256],
                                               start=(j == 0 and part == 0 and n == 0),
                                               stop=(j == 1 and part == 1 and n == 2))
                mm.then_inc(blk_used.sem, 2)

                def swaps(h):
                    for n in range(2):
                        pe.wait_ge(rope_lo.sem, rope_lo.at(l, n + 1) + h * 2)
                        for q in range(2):
                            cols = slice(512 * q, 512 * q + 512)
                            pe.matmul(PS[:, 1 + 3 * n + q, :], SWAP[:], ZH[:, n, cols], start=True, stop=False)
                            mm = pe.matmul(PS[:, 1 + 3 * n + q, :], SWAP[:], ZL[:, n, cols], start=False, stop=True)
                        mm.then_inc(rope_swapped.sem, 1)

                def turn_inputs(h):
                    pe.wait_ge(rope_done.sem, rope_done.at(l, 2) + h * 2)
                    for t in range(2):
                        pe.transpose(PS[:, 0, t * 128:(t + 1) * 128], CKV[:, 0, t, :], IDENT[:])
                        pe.transpose(PS[:, 0, 256 + t * 128:256 + (t + 1) * 128],
                                     KR[:, S_KEYS + t * 128:S_KEYS + (t + 1) * 128], IDENT[:])
                    for t in range(TT):
                        mm = pe.transpose(PSF[:, 512 + t * 128:512 + (t + 1) * 128],
                                          VR[:, t * 128:(t + 1) * 128], IDENT[:])
                    mm.then_inc(prep_turned.sem, 1)

                def head(h, last):
                    pe.wait_ge(qk_split.sem, qk_split.at(l, 1) + h)
                    pe.wait_ge(kl_split.sem, kl_split.at(l, 2) + h * 2)
                    pe.wait_ge(o_placed.sem, o_placed.at(l, 0) + h)

                    def scores(t):
                        k0, kn = ITEMS[t]
                        for m in range(2):
                            if t:
                                pe.wait_ge(probs.sem, probs.at(l, 2 * t - 1 + m) + h * (2 * TT))
                            pieces = [(o, min(512, kn - o)) for o in range(0, kn, 512)]
                            for o, w in pieces:
                                for x, kk in enumerate((KH, KL)):
                                    mm = pe.matmul(PSF[:, 1536 * m + o:1536 * m + o + w],
                                                   QQ[:, m, t * 128:(t + 1) * 128],
                                                   kk[:, m, k0 + o:k0 + o + w], start=(x == 0), stop=(x == 1))
                            mm.then_inc(s_psum.sem, 1)

                    def turn(t, which):
                        for r, (g0, gn) in enumerate(rounds(t)):
                            if r not in which:
                                continue
                            if r == 0:
                                pe.wait_ge(mixed.sem, mixed.at(l, t + 1) + h * TT)
                            if r == 1 and t > 1:
                                pe.wait_ge(o_ready.sem, o_ready.at(l, t - 1) + h * TT)
                            elif r != 1 and (r or t):
                                pe.wait_ge(at_lo.sem, at_lo.at(l, first_round(t) + (1 if r else 0)) + h * ROUNDS)
                            for e in range(gn):
                                mm = pe.transpose(PS[:, 6 + r % 2, e * 128:(e + 1) * 128],
                                                  AB[:, (g0 + e) * 128:(g0 + e + 1) * 128], IDENT[:])
                            mm.then_inc(at_psum.sem, 1)

                    def values(t, seen):
                        k0, kn = ITEMS[t]
                        pe.wait_ge(at_lo.sem, at_lo.at(l, seen) + h * ROUNDS)
                        if t:
                            pe.wait_ge(o_ready.sem, o_ready.at(l, t) + h * TT)
                        else:
                            pe.wait_ge(v_split.sem, v_split.at(l, 1) + h)
                        nk = kn // 128
                        for k in range(nk):
                            kt = k0 // 128 + k
                            pe.matmul(PS[:, 7, 0:256], ATH[:, t % 2, k * 128:(k + 1) * 128], V2[:, kt, :],
                                      start=(k == 0), stop=False)
                            mm = pe.matmul(PS[:, 7, 0:128], ATL[:, t % 2, k * 128:(k + 1) * 128],
                                           V2[:, kt, 0:128], start=False, stop=(k == nk - 1))
                        mm.then_inc(pv_psum.sem, 1)

                    scores(0)
                    scores(1)
                    for t in range(TT):
                        turn(t, (0, 1))
                        if t + 2 < TT:
                            scores(t + 2)
                        turn(t, (2,))
                        if t == ST and not last:
                            swaps(h + 1)
                        if t:
                            values(t - 1, first_round(t) + (2 if len(rounds(t)) > 1 else 0))
                    values(TT - 1, ROUNDS)
                    if not last:
                        turn_inputs(h + 1)
                    pe.wait_ge(o_normed.sem, o_normed.at(l, 1) + h)
                    for t in range(TT):
                        mm = pe.transpose(PSF[:, 2048 + t * 128:2048 + (t + 1) * 128], OB[:, t, :], IDENT[:])
                    mm.then_inc(o_turned.sem, 1)

                pe.wait_ge(hy_done.sem, hy_done.at(l, 6))
                swaps(0)
                turn_inputs(0)
                with pe.Fori(0, HEADS - 1) as h:
                    head(h, False)
                head(HEADS - 1, True)
                pe.wait_ge(o_placed.sem, o_placed.at(l, HEADS))

                for n in range(KT):
                    b = B_OUT + n
                    weights_ready(l, b)
                    for q, (t0, tn) in enumerate(CHUNKS):
                        if n == 0:
                            pe.wait_ge(y_lo.sem, y_lo.at(l, 8 * (q + 1)))
                        pe.wait_ge(o_evac.sem, o_evac.at(l, 3 * n + q - 5))
                        mm = column_product(PS[:, 3 * (n % 2) + q, 0:tn], b % RING,
                                            lambda k: HH[:, k, t0:t0 + tn], lambda k: HL[:, k, t0:t0 + tn])
                        if q < 2:
                            mm.then_inc(o_psum.sem, 1)
                    mm.then_inc(blk_used.sem, 1)

                def norm_sums(which, q, bank):
                    t0, tn = CHUNKS[q]
                    pe.wait_ge(acc_ready.sem, acc_ready.at(l, 3 * which + q + 1))
                    if which:
                        pe.wait_ge(sq_added.sem, sq_added.at(l, 24 + 8 * (q + 1)))
                    for n in range(2):
                        mm = pe.matmul(PS[:, bank + n, 0:tn], ONES[:], (ACC1, ACC2)[which][:, n, t0:t0 + tn],
                                       start=True, stop=True)
                    mm.then_inc(stats.sem, 1)

                for q in range(3):
                    norm_sums(0, q, (6, 0, 2)[q])

                def up(g0, q, i):
                    t0, tn = CHUNKS[q]
                    for e in range(2):
                        b = B_MLP + 4 * g0 + e
                        if q == 0:
                            weights_ready(l, b, i, 12)
                        if e == 0:
                            pe.wait_ge(hid_ready.sem, hid_ready.at(l, 2 * (3 * g0 + q)) + i * 18)
                        mm = column_product(PS[:, e, 0:tn], b % RING,
                                            lambda k: HH[:, k, t0:t0 + tn], lambda k: HL[:, k, t0:t0 + tn])
                        if q < 2:
                            mm.then_inc(m1_psum.sem, 1)
                        else:
                            mm.then_inc(blk_used.sem, 1)

                def down(g0, q, i):
                    t0, tn = CHUNKS[q]
                    b = B_MLP + 4 * g0 + 2
                    if q == 0:
                        weights_ready(l, b + 1, i, 12)
                    pe.wait_ge(hid_ready.sem, hid_ready.at(l, 2 * (3 * g0 + q) + 2) + i * 18)
                    for j in range(KT):
                        m = 8 * (3 * g0 + q) + j
                        pe.wait_ge(m2_evac.sem, m2_evac.at(l, m - 5) + i * 72)
                        for n, (w, x) in enumerate(((RH, hidden_hi(q)), (RH, hidden_lo(q)), (RL, hidden_hi(q)))):
                            for e in range(2):
                                mm = pe.matmul(PS[:, 2 + m % 6, 0:tn], w[:, (b + e) % RING, j * 128:(j + 1) * 128],
                                               x[:, e, 0:tn], start=(n == 0 and e == 0),
                                               stop=(n == 2 and e == 1))
                        if q == 2 and j == KT - 1:
                            mm.then_inc(blk_used.sem, 2)
                        else:
                            mm.then_inc(m2_psum.sem, 1)

                for q in range(3):
                    pe.wait_ge(h_ready.sem, h_ready.at(l, 8 * (q + 1)))
                    pe.wait_ge(var_ready.sem, var_ready.at(l, min(q + 2, 3)))
                    up(0, q, 0)
                    if q:
                        down(0, q - 1, 0)
                with pe.Fori(0, 5) as i:
                    for g in range(1, 4):
                        up(g, 0, i)
                        down(g - 1, 2, i)
                        up(g, 1, i)
                        down(g, 0, i)
                        up(g, 2, i)
                        down(g, 1, i)
                pe.wait_ge(hid_ready.sem, hid_ready.at(l, 6 * GROUPS))
                norm_sums(1, 0, 0)
                down(GROUPS - 1, 2, 0)
                pe.wait_ge(m2_evac.sem, m2_evac.at(l, 24 * GROUPS))
                norm_sums(1, 1, 2)
                norm_sums(1, 2, 4)

            for t in range(TT):
                pe.wait_ge(xs_ready.sem, xs_ready.at(DEPTH - 1, 24 + 8 * (t // 4 + 1)))
                if t >= 2:
                    pe.wait_ge(y_placed.sem, t - 1)
                for j in range(KT):
                    mm = pe.transpose(PSF[:, (t % 2) * 1024 + j * 128:(t % 2) * 1024 + (j + 1) * 128],
                                      XT[:, j, t * 128:(t + 1) * 128], IDENT[:])
                mm.then_inc(y_turned.sem, 1)

        @block.scalar
        def _(act):
            A = Chain(act, a_chain, A_STEPS, A_BEFORE)
            S = nc.scalar

            for dst, src in [(FEAT[0:33, :], feats_d), (DEC[:], decay_d.rearrange("(t p) n -> p t n", p=128))]:
                act.dma_start(dst, src).then_inc(hf_in.sem, 16)
            for l in range(DEPTH):
                for dst, src in ((HW1[0:33, l, 0], hf_w1[l]), (HW1[0:33, l, 1], hf_w1[l]), (HW2[0:64, l, 0], hf_w2[l]),
                                 (HW2[0:64, l, 1], hf_w2[l]), (HW3[0:64, l], hf_w3[l])):
                    act.dma_start(dst, src).then_inc(hf_in.sem, 16)
                for n, v in enumerate((hf_b1, hf_freq, hf_b2)):
                    act.dma_start(HFV[0:64, l, n:n + 1], v[l].rearrange("(p a) -> p a", a=1)).then_inc(hf_in.sem, 16)
            act.wait_ge(row_placed.sem, 1)
            S.activation(CONDS[:], CRAW[:], ACT.Silu).then_inc(silu_done.sem, 1)
            for t in range(TT):
                act.wait_ge(x_turned.sem, t + 1)
                for half in range(2):
                    ins = S.activation(XT[:, 4 * half:4 * half + 4, t * 128:(t + 1) * 128],
                                       PS[:, 2 * (t % 2) + half, :].rearrange("p (j n) -> p j n", j=4),
                                       ACT.Copy, scale=ALPHA)
                ins.then_inc(x_placed.sem, 1)

            def hi_of_h(j, q, scale, bias):
                t0, tn = CHUNKS[q]
                S.activation(HH[:, j, t0:t0 + tn], XT[:, j, t0:t0 + tn], ACT.Identity, scale=scale, bias=bias)\
                    .then_inc(hh_ready.sem, 1)

            for l in range(DEPTH):
                for n, dst in enumerate((HID1, HID2)):
                    act.wait_ge(hf_arg.sem, 2 * l + n + 1)
                    S.activation(dst[0:64, :], ARG[0:64, :], ACT.Sin).then_inc(hf_sin.sem, 1)
                for t in range(TT):
                    act.wait_ge(fout_ready.sem, TT * l + t + 1)
                    p = (TT * l + t) % 4
                    act.dma_start(filt_d[l, t], FOUT[:, p].rearrange("p a n -> p (a n)")).then_inc(fout_stored[p].sem, 16)
            act.wait_ge(const_done.sem, 1)
            for p in range(4):
                act.wait_ge(fout_stored[p].sem, 16 * (DEPTH * TT // 4))
            act.wait_ge(x_placed.sem, TT)
            for q in range(3):
                v = COND[q]
                for j in range(KT):
                    hi_of_h(j, q, AD0[:, 0, 8 + j, v:v + 1], AD0[:, 0, j, v:v + 1])

            def gains(l, which, q):
                t0, tn = CHUNKS[q]
                for j in range(KT):
                    x, at = XT[:, j, t0:t0 + tn], 16 * which + j
                    act.wait_ge(hh_ready.sem, hh_ready.at(l, 8 * (3 * which + q) + j + 1))
                    S.activation(x, x, ACT.Identity, scale=LNV[:, at:at + 1], bias=LNV[:, at + 8:at + 9])\
                     .then_inc(xs_ready.sem, 1)

            def norm(l, which):
                act.wait_ge(mod_ready.sem, mod_ready.at(l, which + 1))
                for q, (t0, tn) in enumerate(CHUNKS):
                    act.wait_ge(var_ready.sem, var_ready.at(l, 3 * which + q + 1))
                    S.activation(MR[:, 1, t0:t0 + tn], MR[:, 1, t0:t0 + tn], ACT.Sqrt).then_inc(sd_ready.sem, 1)
                for q, (t0, tn) in enumerate(CHUNKS):
                    v = COND[q]
                    for j in range(KT):
                        n = 8 * (3 * which + q) + j
                        x = XT[:, j, t0:t0 + tn]
                        scale, bias = HSB[:, 0, j, v:v + 1], HSB[:, 1, j, v:v + 1]
                        act.wait_ge(xn_ready.sem, xn_ready.at(l, n + 1))
                        S.activation(HH[:, j, t0:t0 + tn], x, ACT.Identity, scale=scale, bias=bias)
                        act.wait_ge(h_ready.sem, h_ready.at(l, n - 1))
                        S.activation(HT[:, n % 2, :tn], x, ACT.Identity, scale=scale, bias=bias)\
                         .then_inc(hh_ready.sem, 1)

            with act.Fori(0, DEPTH) as l:
                A.layer(l)
                def conv_store(u):
                    kind, ct, q = UNITS[u]
                    t0, tn = CHUNKS[q]
                    act.wait_ge(conv_done.sem, conv_done.at(l, u + 1))
                    if kind == "hyena":
                        for n in range(2):
                            act.dma_start(hy_d[n, ct, :, t0:t0 + tn], CACC[:, n, :tn]).then_inc(conv_stored.sem, 16)
                    else:
                        act.dma_start(cf_d[ct, :, t0:t0 + tn], CACC[:, 0, :tn]).then_inc(conv_stored.sem, 16)

                def conv_load(u, n):
                    kind, ct, q = UNITS[u]
                    t0, tn = CHUNKS[q]
                    halo = 1 if kind == "hyena" else 15
                    lo = t0 - (halo if q == 1 else 0)
                    hi = t0 + tn + (halo if q == 0 else 0)
                    at = lo - (t0 - halo)
                    done = 3 * n
                    for p in range(2):
                        act.wait_ge(z_stored[p].sem, z_stored[p].at(l, 16 * ((done + 1 - p) // 2)))
                    act.wait_ge(conv_done.sem, conv_done.at(l, u))
                    tiles = (ct, 2 + ct, 4 + ct) if kind == "hyena" else (6 + ct, 8 + ct)
                    dst = HYIN if kind == "hyena" else CFIN
                    for x, tile in enumerate(tiles):
                        act.dma_start(dst[:, x, at:at + hi - lo], z_d[tile, :, lo:hi]).then_inc(conv_in.sem, 16)

                act.wait_ge(h_ready.sem, h_ready.at(l, 0))
                for n in range(ZT):
                    for q, (t0, tn) in enumerate(CHUNKS):
                        u = 3 * n + q
                        if q < 2:
                            act.wait_ge(z_psum.sem, z_psum.at(l, 2 * n + q + 1))
                        else:
                            act.wait_ge(blk_used.sem, blk_used.at(l, n + 1))
                        act.wait_ge(z_stored[u % 2].sem, z_stored[u % 2].at(l, 16 * (u // 2)))
                        S.activation(ZST[:, u % 2, :tn], PS[:, 3 * (n % 2) + q, :tn], ACT.Copy).then_inc(z_evac.sem, 1)
                        act.wait_ge(z_evac.sem, z_evac.at(l, u + 1))
                        act.dma_start(z_d[n, :, t0:t0 + tn], ZST[:, u % 2, :tn]).then_inc(z_stored[u % 2].sem, 16)
                    for u in [u for u, at in enumerate(UNIT_AT) if at == n]:
                        if u:
                            conv_store(u - 1)
                        conv_load(u, n)
                        if UNITS[u][0] == "conformer":
                            t0, tn = CHUNKS[UNITS[u][2]]
                            act.wait_ge(conv_in.sem, conv_in.at(l, 6 * 48 + (u - 5) * 32))
                            act.wait_ge(pads_ready.sem, pads_ready.at(l, u - 5))
                            S.activation(CFIN[:, 1, :tn + 30], CFIN[:, 1, :tn + 30], ACT.Sigmoid)\
                             .then_inc(glu_done.sem, 1)
                conv_store(11)

                act.wait_ge(blk_used.sem, blk_used.at(l, B_FWD))
                act.wait_ge(conv_stored.sem, conv_stored.at(l, 288))
                for ct in range(2):
                    act.dma_start(UIN[:, ct, :], hy_d[0, ct]).then_inc(u_in.sem, 16)
                for p in range(TT // 2):
                    act.dma_start(FPM[:, 2 * p:2 * p + 2].rearrange("p t a n -> p t (a n)"),
                                  filt_d[l].rearrange("t p n -> p t n")[:, 2 * p:2 * p + 2, :]).then_inc(filt_in[p].sem, 16)
                for t in range(TT):
                    act.wait_ge(filt_in[t // 2].sem, filt_in[t // 2].at(l, 16))
                    S.activation(MH[:, t, 0:768].rearrange("p (a n) -> p a n", a=3)[:, 0:3:2, :], FPM[:, t], ACT.Copy)\
                     .then_inc(m_hi.sem, 1)
                    act.wait_ge(u_psum.sem, u_psum.at(l, t + 1))
                    S.activation(MH[:, t, 256:512], PS[:, 2 + t % 2, 0:256], ACT.Copy).then_inc(u_hi.sem, 1)
                for j in range(TT):
                    b0 = 2 * (j % 2)
                    if j < ST:
                        act.wait_ge(blk_used.sem, blk_used.at(l, B_FWD + 2 * j + 2))
                    elif j == ST:
                        act.wait_ge(dft_psum.sem, dft_psum.at(l, 1))
                    else:
                        act.wait_ge(blk_used.sem, blk_used.at(l, B_INV))
                    if j:
                        act.wait_ge(f_sum.sem, f_sum.at(l, j))
                    S.activation(GS[:, 0, :], PS[:, b0, 0:256], ACT.Copy, scale=WF[:, j:j + 1])
                    S.activation(GS[:, 1, :], PS[:, b0 + 1, 256:512], ACT.Copy, scale=WF[:, j:j + 1])\
                     .then_inc(g_scaled.sem, 1)
                    act.wait_ge(f_sum.sem, f_sum.at(l, j + 1))
                    S.activation(FH[:, j] if j < ST else FPH[:, j - ST], YF[:], ACT.Copy).then_inc(f_hi.sem, 1)
                for x in range(2):
                    for ct in range(2):
                        act.dma_start(OLD[:, x, ct], hy_d[x, ct]).then_inc(old_in.sem, 16)
                act.wait_ge(f_ready.sem, f_ready.at(l, TT))
                act.wait_ge(blk_used.sem, blk_used.at(l, B_INV))
                act.dma_start(CFU[:], cf_d.rearrange("c p t -> p c t")).then_inc(cf_in.sem, 32)

                def square(q):
                    t0, tn = CHUNKS[q]
                    S.activation(CFS[:, :, :tn], CFU[:, :, t0:t0 + tn], ACT.Square).then_inc(cf_sq.sem, 1)

                act.wait_ge(cf_in.sem, cf_in.at(l, 32))
                square(0)
                for q, (t0, tn) in enumerate(CHUNKS):
                    act.wait_ge(cf_var.sem, cf_var.at(l, q + 1))
                    S.activation(RS[:, :tn], RS[:, :tn], ACT.Sqrt, bias=EPSC[:, 0:1]).then_inc(cf_sd.sem, 1)
                    if q < 2:
                        act.wait_ge(cf_stats.sem, cf_stats.at(l, q + 1))
                        square(q + 1)
                    act.wait_ge(cf_norm.sem, cf_norm.at(l, q + 1))
                    for ct in range(2):
                        u = CFU[:, ct, t0:t0 + tn]
                        ins = S.activation(u, u, ACT.Silu, scale=VEC[:, V_CFG + ct:V_CFG + ct + 1],
                                           bias=VEC[:, V_CFBB + ct:V_CFBB + ct + 1])
                    ins.then_inc(cf_silu.sem, 1)
                act.wait_ge(cf_silu.sem, cf_silu.at(l, 3))
                for ct in range(2):
                    act.dma_start(y_d[2 + ct], CFU[:, ct]).then_inc(hy_stored.sem, 16)
                for ct in range(2):
                    act.wait_ge(hy_done.sem, hy_done.at(l, 3 * (ct + 1)))
                    act.dma_start(y_d[ct], OY[:, ct]).then_inc(hy_stored.sem, 16)

                act.wait_ge(lam_ready.sem, lam_ready.at(l, 1))
                S.activation(LAMS[:, 2:4], LAMS[:, 0:2], ACT.Exp).then_inc(lam_exp.sem, 1)
                def split_inputs(h):
                    act.wait_ge(prep_turned.sem, prep_turned.at(l, 1) + h)
                    act.wait_ge(kv_stored.sem, kv_stored.at(l, 0) + h * 32)
                    S.activation(KR[:, 0:PAST], PS[:, 0, 0:PAST], ACT.Copy).then_inc(kc_placed.sem, 1)
                    S.activation(KO[:].rearrange("p t n -> p (t n)"), PS[:, 0, 256:512], ACT.Copy)
                    S.activation(VO[:].rearrange("p t n -> p (t n)"), PSF[:, 512 + 1024:512 + 1280], ACT.Copy)\
                     .then_inc(kv_copied.sem, 1)
                    S.activation(V2[:, 0:2, 0:128], CKV[:, 1], ACT.Copy)
                    S.activation(V2[:, 2:TT + 2, 0:128], PSF[:, 512:512 + T].rearrange("p (t n) -> p t n", t=TT),
                                 ACT.Copy).then_inc(v_hi.sem, 1)
                    act.wait_ge(rope_done.sem, rope_done.at(l, 2) + h * 2)
                    act.wait_ge(kc_placed.sem, kc_placed.at(l, 1) + h)
                    for src, dst, scale, flip in ((KR, KH, 1.0, False), (KR, KH, 1.0, True), (QR, QQ, SCALE, False)):
                        for m in range(2):
                            own = slice(64 * m, 64 * m + 64)
                            to = slice(64 - 64 * m, 128 - 64 * m) if flip else own
                            S.activation(dst[to, m, :], src[own, :], ACT.Copy, scale=scale).then_inc(qk_hi.sem, 1)
                    act.wait_ge(kv_copied.sem, kv_copied.at(l, 1) + h)
                    for dst, src in ((new_k, KO), (new_v, VO)):
                        act.dma_start(dst[0, l].rearrange("(t p) m d -> p t (m d)", p=128)
                                      [:, :, h * 128:h * 128 + 128] if isinstance(h, int) else
                                      dst[0, l].rearrange("(t p) m d -> p t (m d)", p=128)[:, :, bass.ts(h, 128)],
                                      src[:]).then_inc(kv_stored.sem, 16)

                def head(h, last):
                    def exps(t, m):
                        k0, kn = ITEMS[t]
                        act.wait_ge(smax.sem, smax.at(l, 2 * t + m + 1) + h * 2 * TT)
                        if t > 1:
                            act.wait_ge(mixed.sem, mixed.at(l, t - 1) + h * TT)
                        S.activation(PB[:, t % 2, m, :kn], PSF[:, 1536 * m:1536 * m + kn], ACT.Exp,
                                     bias=STAT[:, t % 4, m:m + 1],
                                     accum_out=STAT[:, t % 4, 2 + m:3 + m]).then_inc(probs.sem, 1)

                    def hi_of_round(t, r):
                        g0, gn = rounds(t)[r]
                        act.wait_ge(at_psum.sem, at_psum.at(l, first_round(t) + r + 1) + h * ROUNDS)
                        if t > 1 and r == 0:
                            act.wait_ge(pv_psum.sem, pv_psum.at(l, t - 1) + h * TT)
                        S.activation(ATH[:, t % 2, g0 * 128:(g0 + gn) * 128], PS[:, 6 + r % 2, 0:gn * 128],
                                     ACT.Copy).then_inc(at_hi.sem, 1)

                    def part_of_output(t):
                        act.wait_ge(pv_psum.sem, pv_psum.at(l, t + 1) + h * TT)
                        if t:
                            act.wait_ge(o_ready.sem, o_ready.at(l, t) + h * TT)
                        S.activation(O2[:], PS[:, 7, 128:256], ACT.Copy, scale=STAT[:, t % 4, 4:5])\
                         .then_inc(o_part.sem, 1)

                    def square(t):
                        act.wait_ge(o_ready.sem, o_ready.at(l, t + 1) + h * TT)
                        ins = S.activation(SQJ[:], OB[:, t, :], ACT.Square, accum_out=SSQ[:, t:t + 1])
                        if t < TT - 1:
                            A.link(ins)
                        else:
                            ins.then_inc(ssq_done.sem, 1)

                    for t in range(2):
                        for m in range(2):
                            exps(t, m)
                    for t in range(TT):
                        for r in range(len(rounds(t))):
                            hi_of_round(t, r)
                        if t + 2 < TT:
                            exps(t + 2, 0)
                            exps(t + 2, 1)
                        if t:
                            part_of_output(t - 1)
                        if t > 1:
                            square(t - 2)
                    part_of_output(TT - 1)
                    square(TT - 2)
                    square(TT - 1)
                    if not last:
                        split_inputs(h + 1)
                    act.wait_ge(ssq_done.sem, ssq_done.at(l, 1) + h)
                    S.activation(RRS[:], SSQ[:], ACT.Sqrt, scale=1 / 128, bias=EPSC[:, 0:1]).then_inc(sd_head.sem, 1)
                    act.wait_ge(o_turned.sem, o_turned.at(l, 1) + h)
                    act.wait_ge(yat_stored.sem, yat_stored.at(l, 0) + h * 16)
                    S.activation(OT[:], PSF[:, 2048:2048 + T], ACT.Copy, scale=VEC[:, V_SUB:V_SUB + 1])\
                     .then_inc(o_placed.sem, 1)
                    act.wait_ge(o_placed.sem, o_placed.at(l, 1) + h)
                    act.dma_start(y_d[h + 4], OT[:]).then_inc(yat_stored.sem, 16)

                split_inputs(0)
                with act.Fori(0, HEADS - 1) as h:
                    A.loop(h, TT - 1, HEADS - 1)
                    head(h, False)
                A.end_loop()
                head(HEADS - 1, True)

                for n in range(24):
                    q, j = n // 8, n % 8
                    t0, tn = CHUNKS[q]
                    act.wait_ge(y_in[n % 4].sem, y_in[n % 4].at(l, 16 * (n // 4 + 1)))
                    S.activation(HH[:, j, t0:t0 + tn], YIN[:, n % 4, :tn], ACT.Copy).then_inc(y_hi.sem, 1)

                def squares(which, buf):
                    for n in range(24):
                        q, j = (n % 3, n // 3) if which == 0 else (n // 8, n % 8)
                        t0, tn = CHUNKS[q]
                        if which == 0:
                            act.wait_ge(o_evac.sem, o_evac.at(l, n + 1))
                        else:
                            act.wait_ge(m2_evac.sem, m2_evac.at(l, 24 * (GROUPS - 1) + n + 1))
                        act.wait_ge(sq_added.sem, sq_added.at(l, 24 * which + n - 1))
                        S.activation(buf[:, n % 2, :tn], XT[:, j, t0:t0 + tn], ACT.Square).then_inc(sq_ready.sem, 1)

                squares(0, SQO)
                norm(l, 0)

                def hidden(g0, q, i):
                    t0, tn = CHUNKS[q]
                    for e in range(2):
                        u = 2 * (3 * g0 + q) + e
                        if q < 2:
                            act.wait_ge(m1_psum.sem, m1_psum.at(l, 4 * g0 + 2 * q + e + 1) + i * 4)
                        else:
                            act.wait_ge(blk_used.sem, blk_used.at(l, B_MLP + 4 * g0 + e + 1) + i * 4)
                        act.wait_ge(hid_ready.sem, hid_ready.at(l, u - 1) + i * 6)
                        S.activation(RB[:, e, :tn], PS[:, e, :tn], ACT.Relu).then_inc(relu_done.sem, 1)
                        act.wait_ge(relu_done.sem, relu_done.at(l, u + 1) + i * 6)
                        if q == 0:
                            act.wait_ge(m2_psum.sem, m2_psum.at(l, 23 * g0 - 15) + i * 23)
                        elif q == 1:
                            act.wait_ge(m2_psum.sem, m2_psum.at(l, 23 * g0 - 7) + i * 23)
                        else:
                            act.wait_ge(blk_used.sem, blk_used.at(l, B_MLP + 4 * g0) + i * 4)
                        S.activation(hidden_hi(q)[:, e, :tn], RB[:, e, :tn], ACT.Square).then_inc(hid_hi.sem, 1)

                act.wait_ge(kv_stored.sem, kv_stored.at(l, HEADS * 32))
                act.wait_ge(h_ready.sem, h_ready.at(l, 24))
                for q in range(3):
                    hidden(0, q, 0)
                    gains(l, 0, q)
                with act.Fori(1, GROUPS) as g:
                    for q in range(3):
                        hidden(0, q, g)
                act.wait_ge(hid_ready.sem, hid_ready.at(l, 6 * GROUPS))
                squares(1, SQM)
                norm(l, 1)
                for q in range(3):
                    gains(l, 1, q)
                A.end_layer()

            for t in range(TT):
                act.wait_ge(y_placed.sem, t + 1)
                dst = y_sample[0, t * 128:(t + 1) * 128, :] if t < ST else \
                    y_prompt[0, (t - ST) * 128:(t - ST + 1) * 128, :]
                act.dma_start(dst, XIN[:, t % 2]).then_inc(y_stored[t % 2].sem, 16)
            for p in range(2):
                act.wait_ge(y_stored[p].sem, 16 * TT // 2)
            act.wait_ge(kv_stored.sem, kv_stored.at(DEPTH - 1, HEADS * 32))

        @block.vector
        def _(dve):
            V = nc.vector
            C = Chain(dve, v_chain, V_STEPS, V_BEFORE)

            V.memset(ONES[:], 1 / 1024)
            V.memset(EPSC[:], EPS)
            C.link(V.memset(AD0[:], 0.0))
            dve.wait_ge(row_turned.sem, 1)
            V.tensor_copy(CRAW[:], PS[:, 6, 0:16])
            V.tensor_copy(SWAP[:], SWAPF[:])
            V.tensor_copy(B0[:], PS[:, 6, 16:48]).then_inc(row_placed.sem, 1)
            dve.wait_ge(row_placed.sem, 1)
            dve.wait_ge(hf_in.sem, HF_LOADS * 16)
            for l in range(DEPTH):
                for n in range(2):
                    if n or l:
                        dve.wait_ge(hf_sin.sem, 2 * l + n)
                    for q, (t0, tn) in enumerate(CHUNKS):
                        dve.wait_ge(hf_psum.sem, 6 * l + 3 * n + q + 1)
                        b = (0, 2)[n]
                        C.link(V.tensor_scalar(ARG[0:64, t0:t0 + tn], PS[0:64, 3 * n + q, :tn], HFV[0:64, l, b:b + 1],
                                               HFV[0:64, l, 1:2], ALU.add, ALU.mult))
                    C.link(V.tensor_scalar(RND[0:64, :], ARG[0:64, :], 1 / TWO_PI, ROUND, ALU.mult, ALU.add))
                    C.link(V.tensor_scalar(RND[0:64, :], RND[0:64, :], ROUND, -TWO_PI, ALU.subtract, ALU.mult))
                    C.link(V.tensor_tensor(ARG[0:64, :], ARG[0:64, :], RND[0:64, :], ALU.add))
                    V.tensor_scalar(ARG[0:64, :], ARG[0:64, :], PI_BELOW, -PI_BELOW, ALU.min, ALU.max)\
                     .then_inc(hf_arg.sem, 1)
                for t in range(TT):
                    u = TT * l + t
                    dve.wait_ge(hft_psum.sem, u + 1)
                    if u:
                        dve.wait_ge(fout_ready.sem, u)
                    V.tensor_tensor(FB[:], PS[:, t % 2, :], DEC[:, t, :], ALU.mult).then_inc(hft_read.sem, 1)
                    dve.wait_ge(hft_read.sem, u + 1)
                    if u > 3:
                        dve.wait_ge(fout_stored[u % 4].sem, 16 * (u // 4))
                    C.link(V.tensor_tensor(FOUT[:, u % 4, 0, :], FB[:, 0:256], FB[:, 256:512], ALU.add))
                    V.tensor_tensor(FOUT[:, u % 4, 1, :], FB[:, 0:256], FB[:, 256:512], ALU.subtract)\
                     .then_inc(fout_ready.sem, 1)
            dve.wait_ge(ada_used.sem, 34)
            for v in range(2):
                C.link(V.tensor_tensor(AD0[:, 0:DEPTH, :, v], PS[:, 7, 0:64].rearrange("p (l t v) -> p l t v", l=2, v=2)
                                       [:, :, :, v], B0[:].rearrange("p (l t) -> p l t", l=2), ALU.add))
            C.link(V.tensor_scalar(AD0[:, 0:DEPTH, 8:16, :], AD0[:, 0:DEPTH, 8:16, :], 1.0, 1 / ALPHA,
                                   ALU.add, ALU.mult))
            V.memset(MODT[:, 0, 0:2], 0.0).then_inc(const_done.sem, 1)
            dve.wait_ge(const_done.sem, 1)
            dve.wait_ge(x_placed.sem, TT)

            for q, (t0, tn) in enumerate(CHUNKS):
                v = COND[q]
                for j in range(KT):
                    n = 8 * q + j
                    C.link(V.tensor_scalar(MODT[:, n % 2, :tn], XT[:, j, t0:t0 + tn], AD0[:, 0, 8 + j, v:v + 1],
                                           AD0[:, 0, j, v:v + 1], ALU.mult, ALU.add))
                    dve.wait_ge(hh_ready.sem, n + 1)
                    V.tensor_tensor(HL[:, j, t0:t0 + tn], MODT[:, n % 2, :tn], HH[:, j, t0:t0 + tn].bitcast(F32),
                                    ALU.subtract).then_inc(h_ready.sem, 1)
                    if n:
                        dve.wait_ge(h_ready.sem, n)

            def norm(l, which, banks):
                if which:
                    sh, sc = [AD0[:, bass.ds(l + 1, 1), a:a + 8, :].rearrange("p a k v -> p (a k) v") for a in (0, 8)]
                else:
                    sh, sc = ADA[:, A_SH2:A_SH2 + 8, :], ADA[:, A_SC2:A_SC2 + 8, :]
                g, b = [LNV[:, 16 * which + a:16 * which + a + 8].rearrange("p (k a) -> p k a", a=1)
                        .broadcast_to([128, KT, 2]) for a in (0, 8)]
                C.link(V.tensor_tensor(HSB[:, 0], g, sc, ALU.mult))
                C.link(V.tensor_tensor(HSB[:, 1], b, sc, ALU.mult))
                V.tensor_tensor(HSB[:, 1], HSB[:, 1], sh, ALU.add).then_inc(mod_ready.sem, 1)
                for q, (t0, tn) in enumerate(CHUNKS):
                    mu, rs = MR[:, 0, t0:t0 + tn], MR[:, 1, t0:t0 + tn]
                    dve.wait_ge(stats.sem, stats.at(l, 3 * which + q + 1))
                    C.link(V.tensor_copy(mu, PS[:, banks[q], :tn]))
                    C.link(V.tensor_tensor(rs, mu, mu, ALU.mult))
                    V.scalar_tensor_tensor(rs, PS[:, banks[q] + 1, :tn], EPSC[:, 0:1], rs, ALU.add, ALU.subtract)\
                     .then_inc(var_ready.sem, 1)

                def lo(n, j, t0, tn):
                    dve.wait_ge(hh_ready.sem, hh_ready.at(l, n + 1))
                    V.tensor_tensor(HL[:, j, t0:t0 + tn], HT[:, n % 2, :tn], HH[:, j, t0:t0 + tn].bitcast(F32),
                                    ALU.subtract).then_inc(h_ready.sem, 1)

                for q, (t0, tn) in enumerate(CHUNKS):
                    dve.wait_ge(sd_ready.sem, sd_ready.at(l, 3 * which + q + 1))
                    C.link(V.reciprocal(MR[:, 1, t0:t0 + tn], MR[:, 1, t0:t0 + tn]))
                    for j in range(KT):
                        n = 8 * (3 * which + q) + j
                        x = XT[:, j, t0:t0 + tn]
                        dve.wait_ge(centred.sem, centred.at(l, n + 1))
                        V.tensor_tensor(x, x, MR[:, 1, t0:t0 + tn], ALU.mult).then_inc(xn_ready.sem, 1)
                        if j:
                            lo(n - 1, j - 1, t0, tn)
                    lo(n, KT - 1, t0, tn)

            with dve.Fori(0, DEPTH) as l:
                C.layer(l)
                dve.wait_ge(vec_turned.sem, vec_turned.at(l, 1))
                C.link(V.tensor_copy(VEC[:], PS[:, 6, 0:ROWS_A + ROWS_B]))
                dve.wait_ge(xs_ready.sem, xs_ready.at(l, 0))
                C.link(V.tensor_scalar(LNV[:], VEC[:, V_LN:V_LN + 32], ALPHA, None, ALU.mult))
                C.link(V.tensor_tensor(LAMR[:, 0:4:2, :], LAMR[:, 0:4:2, :], LAMR[:, 1:4:2, :], ALU.mult))
                V.tensor_reduce(LAMS[:, 0:2], LAMR[:, 0:4:2, :], AX_X, ALU.add).then_inc(lam_ready.sem, 1)

                for u, (kind, ct, q) in enumerate(UNITS):
                    t0, tn = CHUNKS[q]
                    if kind == "hyena":
                        buf, halo, width, parts = HYIN, 1, tn + 2, 3
                    else:
                        buf, halo, width, parts = CFIN, 15, tn + 30, 2
                    pads = []
                    if q != 1:
                        pads.append(buf[:, 0:parts, 0:halo])
                    if q != 0:
                        pads.append(buf[:, 0:parts, halo + tn:width])
                    for n, pad in enumerate(pads):
                        ins = V.memset(pad, 0.0)
                        if n < len(pads) - 1 or kind == "hyena":
                            C.link(ins)
                    if kind == "conformer":
                        ins.then_inc(pads_ready.sem, 1)
                        dve.wait_ge(glu_done.sem, glu_done.at(l, u - 5))
                    else:
                        dve.wait_ge(conv_in.sem, conv_in.at(l, 48 * (u + 1)))
                    stored = 32 * u if u <= 6 else 192 + 16 * (u - 6)
                    dve.wait_ge(conv_stored.sem, conv_stored.at(l, stored))
                    if kind == "hyena":
                        def conv(x, dst):
                            col = 2 * x + ct
                            C.link(V.tensor_scalar(dst, HYIN[:, x, 0:tn], VEC[:, V_HYW + col:V_HYW + col + 1],
                                                   VEC[:, V_HYB + col:V_HYB + col + 1], ALU.mult, ALU.add))
                            for k in (1, 2):
                                w = V_HYW + 6 * k + col
                                C.link(V.scalar_tensor_tensor(dst, HYIN[:, x, k:k + tn], VEC[:, w:w + 1], dst,
                                                              ALU.mult, ALU.add))
                        conv(1, CACC[:, 0, :tn])
                        conv(2, CACC[:, 1, :tn])
                        C.link(V.tensor_tensor(CACC[:, 0, :tn], CACC[:, 0, :tn], CACC[:, 1, :tn], ALU.mult))
                        conv(0, CACC[:, 1, :tn])
                    else:
                        C.link(V.tensor_tensor(CFIN[:, 0, :width], CFIN[:, 0, :width], CFIN[:, 1, :width], ALU.mult))
                        dst = CACC[:, 0, :tn]
                        C.link(V.tensor_scalar(dst, CFIN[:, 0, 0:tn], VEC[:, V_CFW + ct:V_CFW + ct + 1],
                                               VEC[:, V_CFB + ct:V_CFB + ct + 1], ALU.mult, ALU.add))
                        for k in range(1, 31):
                            w = V_CFW + 2 * k + ct
                            C.link(V.scalar_tensor_tensor(dst, CFIN[:, 0, k:k + tn], VEC[:, w:w + 1], dst,
                                                          ALU.mult, ALU.add))
                    V.memset(STAT[:, 0, 7:8], 0.0).then_inc(conv_done.sem, 1)
                    dve.wait_ge(conv_done.sem, conv_done.at(l, u + 1))

                dve.wait_ge(ada_used.sem, ada_used.at(l, 32))
                for v in range(2):
                    C.link(V.tensor_tensor(ADA[:, :, v], PS[:, 7, 0:64].rearrange("p (t v) -> p t v", v=2)[:, :, v],
                                           VEC[:, V_BADA:V_BADA + 32], ALU.add))
                C.link(V.tensor_scalar(ADA[:, A_SC2:A_SC2 + 8, :], ADA[:, A_SC2:A_SC2 + 8, :], 1.0, 1 / ALPHA,
                                       ALU.add, ALU.mult))

                for t in range(TT):
                    dve.wait_ge(m_hi.sem, m_hi.at(l, t + 1))
                    V.tensor_tensor(ML[:, t, :].rearrange("p (a n) -> p a n", a=3)[:, 0:3:2, :], FPM[:, t],
                                    MH[:, t, :].rearrange("p (a n) -> p a n", a=3)[:, 0:3:2, :].bitcast(F32),
                                    ALU.subtract).then_inc(filt_ready.sem, 1)
                    dve.wait_ge(u_hi.sem, u_hi.at(l, t + 1))
                    V.tensor_tensor(ML[:, t, 256:512], PS[:, 2 + t % 2, 0:256], MH[:, t, 256:512].bitcast(F32),
                                    ALU.subtract).then_inc(u_ready.sem, 1)
                for j in range(TT):
                    b0 = 2 * (j % 2)
                    dve.wait_ge(g_scaled.sem, g_scaled.at(l, j + 1))
                    if j:
                        dve.wait_ge(f_hi.sem, f_hi.at(l, j))
                    uc, us = PS[:, b0, 256:512], PS[:, b0 + 1, 0:256]
                    V.tensor_tensor(PR[:, 0, :], uc, GS[:, 0, :], ALU.mult)
                    V.tensor_tensor(PR[:, 1, :], us, GS[:, 0, :], ALU.mult)
                    V.tensor_tensor(PR2[:, 0, :], us, GS[:, 1, :], ALU.mult)
                    C.link(V.tensor_tensor(PR2[:, 1, :], uc, GS[:, 1, :], ALU.mult))
                    C.link(V.tensor_tensor(YF[:, 0, :], PR[:, 0, :], PR2[:, 0, :], ALU.subtract))
                    V.tensor_tensor(YF[:, 1, :], PR[:, 1, :], PR2[:, 1, :], ALU.add).then_inc(f_sum.sem, 1)
                    dve.wait_ge(f_hi.sem, f_hi.at(l, j + 1))
                    fh = FH[:, j] if j < ST else FPH[:, j - ST]
                    fl = FL[:, j] if j < ST else FPL[:, j - ST]
                    V.tensor_tensor(fl, YF[:], fh.bitcast(F32), ALU.subtract).then_inc(f_ready.sem, 1)
                    dve.wait_ge(f_ready.sem, f_ready.at(l, j + 1))
                for q, (t0, tn) in enumerate(CHUNKS):
                    if q:
                        dve.wait_ge(cf_norm.sem, cf_norm.at(l, q))
                    dve.wait_ge(cf_stats.sem, cf_stats.at(l, q + 1))
                    C.link(V.tensor_scalar(MU[:, :tn], PS[:, 2, :tn], 4.0, None, ALU.mult))
                    C.link(V.tensor_tensor(LT[:, :tn], MU[:, :tn], MU[:, :tn], ALU.mult))
                    V.scalar_tensor_tensor(RS[:, :tn], PS[:, 3, :tn], 4.0, LT[:, :tn], ALU.mult, ALU.subtract)\
                     .then_inc(cf_var.sem, 1)
                    dve.wait_ge(cf_sd.sem, cf_sd.at(l, q + 1))
                    C.link(V.reciprocal(RS[:, :tn], RS[:, :tn]))
                    for ct in range(2):
                        u = CFU[:, ct, t0:t0 + tn]
                        C.link(V.tensor_tensor(LT[:, :tn], u, MU[:, :tn], ALU.subtract))
                        ins = V.tensor_tensor(u, LT[:, :tn], RS[:, :tn], ALU.mult)
                        if ct == 0:
                            C.link(ins)
                    ins.then_inc(cf_norm.sem, 1)
                dve.wait_ge(old_in.sem, old_in.at(l, 4 * 16))
                dve.wait_ge(blk_used.sem, blk_used.at(l, B_OUT))
                for ct in range(2):
                    for q, (t0, tn) in enumerate(CHUNKS):
                        y = PS[:, 4 + 2 * ct + q, :tn] if q < 2 else PS[:, ct, :tn]
                        u, x0 = [OLD[:, x, ct, t0:t0 + tn] for x in range(2)]
                        C.link(V.scalar_tensor_tensor(u, u, VEC[:, V_BIAS + ct:V_BIAS + ct + 1], y, ALU.mult, ALU.add))
                        V.tensor_tensor(OY[:, ct, t0:t0 + tn], u, x0, ALU.mult).then_inc(hy_done.sem, 1)

                dve.wait_ge(at_tab.sem, at_tab.at(l, 16))
                dve.wait_ge(lam_exp.sem, lam_exp.at(l, 1))
                C.link(V.tensor_tensor(LAMS[:, 0:1], LAMS[:, 3:4], LAMS[:, 2:3], ALU.subtract))
                V.tensor_tensor(LAMC[:, 2:3], LAMS[:, 0:1], LAMC[:, 0:1], ALU.subtract).then_inc(lam_known.sem, 1)
                def rotate(h):
                    for n, src in enumerate((QR[:], KR[:, PAST:PAST + LS])):
                        dve.wait_ge(rope_swapped.sem, rope_swapped.at(l, n + 1) + h * 2)
                        C.link(V.tensor_tensor(RT[:], PSF[:, 512 + 1536 * n:512 + 1536 * n + LS], ROPE[:, 1, :], ALU.mult))
                        dve.wait_ge(rope_cos.sem, rope_cos.at(l, n + 1) + h * 2)
                        V.tensor_tensor(src[:, 0:LS], src[:, 0:LS], RT[:], ALU.add).then_inc(rope_done.sem, 1)
                        dve.wait_ge(rope_done.sem, rope_done.at(l, n + 1) + h * 2)

                def split_inputs(h):
                    dve.wait_ge(v_hi.sem, v_hi.at(l, 1) + h)
                    V.tensor_tensor(V2[:, 0:2, 128:256], CKV[:, 1], V2[:, 0:2, 0:128].bitcast(F32), ALU.subtract)
                    V.tensor_tensor(V2[:, 2:TT + 2, 128:256], PSF[:, 512:512 + T].rearrange("p (t n) -> p t n", t=TT),
                                    V2[:, 2:TT + 2, 0:128].bitcast(F32), ALU.subtract).then_inc(v_split.sem, 1)
                    for m in range(2):
                        own, other = slice(64 * m, 64 * m + 64), slice(64 - 64 * m, 128 - 64 * m)
                        dve.wait_ge(qk_hi.sem, qk_hi.at(l, m + 1) + h * 6)
                        V.tensor_tensor(KL[other, m, :], KR[own, :], KH[own, m, :].bitcast(F32), ALU.subtract)
                    for m in range(2):
                        own, other = slice(64 * m, 64 * m + 64), slice(64 - 64 * m, 128 - 64 * m)
                        dve.wait_ge(qk_hi.sem, qk_hi.at(l, m + 5) + h * 6)
                        ins = V.scalar_tensor_tensor(QQ[other, m, :], QR[own, :], SCALE, QQ[own, m, :].bitcast(F32),
                                                     ALU.mult, ALU.subtract)
                    ins.then_inc(qk_split.sem, 1)

                def head(h, last):
                    dve.wait_ge(lam_known.sem, lam_known.at(l, 1))

                    def maxima(t):
                        k0, kn = ITEMS[t]
                        for m in range(2):
                            dve.wait_ge(s_psum.sem, s_psum.at(l, 2 * t + m + 1) + h * 2 * TT)
                            V.tensor_reduce(STAT[:, t % 4, m:m + 1], PSF[:, 1536 * m:1536 * m + kn],
                                            AX_X, ALU.max, negate=True).then_inc(smax.sem, 1)

                    def mix(t):
                        k0, kn = ITEMS[t]
                        st_ = STAT[:, t % 4, :]
                        dve.wait_ge(probs.sem, probs.at(l, 2 * t + 2) + h * 2 * TT)
                        C.link(V.reciprocal(st_[:, 4:6], st_[:, 2:4]))
                        C.link(V.scalar_tensor_tensor(st_[:, 6:7], st_[:, 2:3], LAMC[:, 2:3], st_[:, 5:6],
                                                      ALU.mult, ALU.mult))
                        if t:
                            dve.wait_ge(at_psum.sem, at_psum.at(l, first_round(t)) + h * ROUNDS)
                        V.scalar_tensor_tensor(AB[:, :kn], PB[:, t % 2, 1, :kn], st_[:, 6:7], PB[:, t % 2, 0, :kn],
                                               ALU.mult, ALU.add).then_inc(mixed.sem, 1)

                    def lo_of_round(t, r):
                        g0, gn = rounds(t)[r]
                        cols = slice(g0 * 128, (g0 + gn) * 128)
                        dve.wait_ge(at_hi.sem, at_hi.at(l, first_round(t) + r + 1) + h * ROUNDS)
                        V.tensor_tensor(ATL[:, t % 2, cols], PS[:, 6 + r % 2, 0:gn * 128],
                                        ATH[:, t % 2, cols].bitcast(F32), ALU.subtract).then_inc(at_lo.sem, 1)

                    def output(t):
                        dve.wait_ge(o_part.sem, o_part.at(l, t + 1) + h * TT)
                        V.scalar_tensor_tensor(OB[:, t, :], PS[:, 7, 0:128], STAT[:, t % 4, 4:5], O2[:],
                                               ALU.mult, ALU.add).then_inc(o_ready.sem, 1)

                    maxima(0)
                    maxima(1)
                    mix(0)
                    for t in range(TT):
                        for r in range(min(2, len(rounds(t)))):
                            lo_of_round(t, r)
                        if t + 2 < TT:
                            maxima(t + 2)
                        if t + 1 < TT:
                            mix(t + 1)
                        if len(rounds(t)) > 2:
                            lo_of_round(t, 2)
                        if t:
                            output(t - 1)
                        if t == ST and not last:
                            rotate(h + 1)
                    output(TT - 1)
                    if not last:
                        split_inputs(h + 1)
                    dve.wait_ge(sd_head.sem, sd_head.at(l, 1) + h)
                    C.link(V.reciprocal(RRS[:], RRS[:]))
                    C.link(V.tensor_scalar(RRS[:], RRS[:], LAMC[:, 1:2], None, ALU.mult))
                    V.tensor_tensor(OB[:], OB[:], RRS[:].rearrange("p (t a) -> p t a", a=1).broadcast_to([128, TT, 128]),
                                    ALU.mult).then_inc(o_normed.sem, 1)
                    dve.wait_ge(o_normed.sem, o_normed.at(l, 1) + h)

                rotate(0)
                split_inputs(0)
                with dve.Fori(0, HEADS - 1) as h:
                    C.loop(h, V_HEAD, HEADS - 1)
                    head(h, False)
                C.end_loop()
                head(HEADS - 1, True)

                for n in range(24):
                    q, j = n // 8, n % 8
                    t0, tn = CHUNKS[q]
                    dve.wait_ge(y_hi.sem, y_hi.at(l, n + 1))
                    V.tensor_tensor(HL[:, j, t0:t0 + tn], YIN[:, n % 4, :tn], HH[:, j, t0:t0 + tn].bitcast(F32),
                                    ALU.subtract).then_inc(y_lo.sem, 1)

                def add_sums(n, j, q):
                    t0, tn = CHUNKS[q]
                    for x in range(2):
                        if x:
                            dve.wait_ge(sq_ready.sem, sq_ready.at(l, n + 1))
                        src = SQO[:, n % 2, :tn] if x else XT[:, j, t0:t0 + tn]
                        dst = ACC1[:, x, t0:t0 + tn]
                        ins = V.tensor_copy(dst, src) if j == 0 else V.tensor_tensor(dst, dst, src, ALU.add)
                        if x:
                            ins.then_inc(sq_added.sem, 1)
                            dve.wait_ge(sq_added.sem, sq_added.at(l, n + 1))
                        else:
                            C.link(ins)
                    if j == KT - 1:
                        V.memset(STAT[:, 0, 7:8], 0.0).then_inc(acc_ready.sem, 1)
                        dve.wait_ge(acc_ready.sem, acc_ready.at(l, q + 1))

                for n in range(24):
                    q, j = n % 3, n // 3
                    t0, tn = CHUNKS[q]
                    if q < 2:
                        dve.wait_ge(o_psum.sem, o_psum.at(l, 2 * j + q + 1))
                    else:
                        dve.wait_ge(blk_used.sem, blk_used.at(l, B_OUT + j + 1))
                    x = XT[:, j, t0:t0 + tn]
                    V.scalar_tensor_tensor(x, PS[:, 3 * (j % 2) + q, :tn], ADA[:, A_G1 + j, COND[q]:COND[q] + 1], x,
                                           ALU.mult, ALU.add).then_inc(o_evac.sem, 1)
                    dve.wait_ge(o_evac.sem, o_evac.at(l, n + 1))
                    add_sums(n, j, q)
                norm(l, 0, (6, 0, 2))

                def hidden(g, q):
                    t0, tn = CHUNKS[q]
                    for e in range(2):
                        u = 2 * q + e
                        dve.wait_ge(relu_done.sem, relu_done.at(l, u + 1) + g * 6)
                        V.tensor_tensor(SB2[:, e, :tn], RB[:, e, :tn], RB[:, e, :tn], ALU.mult).then_inc(sq_kept.sem, 1)
                        dve.wait_ge(sq_kept.sem, sq_kept.at(l, u + 1) + g * 6)
                        dve.wait_ge(hid_hi.sem, hid_hi.at(l, u + 1) + g * 6)
                        V.tensor_tensor(hidden_lo(q)[:, e, :tn], SB2[:, e, :tn], hidden_hi(q)[:, e, :tn].bitcast(F32),
                                        ALU.subtract).then_inc(hid_ready.sem, 1)

                def down(g, q, back, sums=False):
                    t0, tn = CHUNKS[q]
                    for j in range(KT):
                        m = 8 * (q - 3 * back) + j
                        if q == 2 and j == KT - 1:
                            dve.wait_ge(blk_used.sem, blk_used.at(l, B_MLP + 4 * (1 - back)) + g * 4)
                        else:
                            dve.wait_ge(m2_psum.sem, m2_psum.at(l, 8 * q + j + 1 - 23 * back) + g * 23)
                        x = XT[:, j, t0:t0 + tn]
                        V.scalar_tensor_tensor(x, PS[:, 2 + m % 6, :tn], ADA[:, A_G2 + j, COND[q]:COND[q] + 1], x,
                                               ALU.mult, ALU.add).then_inc(m2_evac.sem, 1)
                        if sums:
                            dve.wait_ge(m2_evac.sem, m2_evac.at(l, 24 * g + 8 * q + j + 1))
                            dst = ACC2[:, 0, t0:t0 + tn]
                            ins = V.tensor_copy(dst, x) if j == 0 else V.tensor_tensor(dst, dst, x, ALU.add)
                            if j < KT - 1:
                                C.link(ins)
                            else:
                                ins.then_inc(acc_ready.sem, 1)

                def group(g, first=False):
                    hidden(g, 0)
                    if not first:
                        down(g, 2, 1)
                    hidden(g, 1)
                    down(g, 0, 0)
                    hidden(g, 2)
                    down(g, 1, 0)

                group(0, True)
                with dve.Fori(1, GROUPS - 1) as g:
                    group(g)
                g = GROUPS - 1
                hidden(g, 0)
                down(g, 2, 1)
                hidden(g, 1)
                down(g, 0, 0, True)
                hidden(g, 2)
                down(g, 1, 0, True)
                down(g, 2, 0, True)
                norm(l, 1, (0, 2, 4))
                C.end_layer()

            dve.wait_ge(h_ready.sem, h_ready.at(DEPTH - 1, 48))
            for t in range(TT):
                dve.wait_ge(y_turned.sem, t + 1)
                if t >= 2:
                    dve.wait_ge(y_stored[t % 2].sem, 16 * (t // 2))
                for half in range(2):
                    ins = V.tensor_scalar(XIN[:, t % 2, 512 * half:512 * half + 512], PS[:, 2 * (t % 2) + half, :],
                                          1 / ALPHA, None, ALU.mult)
                ins.then_inc(y_placed.sem, 1)


def bass_hyena_conformer_diffattn_dit(nc, ins, consts, outs):
    program(nc, ins, consts, outs)


_INS = ['x_prompt', 'x_sample', 'cache_k', 'cache_v', 'c', 'c_ctx', 'w_ada', 'b_ada', 'w_in',
        'hy_conv_w', 'hy_conv_b', 'hf_w1', 'hf_b1', 'hf_freq', 'hf_w2', 'hf_b2', 'hf_w3', 'hy_bias',
        'cf_conv_w', 'cf_conv_b', 'cf_ln_g', 'cf_ln_b', 'lam_q1', 'lam_k1', 'lam_q2', 'lam_k2',
        'subln_g', 'w_out', 'ln1_g', 'ln1_b', 'w_mlp1', 'w_mlp2', 'ln2_g', 'ln2_b']
_OUTS = [(1, 256, 1024), (1, 1024, 1024), (1, 2, 256, 8, 64), (1, 2, 256, 4, 128)]


def _constants():
    import numpy as np
    ident = np.eye(128)
    d = np.arange(128)
    partner = np.where(d % 32 < 16, d + 16, d - 16)
    swap = np.zeros((128, 128))
    swap[partner, d] = 1.0
    tok = np.arange(1024)
    f32 = np.float32
    inv = (f32(10000.0) ** (-(np.arange(0, 32, 2, dtype=f32)) / f32(32))).astype(f32)
    pos = np.where(((d // 32) % 2 == 0)[:, None], (tok // 64)[None, :], (tok % 64)[None, :]).astype(f32)
    ang = (pos * inv[d % 16][:, None]).astype(f32).astype(np.float64)
    sign = np.where(d % 32 < 16, -1.0, 1.0)[:, None]
    rope = np.stack([np.cos(ang), sign * np.sin(ang)], 1)
    feats, decay = [], []
    deltas = np.abs(np.linspace(math.log(1e-2) / 0.3, math.log(1e-2) / 1.5, 256))
    for n in (1024, 256):
        t = np.linspace(0.0, 1.0, n)[:, None]
        w = (2.0 * math.pi / n) * np.arange(n)[:, None]
        fr = np.linspace(1e-4, 15, 16)[None, :]
        feats.append(np.concatenate([t, np.cos(fr * w), -np.sin(fr * w)], -1))
        dec = np.exp(-t * deltas[None, :])
        back = dec.copy()
        back[0] = 0.0
        decay.append(np.concatenate([dec, back], 1))

    def dft(n):
        a = 2 * math.pi * ((np.arange(n)[:, None] * np.arange(n)[None, :]) % (2 * n - 1)) / (2 * n - 1)
        return np.stack([np.cos(a), np.sin(a)])

    small = dft(256).reshape(2, 2, 128, 256).transpose(2, 1, 0, 3).reshape(128, 1024)
    weight = np.full((128, 10), 2.0)
    weight[:, :8] /= 2047
    weight[:, 8:] /= 511
    weight[0, 0] /= 2
    weight[0, 8] /= 2
    lam = [0.8 - 0.6 * math.exp(-0.3 * k) for k in range(2)]
    lam = np.broadcast_to(np.array([[v, 1 - v] for v in lam])[:, None, :], (2, 128, 2))
    out = [ident, swap, rope, np.concatenate(feats).T, np.concatenate(decay), dft(1024), small, weight, lam]
    return [np.ascontiguousarray(a, dtype=f32) for a in out]


def kernel(**inputs):
    import numpy as _np
    import concourse.bacc as _bacc
    from concourse import mybir as _mybir
    from concourse.bass_utils import run_bass_kernel_spmd as _run

    nc = _bacc.Bacc("TRN2", target_bir_lowering=False, num_devices=1)
    arrays = {}

    def external(name, a):
        a = _np.ascontiguousarray(a)
        arrays[name] = a
        return nc.dram_tensor(name, a.shape, _mybir.dt.from_np(a.dtype), kind="ExternalInput").ap()

    ins = [external(f"in_{n}_dram", inputs[n]) for n in _INS]
    consts = [external(f"const_{i}_dram", a) for i, a in enumerate(_constants())]
    outs = [nc.dram_tensor(f"out_{i}_dram", s, _mybir.dt.from_np(_np.dtype("float32")), kind="ExternalOutput").ap()
            for i, s in enumerate(_OUTS)]
    bass_hyena_conformer_diffattn_dit(nc, ins, consts, outs)
    r = _run(nc, [arrays], core_ids=[0])
    return tuple(r.results[0][f"out_{i}_dram"] for i in range(len(_OUTS)))
```
